# Optimizing a Trainium2 kernel written in Bass

```python
import jax, jax.numpy as jnp
from jax import lax
import numpy as np
import math
import jax
import jax.numpy as jnp

D_MODEL = 2048
BATCH = 1
SEQ = 256
DEPTH = 1

N_HEADS_MLA = 8
Q_LORA_RANK = 512
KV_LORA_RANK = 512
QK_NOPE_DIM = 128
QK_ROPE_DIM = 64
QK_HEAD_DIM = QK_NOPE_DIM + QK_ROPE_DIM
V_HEAD_DIM = 128
MLA_WIDTH = N_HEADS_MLA * V_HEAD_DIM
N_HEADS_SB = 8
SB_HEAD_DIM = 128
SB_WIDTH = N_HEADS_SB * SB_HEAD_DIM
D_FF = -(-8 * D_MODEL // (3 * 256)) * 256
D_IN = Q_LORA_RANK + KV_LORA_RANK + QK_ROPE_DIM + 3 * SB_WIDTH + 2 * D_MODEL
Q_BLOCK = 128
ROPE_THETA = 10000.0
EPS = 1e-6


def _rms(x, g):
    xf = x.astype(jnp.float32)
    y = xf * lax.rsqrt(jnp.mean(xf * xf, axis=-1, keepdims=True) + EPS)
    return (y * g.astype(jnp.float32)).astype(x.dtype)

def _rope(x, pos):
    half = x.shape[-1] // 2
    freqs = ROPE_THETA ** (-jnp.arange(half, dtype=jnp.float32) / half)
    ang = pos.astype(jnp.float32)[..., None] * freqs
    cos = jnp.cos(ang)[:, :, None, :]
    sin = jnp.sin(ang)[:, :, None, :]
    xf = x.astype(jnp.float32)
    x1, x2 = xf[..., :half], xf[..., half:]
    return jnp.concatenate([x1 * cos - x2 * sin, x1 * sin + x2 * cos], axis=-1).astype(x.dtype)

def _mla_attention(q, k, v):
    S = q.shape[2]
    scale = QK_HEAD_DIM ** -0.5
    outs = []
    for i in range(S // Q_BLOCK):
        end = (i + 1) * Q_BLOCK
        qb = q[:, :, i * Q_BLOCK:end]
        s = jnp.einsum('bhqd,bhkd->bhqk', qb, k[:, :, :end]).astype(jnp.float32) * scale
        qi = i * Q_BLOCK + jnp.arange(Q_BLOCK)
        ki = jnp.arange(end)
        s = jnp.where(ki[None, :] <= qi[:, None], s, -jnp.inf)
        p = jax.nn.softmax(s, axis=-1).astype(v.dtype)
        outs.append(jnp.einsum('bhqk,bhkd->bhqd', p, v[:, :, :end]))
    return jnp.concatenate(outs, axis=2)

def _stick_breaking(q, k, v):
    S = q.shape[2]
    scale = SB_HEAD_DIM ** -0.5
    outs = []
    for i in range(S // Q_BLOCK):
        end = (i + 1) * Q_BLOCK
        qb = q[:, :, i * Q_BLOCK:end]
        z = jnp.einsum('bhqd,bhkd->bhqk', qb, k[:, :, :end]).astype(jnp.float32) * scale
        qi = i * Q_BLOCK + jnp.arange(Q_BLOCK)
        ki = jnp.arange(end)
        mask = ki[None, :] < qi[:, None]
        log_beta = jax.nn.log_sigmoid(z)
        log_one_minus = jnp.where(mask, jax.nn.log_sigmoid(-z), 0.0)
        tail = lax.cumsum(log_one_minus, axis=3, reverse=True) - log_one_minus
        a = jnp.where(mask, jnp.exp(log_beta + tail), 0.0).astype(v.dtype)
        outs.append(jnp.einsum('bhqk,bhkd->bhqd', a, v[:, :, :end]))
    return jnp.concatenate(outs, axis=2)

def _layer(x, c_act, pos, w_ada, b_ada, g_norm1, g_norm2, w_in, g_q_latent, g_kv_latent,
           w_uq, w_ukv, g_q_head, g_k_head, w_proj_mla, w_proj_sb, w_out, w_ffn_in, w_ffn_out):
    B, S, _ = x.shape
    ada = (c_act @ w_ada + b_ada)[:, None, :]
    sh1, sc1, gt1, sh2, sc2, gt2 = jnp.split(ada, 6, axis=-1)

    h = _rms(x, g_norm1) * (1 + sc1) + sh1
    proj = h @ w_in
    offs = np.cumsum([Q_LORA_RANK, KV_LORA_RANK, QK_ROPE_DIM, SB_WIDTH, SB_WIDTH, SB_WIDTH, D_MODEL])
    c_q, c_kv, k_pe, q_sb, k_sb, v_sb, gl_a, gl_b = jnp.split(proj, [int(o) for o in offs], axis=-1)

    q = (_rms(c_q, g_q_latent) @ w_uq).reshape(B, S, N_HEADS_MLA, QK_HEAD_DIM)
    kv = (_rms(c_kv, g_kv_latent) @ w_ukv).reshape(B, S, N_HEADS_MLA, QK_NOPE_DIM + V_HEAD_DIM)
    k_nope, v = kv[..., :QK_NOPE_DIM], kv[..., QK_NOPE_DIM:]
    k_pe_h = jnp.broadcast_to(k_pe[:, :, None, :], (B, S, N_HEADS_MLA, QK_ROPE_DIM))
    k = jnp.concatenate([k_nope, k_pe_h], axis=-1)
    q = _rms(q, g_q_head)
    k = _rms(k, g_k_head)
    q = jnp.concatenate([q[..., :QK_NOPE_DIM], _rope(q[..., QK_NOPE_DIM:], pos)], axis=-1)
    k = jnp.concatenate([k[..., :QK_NOPE_DIM], _rope(k[..., QK_NOPE_DIM:], pos)], axis=-1)
    y_a = _mla_attention(q.transpose(0, 2, 1, 3), k.transpose(0, 2, 1, 3), v.transpose(0, 2, 1, 3))
    y_a = y_a.transpose(0, 2, 1, 3).reshape(B, S, MLA_WIDTH)

    to_heads = lambda t: t.reshape(B, S, N_HEADS_SB, SB_HEAD_DIM).transpose(0, 2, 1, 3)
    y_b = _stick_breaking(to_heads(q_sb), to_heads(k_sb), to_heads(v_sb))
    y_b = y_b.transpose(0, 2, 1, 3).reshape(B, S, SB_WIDTH)

    merged = jax.nn.sigmoid(gl_a) * (y_a @ w_proj_mla) + jax.nn.sigmoid(gl_b) * (y_b @ w_proj_sb)
    x = x + gt1 * (merged @ w_out)

    h2 = _rms(x, g_norm2) * (1 + sc2) + sh2
    gate, up = jnp.split(h2 @ w_ffn_in, 2, axis=-1)
    x = x + gt2 * ((jax.nn.silu(gate) * up) @ w_ffn_out)
    return x

def first_inputs(seed: int = 0) -> dict:
    key = jax.random.key(seed)
    ks = jax.random.split(key, 24)
    f32 = jnp.float32

    def nrm(k, shape, fan_in):
        return jax.random.normal(k, shape, f32) * (fan_in ** -0.5)

    def gain(k, n):
        return 1.0 + 0.02 * jax.random.normal(k, (DEPTH, n), f32)

    x = jax.random.normal(ks[0], (BATCH, SEQ, D_MODEL), f32)
    c = jax.random.normal(ks[1], (BATCH, D_MODEL), f32)
    offset = jax.random.randint(ks[2], (BATCH, 1), 0, 1024, dtype=jnp.int32)
    positions = offset + jnp.arange(SEQ, dtype=jnp.int32)[None, :]
    return {
        "x": x,
        "c": c,
        "positions": positions,
        "w_ada": nrm(ks[3], (DEPTH, D_MODEL, 6 * D_MODEL), D_MODEL),
        "b_ada": 0.02 * jax.random.normal(ks[4], (DEPTH, 6 * D_MODEL), f32),
        "g_norm1": gain(ks[5], D_MODEL),
        "g_norm2": gain(ks[6], D_MODEL),
        "w_in": nrm(ks[7], (DEPTH, D_MODEL, D_IN), D_MODEL),
        "g_q_latent": gain(ks[8], Q_LORA_RANK),
        "g_kv_latent": gain(ks[9], KV_LORA_RANK),
        "w_uq": nrm(ks[10], (DEPTH, Q_LORA_RANK, N_HEADS_MLA * QK_HEAD_DIM), Q_LORA_RANK),
        "w_ukv": nrm(ks[11], (DEPTH, KV_LORA_RANK, N_HEADS_MLA * (QK_NOPE_DIM + V_HEAD_DIM)), KV_LORA_RANK),
        "g_q_head": gain(ks[12], QK_HEAD_DIM),
        "g_k_head": gain(ks[13], QK_HEAD_DIM),
        "w_proj_mla": nrm(ks[14], (DEPTH, MLA_WIDTH, D_MODEL), MLA_WIDTH),
        "w_proj_sb": nrm(ks[15], (DEPTH, SB_WIDTH, D_MODEL), SB_WIDTH),
        "w_out": nrm(ks[16], (DEPTH, D_MODEL, D_MODEL), D_MODEL),
        "w_ffn_in": nrm(ks[17], (DEPTH, D_MODEL, 2 * D_FF), D_MODEL),
        "w_ffn_out": nrm(ks[18], (DEPTH, D_FF, D_MODEL), D_FF),
    }

def first_block(x, c, positions, w_ada, b_ada, g_norm1, g_norm2, w_in, g_q_latent, g_kv_latent,
              w_uq, w_ukv, g_q_head, g_k_head, w_proj_mla, w_proj_sb, w_out, w_ffn_in, w_ffn_out):
    c_act = jax.nn.silu(c)
    for l in range(DEPTH):
        x = _layer(x, c_act, positions, w_ada[l], b_ada[l], g_norm1[l], g_norm2[l], w_in[l],
                   g_q_latent[l], g_kv_latent[l], w_uq[l], w_ukv[l], g_q_head[l], g_k_head[l],
                   w_proj_mla[l], w_proj_sb[l], w_out[l], w_ffn_in[l], w_ffn_out[l])
    return x


D_MIX = D_MODEL
SSD_WIDTH = D_MIX // 2
ATT_WIDTH = D_MIX - SSD_WIDTH

SSD_HEAD_DIM = 64
SSD_HEADS = SSD_WIDTH // SSD_HEAD_DIM
SSD_GROUPS = 2
SSD_STATE = 128
SSD_CHUNK = 128
CONV_WIDTH = 4
CONV_CH = SSD_WIDTH + 2 * SSD_GROUPS * SSD_STATE

ATT_HEAD_DIM = 64
ATT_HEADS = ATT_WIDTH // ATT_HEAD_DIM
ATT_KV_HEADS = 4
ATT_GROUP = ATT_HEADS // ATT_KV_HEADS
KV_WIDTH = ATT_KV_HEADS * ATT_HEAD_DIM
CMP_BLOCK = 32
CMP_STRIDE = 16
CMP_HIDDEN = 256
SEL_BLOCK = 64
N_SELECT = 16
WINDOW = 512
N_BRANCH = 3

ROPE_THETA_2 = 500000.0
ROPE_DIM = ATT_HEAD_DIM // 4

D_FF_2 = -((-8 * D_MODEL) // (3 * 256)) * 256

NORM_EPS = 1e-6
NEG_INF = -1e30
FORCE_SCORE = 1e4

IN_WIDTHS = (SSD_WIDTH, CONV_CH, SSD_HEADS, ATT_WIDTH, KV_WIDTH, KV_WIDTH, KV_WIDTH, KV_WIDTH, KV_WIDTH, KV_WIDTH, ATT_HEADS * N_BRANCH)
D_IN_2 = sum(IN_WIDTHS)


def rmsnorm(x, w):
    xf = x.astype(jnp.float32)
    xf = xf * lax.rsqrt(jnp.mean(xf * xf, axis=-1, keepdims=True) + NORM_EPS)
    return xf.astype(x.dtype) * w

def rope_tables(seq, dtype):
    inv = 1.0 / (ROPE_THETA_2 ** (jnp.arange(0, ROPE_DIM, 2, dtype=jnp.float32) / ROPE_DIM))
    ang = jnp.arange(seq, dtype=jnp.float32)[:, None] * inv[None, :]
    return jnp.cos(ang).astype(dtype), jnp.sin(ang).astype(dtype)

def partial_rope(x, cos, sin):
    half = ROPE_DIM // 2
    c = cos[None, :, None, :]
    s = sin[None, :, None, :]
    x1 = x[..., :half]
    x2 = x[..., half:ROPE_DIM]
    return jnp.concatenate([x1 * c - x2 * s, x2 * c + x1 * s, x[..., ROPE_DIM:]], axis=-1)

def causal_depthwise_conv(u, w, b):
    y = lax.conv_general_dilated(u, w[:, None, :].astype(u.dtype), window_strides=(1,), padding=((CONV_WIDTH - 1, 0),), dimension_numbers=('NWC', 'WIO', 'NWC'), feature_group_count=u.shape[-1])
    return y + b

def ssd_chunked(xdt, adt, bm, cm):
    bsz, seq = xdt.shape[:2]
    nc = seq // SSD_CHUNK
    hg = SSD_HEADS // SSD_GROUPS
    x = xdt.reshape(bsz, nc, SSD_CHUNK, SSD_GROUPS, hg, SSD_HEAD_DIM)
    a = adt.reshape(bsz, nc, SSD_CHUNK, SSD_GROUPS, hg)
    b = bm.reshape(bsz, nc, SSD_CHUNK, SSD_GROUPS, SSD_STATE)
    c = cm.reshape(bsz, nc, SSD_CHUNK, SSD_GROUPS, SSD_STATE)
    a_cum = jnp.cumsum(a, axis=2)
    causal = jnp.tril(jnp.ones((SSD_CHUNK, SSD_CHUNK), dtype=bool))[:, :, None, None]
    seg = a_cum[:, :, :, None] - a_cum[:, :, None, :]
    decay = jnp.exp(jnp.where(causal, seg, -jnp.inf))
    cb = jnp.einsum('bclgn,bcsgn->bclsg', c, b)
    y_diag = jnp.einsum('bclsgh,bcsghp->bclghp', cb[..., None] * decay, x)
    decay_states = jnp.exp(a_cum[:, :, -1:] - a_cum)
    states = jnp.einsum('bclgn,bclghp->bcghpn', b, x * decay_states[..., None])
    chunk_decay = jnp.exp(a_cum[:, :, -1])

    def step(h, inp):
        st, dec = inp
        return h * dec[..., None, None] + st, h

    h0 = jnp.zeros_like(states[:, 0])
    _, prev = lax.scan(step, h0, (jnp.moveaxis(states, 1, 0), jnp.moveaxis(chunk_decay, 1, 0)))
    prev = jnp.moveaxis(prev, 0, 1)
    y_off = jnp.einsum('bclgn,bcghpn->bclghp', c, prev) * jnp.exp(a_cum)[..., None]
    return (y_diag + y_off).reshape(bsz, seq, SSD_HEADS, SSD_HEAD_DIM)

def ssd_mixer(z, xbc, dt_raw, conv_w, conv_b, dt_bias, a_log, d_skip, norm_w):
    bsz, seq = z.shape[:2]
    xbc = jax.nn.silu(causal_depthwise_conv(xbc, conv_w, conv_b))
    xs, bm, cm = jnp.split(xbc, [SSD_WIDTH, SSD_WIDTH + SSD_GROUPS * SSD_STATE], axis=-1)
    xh = xs.reshape(bsz, seq, SSD_HEADS, SSD_HEAD_DIM)
    dt = jax.nn.softplus(dt_raw.astype(jnp.float32) + dt_bias.astype(jnp.float32))
    a = -jnp.exp(a_log.astype(jnp.float32))
    y = ssd_chunked(xh * dt[..., None], a * dt, bm.reshape(bsz, seq, SSD_GROUPS, SSD_STATE), cm.reshape(bsz, seq, SSD_GROUPS, SSD_STATE))
    y = y + d_skip[:, None] * xh
    y = y.reshape(bsz, seq, SSD_WIDTH).astype(z.dtype)
    return rmsnorm(y * jax.nn.silu(z), norm_w)

def selection_overlap(n_cmp, n_sel):
    cs = np.arange(n_cmp)[:, None] * CMP_STRIDE
    ce = cs + CMP_BLOCK
    ss = np.arange(n_sel)[None, :] * SEL_BLOCK
    se = ss + SEL_BLOCK
    ov = np.clip(np.minimum(ce, se) - np.maximum(cs, ss), 0, None)
    return (ov / CMP_BLOCK).astype(np.float32)

def compress_tokens(kv, w1, w2, pe):
    bsz, seq = kv.shape[:2]
    n_cmp = (seq - CMP_BLOCK) // CMP_STRIDE + 1
    idx = np.arange(n_cmp)[:, None] * CMP_STRIDE + np.arange(CMP_BLOCK)[None, :]
    blocks = kv[:, idx] + pe[None, None, :, None, :]
    flat = jnp.swapaxes(blocks, 2, 3).reshape(bsz, n_cmp, ATT_KV_HEADS, CMP_BLOCK * ATT_HEAD_DIM)
    return jax.nn.silu(flat @ w1) @ w2

def nsa_mixer(q, kc, vc, ks, vs, kw, vw, gate_raw, cmp_w1_k, cmp_w2_k, cmp_w1_v, cmp_w2_v, cmp_pe_k, cmp_pe_v, cos, sin):
    bsz, seq = q.shape[:2]
    hd = ATT_HEAD_DIM
    scale = hd ** -0.5
    q = q.reshape(bsz, seq, ATT_HEADS, hd)
    kc, vc, ks, vs, kw, vw = [t.reshape(bsz, seq, ATT_KV_HEADS, hd) for t in (kc, vc, ks, vs, kw, vw)]
    q_grp = q.reshape(bsz, seq, ATT_KV_HEADS, ATT_GROUP, hd)
    q_rot = partial_rope(q, cos, sin).reshape(bsz, seq, ATT_KV_HEADS, ATT_GROUP, hd)
    ks = partial_rope(ks, cos, sin)
    kw = partial_rope(kw, cos, sin)
    t_pos = jnp.arange(seq)

    k_cmp = compress_tokens(kc, cmp_w1_k, cmp_w2_k, cmp_pe_k)
    v_cmp = compress_tokens(vc, cmp_w1_v, cmp_w2_v, cmp_pe_v)
    n_cmp = k_cmp.shape[1]
    cmp_end = jnp.arange(n_cmp) * CMP_STRIDE + CMP_BLOCK - 1
    cmp_mask = cmp_end[None, :] <= t_pos[:, None]
    s_cmp = jnp.einsum('bshgd,bihd->bhgsi', q_grp, k_cmp).astype(jnp.float32) * scale
    p_cmp = jax.nn.softmax(jnp.where(cmp_mask, s_cmp, NEG_INF), axis=-1) * cmp_mask
    o_cmp = jnp.einsum('bhgsi,bihd->bshgd', p_cmp.astype(v_cmp.dtype), v_cmp)

    n_sel = seq // SEL_BLOCK
    k_top = min(N_SELECT, n_sel)
    overlap = jnp.asarray(selection_overlap(n_cmp, n_sel))
    imp = jnp.einsum('bhgsi,ij->bhsj', p_cmp, overlap)
    blk = jnp.arange(n_sel)[None, :]
    cur = (t_pos // SEL_BLOCK)[:, None]
    imp = jnp.where((blk == 0) | (blk == cur) | (blk == cur - 1), FORCE_SCORE, imp)
    imp = jnp.where(blk <= cur, imp, -1.0)
    top_val, top_idx = lax.top_k(imp, k_top)
    top_valid = top_val >= 0.0

    ks_blocks = ks.reshape(bsz, n_sel, SEL_BLOCK, ATT_KV_HEADS, hd).transpose(0, 3, 1, 2, 4)
    vs_blocks = vs.reshape(bsz, n_sel, SEL_BLOCK, ATT_KV_HEADS, hd).transpose(0, 3, 1, 2, 4)
    kw_pad = jnp.pad(kw, ((0, 0), (WINDOW, 0), (0, 0), (0, 0)))
    vw_pad = jnp.pad(vw, ((0, 0), (WINDOW, 0), (0, 0), (0, 0)))
    gather_blocks = jax.vmap(jax.vmap(lambda blocks, ix: blocks[ix]))
    q_offs = jnp.arange(Q_BLOCK)
    w_offs = jnp.arange(WINDOW + Q_BLOCK)
    s_offs = jnp.arange(SEL_BLOCK)

    def query_block(qb):
        s0 = qb * Q_BLOCK
        tq = s0 + q_offs
        qblk = lax.dynamic_slice_in_dim(q_rot, s0, Q_BLOCK, axis=1)
        ib = lax.dynamic_slice_in_dim(top_idx, s0, Q_BLOCK, axis=2)
        vb = lax.dynamic_slice_in_dim(top_valid, s0, Q_BLOCK, axis=2)
        kg = gather_blocks(ks_blocks, ib)
        vg = gather_blocks(vs_blocks, ib)
        kpos = ib[..., None] * SEL_BLOCK + s_offs
        m_sel = (kpos <= tq[:, None, None]) & vb[..., None]
        s_sel = jnp.einsum('bqhgd,bhqjkd->bhgqjk', qblk, kg).astype(jnp.float32) * scale
        s_sel = jnp.where(m_sel[:, :, None], s_sel, NEG_INF).reshape(bsz, ATT_KV_HEADS, ATT_GROUP, Q_BLOCK, k_top * SEL_BLOCK)
        p_sel = jax.nn.softmax(s_sel, axis=-1).astype(vg.dtype)
        o_sel = jnp.einsum('bhgqn,bhqnd->bqhgd', p_sel, vg.reshape(bsz, ATT_KV_HEADS, Q_BLOCK, k_top * SEL_BLOCK, hd))
        kwb = lax.dynamic_slice_in_dim(kw_pad, s0, WINDOW + Q_BLOCK, axis=1)
        vwb = lax.dynamic_slice_in_dim(vw_pad, s0, WINDOW + Q_BLOCK, axis=1)
        kp = s0 - WINDOW + w_offs
        dist = tq[:, None] - kp[None, :]
        m_win = (dist >= 0) & (dist < WINDOW) & (kp[None, :] >= 0)
        s_win = jnp.einsum('bqhgd,bkhd->bhgqk', qblk, kwb).astype(jnp.float32) * scale
        p_win = jax.nn.softmax(jnp.where(m_win, s_win, NEG_INF), axis=-1).astype(vwb.dtype)
        o_win = jnp.einsum('bhgqk,bkhd->bqhgd', p_win, vwb)
        return o_sel, o_win

    o_sel, o_win = lax.map(query_block, jnp.arange(seq // Q_BLOCK))
    o_sel = jnp.moveaxis(o_sel, 0, 1).reshape(bsz, seq, ATT_KV_HEADS, ATT_GROUP, hd)
    o_win = jnp.moveaxis(o_win, 0, 1).reshape(bsz, seq, ATT_KV_HEADS, ATT_GROUP, hd)
    g = jax.nn.sigmoid(gate_raw.astype(jnp.float32)).reshape(bsz, seq, ATT_KV_HEADS, ATT_GROUP, N_BRANCH, 1).astype(q.dtype)
    o = g[..., 0, :] * o_cmp + g[..., 1, :] * o_sel + g[..., 2, :] * o_win
    return o.reshape(bsz, seq, ATT_WIDTH)

def second_inputs(seed: int = 0) -> dict:
    key = jax.random.key(seed)
    k = jax.random.split(key, 24)
    f32 = jnp.float32
    L = DEPTH

    def dense(kk, shape, fan_in):
        return jax.random.normal(kk, shape, f32) * fan_in ** -0.5

    def gain(kk, shape):
        return 1.0 + 0.05 * jax.random.normal(kk, shape, f32)

    dt = jnp.exp(jax.random.uniform(k[5], (L, SSD_HEADS), f32, math.log(1e-3), math.log(1e-1)))
    return {
        'x': jax.random.normal(k[0], (BATCH, SEQ, D_MODEL), f32),
        'attn_norm_w': gain(k[1], (L, D_MODEL)),
        'w_in': dense(k[2], (L, D_MODEL, D_IN_2), D_MODEL),
        'conv_w': dense(k[3], (L, CONV_WIDTH, CONV_CH), CONV_WIDTH),
        'conv_b': 0.01 * jax.random.normal(k[4], (L, CONV_CH), f32),
        'dt_bias': dt + jnp.log(-jnp.expm1(-dt)),
        'a_log': jnp.log(jax.random.uniform(k[6], (L, SSD_HEADS), f32, 1.0, 16.0)),
        'd_skip': 1.0 + 0.1 * jax.random.normal(k[7], (L, SSD_HEADS), f32),
        'ssd_norm_w': gain(k[8], (L, SSD_WIDTH)),
        'cmp_w1_k': dense(k[9], (L, CMP_BLOCK * ATT_HEAD_DIM, CMP_HIDDEN), CMP_BLOCK * ATT_HEAD_DIM),
        'cmp_w2_k': dense(k[10], (L, CMP_HIDDEN, ATT_HEAD_DIM), CMP_HIDDEN),
        'cmp_w1_v': dense(k[11], (L, CMP_BLOCK * ATT_HEAD_DIM, CMP_HIDDEN), CMP_BLOCK * ATT_HEAD_DIM),
        'cmp_w2_v': dense(k[12], (L, CMP_HIDDEN, ATT_HEAD_DIM), CMP_HIDDEN),
        'cmp_pe_k': 0.1 * jax.random.normal(k[13], (L, CMP_BLOCK, ATT_HEAD_DIM), f32),
        'cmp_pe_v': 0.1 * jax.random.normal(k[14], (L, CMP_BLOCK, ATT_HEAD_DIM), f32),
        'w_out': dense(k[15], (L, D_MIX, D_MODEL), D_MIX),
        'ffn_norm_w': gain(k[16], (L, D_MODEL)),
        'w_gate': dense(k[17], (L, D_MODEL, D_FF_2), D_MODEL),
        'w_up': dense(k[18], (L, D_MODEL, D_FF_2), D_MODEL),
        'w_down': dense(k[19], (L, D_FF_2, D_MODEL), D_FF_2),
        'final_norm_w': gain(k[20], (D_MODEL,)),
    }

def second_block(x, attn_norm_w, w_in, conv_w, conv_b, dt_bias, a_log, d_skip, ssd_norm_w, cmp_w1_k, cmp_w2_k, cmp_w1_v, cmp_w2_v, cmp_pe_k, cmp_pe_v, w_out, ffn_norm_w, w_gate, w_up, w_down, final_norm_w):
    cos, sin = rope_tables(x.shape[1], x.dtype)
    split_at = np.cumsum(IN_WIDTHS)[:-1].tolist()
    h = x
    for l in range(DEPTH):
        u = rmsnorm(h, attn_norm_w[l])
        z, xbc, dt_raw, q, kc, vc, ks, vs, kw, vw, gate_raw = jnp.split(u @ w_in[l], split_at, axis=-1)
        y_ssd = ssd_mixer(z, xbc, dt_raw, conv_w[l], conv_b[l], dt_bias[l], a_log[l], d_skip[l], ssd_norm_w[l])
        y_att = nsa_mixer(q, kc, vc, ks, vs, kw, vw, gate_raw, cmp_w1_k[l], cmp_w2_k[l], cmp_w1_v[l], cmp_w2_v[l], cmp_pe_k[l], cmp_pe_v[l], cos, sin)
        mixed = jnp.concatenate([y_ssd.astype(h.dtype), y_att.astype(h.dtype)], axis=-1)
        h = h + mixed @ w_out[l]
        v = rmsnorm(h, ffn_norm_w[l])
        h = h + (jax.nn.silu(v @ w_gate[l]) * (v @ w_up[l])) @ w_down[l]
    return rmsnorm(h, final_norm_w)


def setup_inputs(seed=0):
    out = dict(first_inputs(seed))
    for name, value in second_inputs(seed + 1).items():
        if name != "x":
            out[name + "_2"] = value
    return out


def reference(
    x, c, positions, w_ada, b_ada, g_norm1, g_norm2, w_in, g_q_latent, g_kv_latent, w_uq, w_ukv,
    g_q_head, g_k_head, w_proj_mla, w_proj_sb, w_out, w_ffn_in, w_ffn_out, attn_norm_w_2,
    w_in_2, conv_w_2, conv_b_2, dt_bias_2, a_log_2, d_skip_2, ssd_norm_w_2, cmp_w1_k_2,
    cmp_w2_k_2, cmp_w1_v_2, cmp_w2_v_2, cmp_pe_k_2, cmp_pe_v_2, w_out_2, ffn_norm_w_2, w_gate_2,
    w_up_2, w_down_2, final_norm_w_2,
):
    x = first_block(
        x, c, positions, w_ada, b_ada, g_norm1, g_norm2, w_in, g_q_latent, g_kv_latent, w_uq,
        w_ukv, g_q_head, g_k_head, w_proj_mla, w_proj_sb, w_out, w_ffn_in, w_ffn_out,
    )
    return second_block(
        x, attn_norm_w_2, w_in_2, conv_w_2, conv_b_2, dt_bias_2, a_log_2, d_skip_2,
        ssd_norm_w_2, cmp_w1_k_2, cmp_w2_k_2, cmp_w1_v_2, cmp_w2_v_2, cmp_pe_k_2, cmp_pe_v_2,
        w_out_2, ffn_norm_w_2, w_gate_2, w_up_2, w_down_2, final_norm_w_2,
    )


_drawn_inputs = setup_inputs


def setup_inputs(seed=0):
    import zlib

    import numpy as np

    out = dict(_drawn_inputs(seed))
    spreads = {}
    factors = {'g_norm1': 5.475,
     'g_norm2': 3.36,
     'g_q_latent': 8.0,
     'g_kv_latent': 8.0,
     'g_q_head': 8.0,
     'g_k_head': 8.0,
     'conv_b_2': 48.924,
     'cmp_pe_k_2': 64.0,
     'cmp_pe_v_2': 22.94,
     'attn_norm_w_2': 8.0,
     'd_skip_2': 64.0,
     'ssd_norm_w_2': 27.791,
     'cmp_w1_k_2': 8.0,
     'cmp_w2_k_2': 8.0,
     'cmp_w1_v_2': 3.764,
     'cmp_w2_v_2': 2.865,
     'ffn_norm_w_2': 8.0}
    for name, (base, spread) in spreads.items():
        noise = np.random.default_rng([zlib.crc32(name.encode()), seed]).standard_normal(out[name].shape)
        drawn = base * np.exp(spread * noise) if base else spread * noise
        out[name] = jnp.asarray(drawn.astype(out[name].dtype))
    for name, factor in factors.items():
        out[name] = (out[name] * factor).astype(out[name].dtype)
    return out
```

```python
from contextlib import ExitStack

import numpy as np

import concourse.bass as bass
from concourse import mybir

F32 = mybir.dt.float32
F32R = mybir.dt.float32r
I32 = mybir.dt.int32
ALU = mybir.AluOpType
ACT = mybir.ActivationFunctionType
AX_X = mybir.AxisListType.X

P = 128
SEQ = 256
T = SEQ // P
D = 2048
KD = D // P
CW = 512
RAW, HI, LO = 4, 4, 2
PEELED = 1
NEG = -1e30
EPS = 1e-6


class Gemm:

    def __init__(self, at, weights, k, n, lhs, col0=0, ada=0, width=CW, cols=None,
                 peeled=PEELED):
        self.weights, self.n, self.lhs, self.width = weights, n, lhs, width
        self.peeled = peeled
        self.S = k // 2
        self.ada = ada
        self.col = cols or (lambda u: (col0 + CW * u, 2 * CW))
        self.q, self.w, self.c, self.a = at["q"], at["w"], at["c"], at["a"]
        self.qper = self.S + self.ada
        at["q"] += n * self.qper
        at["w"] += n * self.S
        at["c"] += n if k else 0
        at["a"] += n if ada else 0
        assert self.qper % 2 == 0 and self.S % 2 == 0

    def order(self):
        if not self.S:
            return [("ada", s) for s in range(self.ada)]
        both = [(("w", s), ("ada", s)) for s in range(self.S)]
        return [x for pair in both for x in pair if x[0] == "w" or self.ada]

    def slots(self, u, j):
        w = 0
        for n, (kind, s) in enumerate(self.order()):
            yield kind, s, Count(self.q + u * self.qper + n, 2 * self.qper, j), \
                Count(self.w + u * self.S + w, 2 * self.S, j)
            w += kind == "w"


class Count:

    def __init__(self, first, per=0, j=None):
        self.first, self.per, self.j = first, per, j

    def __add__(self, n):
        return Count(self.first + n, self.per, self.j)

    def __sub__(self, n):
        return self + -n

    def __mod__(self, n):
        assert self.j is None or self.per % n == 0
        return self.first % n

    def times(self, n, of=1):
        assert self.j is None or self.per % of == 0
        return Count(self.first // of * n, self.per // of * n, self.j)

    @property
    def above_zero(self):
        assert self.j is None or self.first + self.per * PEELED > 0
        return self.j is not None or self.first > 0

    @property
    def value(self):
        return self.first if self.j is None else self.first + self.per * self.j


def in_pairs(eng, g, chunk, tail):
    for u in range(min(g.n, 2 * g.peeled)):
        chunk(u, None, u > 0)
    if g.n // 2 > g.peeled:
        with eng.Fori(g.peeled, g.n // 2) as j:
            chunk(0, j, True)
            chunk(1, j, True)
    if g.n % 2 and g.n > 2 * g.peeled:
        chunk(g.n - 1, None, True)
    tail(g.n)


def steps(*names):
    return {name: n + 1 for n, name in enumerate(names)}


C_IDENT, C_ONES, C_MASKQ, C_MASKT, C_MASKS, C_CUM, C_AFTER = (i * P for i in range(7))
C_FREQ = 7 * P
C_COS2, C_SIN2 = C_FREQ + 32, C_FREQ + 48
C_CMPADD, C_CMPMUL = C_FREQ + 64, C_FREQ + 94
NCONST = 1024


def constants():
    k = np.zeros((P, NCONST), np.float32)
    row, col = np.arange(P)[:, None], np.arange(P)[None, :]
    k[:, C_IDENT:C_IDENT + P] = row == col
    k[:, C_ONES:C_ONES + P] = 1.0
    k[:, C_MASKQ:C_MASKQ + P] = np.where(col <= row, 0.0, NEG)
    k[:, C_MASKT:C_MASKT + P] = np.where(row <= col, 0.0, NEG)
    k[:, C_MASKS:C_MASKS + P] = np.where(row < col, 0.0, NEG)
    k[:, C_CUM:C_CUM + P] = row <= col
    k[:, C_AFTER:C_AFTER + P] = row > col
    f32 = np.float32
    k[:, C_FREQ:C_FREQ + 32] = f32(10000.0) ** (-np.arange(32, dtype=f32) / f32(32))
    inv = f32(1.0) / (f32(500000.0) ** (np.arange(0, 16, 2, dtype=f32) / f32(16)))
    ang = (np.arange(SEQ, dtype=f32)[:, None] * inv[None, :]).reshape(T, P, 8)
    k[:, C_COS2:C_COS2 + 16] = np.cos(ang).transpose(1, 0, 2).reshape(P, 16)
    k[:, C_SIN2:C_SIN2 + 16] = np.sin(ang).transpose(1, 0, 2).reshape(P, 16)
    seen = (16 * np.arange(15) + 31)[None, None, :] <= np.arange(SEQ).reshape(T, P).T[:, :, None]
    k[:, C_CMPADD:C_CMPADD + 30] = np.where(seen, 0.0, NEG).reshape(P, 30)
    k[:, C_CMPMUL:C_CMPMUL + 30] = seen.reshape(P, 30)
    return k


ROWS = {}
for _name, _n in (("g1", 16), ("g2", 16), ("gql", 4), ("gkv", 4), ("ga", 16), ("gs", 8), ("gf", 16),
                  ("pek", 16), ("pev", 16), ("c", 16)):
    ROWS[_name] = (sum(n for _, n in ROWS.values()), _n)
NROWS = 128


def program(nc, A, out):
    base = (nc.sbuf_base + 63) // 64 * 64
    slab = nc.alloc_sbuf_tensor("slab", [P, (nc.sbuf_bytes_remaining - 64) // 4], F32)
    names = {}

    def place(name, at, shape, dt=F32):
        t = nc.alloc_sbuf_tensor_at(name, [P] + shape, dt, offset=base + at)
        names[name] = t.name
        return t

    x = place("x", 0, [T, D])
    raw = place("raw", 16384, [RAW, 2, CW])
    w_hi = place("w_hi", 32768, [HI, 2, CW], F32R)
    w_lo = place("w_lo", 49152, [LO, 2, CW], F32R)
    XT = 57344
    xt_hi = place("xt_hi", XT, [KD, SEQ], F32R)
    xt_lo = place("xt_lo", XT + 16384, [KD, SEQ], F32R)
    const = place("const", 90112, [NCONST])
    SM = 94208
    cols = place("cols", SM, [P])
    colb = place("colb", SM + 512, [64])
    adacol = place("adacol", SM + 768, [4, KD])
    ccol = place("ccol", SM + 1024, [KD])
    scol = place("scol", SM + 1088, [4, KD])
    stat = place("stat", SM + 1344, [64])
    GT2, GT1, PROJ = 98304, 106496, 114688
    gt2 = place("gt2", GT2, [D])
    gt1 = place("gt1", GT1, [D])
    NIN = 8256
    proj = place("proj", PROJ, [T, NIN])
    xn = place("xn", PROJ, [T, D])
    rows_in = place("rows_in", PROJ + 16384, [2, P])
    ACC = 180736
    acc = place("acc", ACC, [2, CW])
    yt_hi = place("yt_hi", 184832, [8, SEQ], F32R)
    yt_lo = place("yt_lo", 193024, [8, SEQ], F32R)
    SCR = 201216
    arow = place("arow", SCR, [2, CW])
    tmp = place("tmp", SCR + 4096, [2, 2, SEQ])
    ident = const[:, C_IDENT:C_IDENT + P]
    ones = const[:, C_ONES:C_ONES + P]

    ps = [nc.alloc_psum_tensor(f"ps{i}", [P, CW], F32) for i in range(8)]
    ps_gemm = ps[0:4]
    ps_ada = ps[4]
    ps_turn = ps[5:8]

    scratch = nc.dram_tensor("ada_scratch", [6 * D], F32, kind="Internal").ap()

    sems = {}

    def sem(name):
        if name not in sems:
            sems[name] = nc.alloc_semaphore(name)
        return sems[name]

    loaded = [sem(f"loaded{i}") for i in range(RAW)]
    raw_used, hi_ready, w_used = sem("raw_used"), sem("hi_ready"), sem("w_used")
    evac_done = sem("evac_done")
    ada_half, ada_summed, ada_evac = sem("ada_half"), sem("ada_summed"), sem("ada_evac")
    ada_stored = [sem("ada_stored0"), sem("ada_stored1")]
    turn_filled, turn_scaled = sem("turn_filled"), sem("turn_scaled")
    turn_hi, turn_lo = sem("turn_hi"), sem("turn_lo")
    start = sem("start_loaded")

    def wview(name):
        return A[name].rearrange("o (c p) n -> p (o c) n", p=P)

    at = dict(q=0, w=0, c=0, a=0)
    NADA = 8
    g_ada = Gemm(at, None, 0, 8, None, ada=NADA)
    lhs_x = lambda part, k, t: (xt_lo if part else xt_hi)[:, k, t * P:(t + 1) * P]
    lhs_y = lambda part, k, t: (yt_lo if part else yt_hi)[:, k, t * P:(t + 1) * P]
    g_in = Gemm(at, wview("w_in"), KD, 16, lhs_x, ada=NADA)
    g_in2 = Gemm(at, wview("w_in"), KD, 1, lhs_x, col0=8192, width=NIN - 8192)

    def sync_gemm(sp, g):
        w_ada = wview("w_ada")

        def chunk(u, j, before):
            for kind, s, q, w in g.slots(u, j):
                if (q + (1 - RAW)).above_zero:
                    sp.wait_ge(raw_used, (q + (1 - RAW)).value)
                if kind == "ada":
                    a = Count(g.a + u, 2, j).times(CW).value
                    src = w_ada[:, 2 * s:2 * s + 2, bass.ds(a, CW)]
                    width = CW
                else:
                    first, step = g.col(u)
                    src = halves(g, u)[:, 2 * s:2 * s + 2, bass.ds(Count(first, step, j).value, g.width)]
                    width = g.width
                sp.dma_start(raw[:, q % RAW, :, 0:width], src).then_inc(loaded[q % RAW], 16)
        in_pairs(sp, g, chunk, lambda n: None)

    def scalar_gemm(act, g, evac):
        def hook(u, j):
            if g.S and evac:
                c = Count(g.c + u, 2, j)
                act.wait_ge(w_used, Count(g.w + (u + 1) * g.S, 2 * g.S, j).value)
                evac(c, u, j)
            if g.ada:
                a = Count(g.a + u, 2, j)
                par = a % 2
                act.wait_ge(ada_summed, (a + 1).value)
                act.wait_ge(ada_stored[par], ((a.times(16, 2) if par == 0 else (a - 1).times(16, 2)) + 16).value)
                act.activation(arow[0:1, par, :], ps_ada[0:1, :], ACT.Copy).then_inc(ada_evac, 1)
                act.wait_ge(ada_evac, (a + 1).value)
                act.dma_start(scratch[bass.ds(a.times(CW).value, CW)].rearrange("(o n) -> o n", o=1),
                              arow[0:1, par, :]).then_inc(ada_stored[par], 16)

        def chunk(u, j, before):
            for n, (kind, s, q, w) in enumerate(g.slots(u, j)):
                if n == g.qper // 2 and before:
                    hook(u - 1, j)
                if kind == "w":
                    act.wait_ge(loaded[q % RAW], (q.times(16, RAW) + 16).value)
                    if (w + (1 - HI)).above_zero:
                        act.wait_ge(w_used, (w + (1 - HI)).value)
                    act.activation(w_hi[:, w % HI, :, 0:g.width], raw[:, q % RAW, :, 0:g.width],
                                   ACT.Copy).then_inc(hi_ready, 1)
        in_pairs(act, g, chunk, lambda n: hook(n - 1, None))

    def vector_gemm(dve, g, evac=None):
        def hook(u, j):
            if evac:
                dve.wait_ge(w_used, Count(g.w + (u + 1) * g.S, 2 * g.S, j).value)
                evac(Count(g.c + u, 2, j), u, j)

        def chunk(u, j, before):
            for n, (kind, s, q, w) in enumerate(g.slots(u, j)):
                if n == g.qper // 2 and before:
                    hook(u - 1, j)
                if kind == "w":
                    dve.wait_ge(hi_ready, (w + 1).value)
                    if (w + (1 - LO)).above_zero:
                        dve.wait_ge(w_used, (w + (1 - LO)).value)
                    dve.tensor_tensor(w_lo[:, w % LO, :, 0:g.width], raw[:, q % RAW, :, 0:g.width],
                                      w_hi[:, w % HI, :, 0:g.width].bitcast(F32),
                                      ALU.subtract).then_inc(raw_used, 1)
                else:
                    a = Count(g.a + u, 2, j)
                    part = acc[:, a % 2, :]
                    dve.wait_ge(loaded[q % RAW], (q.times(16, RAW) + 16).value)
                    if s == 0:
                        if (a - 1).above_zero:
                            dve.wait_ge(ada_summed, (a - 1).value)
                        dve.tensor_scalar(part, raw[:, q % RAW, 0, :], ccol[:, 0:1], None,
                                          ALU.mult).then_inc(ada_half, 1)
                    else:
                        dve.wait_ge(raw_used, (q + (0 if not g.S else -1)).value)
                        dve.scalar_tensor_tensor(part, raw[:, q % RAW, 0, :], ccol[:, 2 * s:2 * s + 1],
                                                 part, ALU.mult, ALU.add).then_inc(ada_half, 1)
                    dve.wait_ge(ada_half, Count((g.a + u) * NADA + s + 1, 2 * NADA, j).value)
                    dve.scalar_tensor_tensor(part, raw[:, q % RAW, 1, :], ccol[:, 2 * s + 1:2 * s + 2],
                                             part, ALU.mult, ALU.add).then_inc(raw_used, 1)
        in_pairs(dve, g, chunk, lambda n: hook(n - 1, None))

    def tensor_gemm(pe, g, middle=None):
        def hook(u, j):
            if g.ada:
                a = Count(g.a + u, 2, j)
                pe.wait_ge(raw_used, Count(g.q + (u + 1) * g.qper, 2 * g.qper, j).value)
                if a.above_zero:
                    pe.wait_ge(ada_evac, a.value)
                pe.matmul(ps_ada[0:1, :], ones[:, 0:1], acc[:, a % 2, :], start=True,
                          stop=True).then_inc(ada_summed, 1)
            if middle:
                middle(u, j)

        def chunk(u, j, before):
            c = Count(g.c + u, 2, j)
            bank = ps_gemm[2 * (c % 2):2 * (c % 2) + 2]
            if g.S:
                if (c - 1).above_zero:
                    pe.wait_ge(evac_done, (c - 1).value)
            for n, (kind, s, q, w) in enumerate(g.slots(u, j)):
                if n == g.qper // 2 and before:
                    hook(u - 1, j)
                if kind != "w":
                    continue
                pe.wait_ge(raw_used, (q + 1).value)
                for k in range(2):
                    for t in range(T):
                        for n3, (part, weights) in enumerate(((0, w_hi[:, w % HI]), (0, w_lo[:, w % LO]),
                                                              (1, w_hi[:, w % HI]))):
                            mm = pe.matmul(bank[t][:, 0:g.width], g.lhs(part, 2 * s + k, t),
                                           weights[:, k, 0:g.width],
                                           start=(s == 0 and k == 0 and n3 == 0),
                                           stop=(s == g.S - 1 and k == 1 and n3 == 2))
                mm.then_inc(w_used, 1)
        in_pairs(pe, g, chunk, lambda n: hook(n - 1, None))

    turns = dict(n=0, split=0)

    class Turn:

        def __init__(self, src, k, hi, lo, scale=None, bias=None):
            self.src, self.units, self.hi, self.lo, self.scale, self.bias = src, k // 2, hi, lo, scale, bias
            self.at, self.at_split = turns["n"], turns["split"]
            turns["n"] += self.units
            turns["split"] += self.units

        def tensor(self, pe):
            for v in range(self.units):
                n = self.at + v
                if n - 2 > 0:
                    pe.wait_ge(turn_scaled, n - 2)
                for k in range(2):
                    for t in range(T):
                        mm = pe.transpose(ps_turn[n % 3][:, k * SEQ + t * P:k * SEQ + (t + 1) * P],
                                          self.src(2 * v + k, t), ident)
                mm.then_inc(turn_filled, 1)

        def vector(self, dve):
            def low(v):
                n = self.at_split + v
                dve.wait_ge(turn_hi, n + 1)
                dve.tensor_tensor(self.lo[:, 2 * v:2 * v + 2, :], tmp[:, n % 2, :, :],
                                  self.hi[:, 2 * v:2 * v + 2, :].bitcast(F32),
                                  ALU.subtract).then_inc(turn_lo, 1)
            for v in range(self.units):
                n, m = self.at + v, self.at_split + v
                dve.wait_ge(turn_filled, n + 1)
                if m - 1 > 0:
                    dve.wait_ge(turn_lo, m - 1)
                for k in range(2):
                    kk = 2 * v + k
                    src = ps_turn[n % 3][:, k * SEQ:(k + 1) * SEQ]
                    if self.scale is None:
                        last = dve.tensor_copy(tmp[:, m % 2, k, :], src)
                    elif self.bias is None:
                        last = dve.tensor_scalar(tmp[:, m % 2, k, :], src, self.scale(kk), None, ALU.mult)
                    else:
                        last = dve.tensor_scalar(tmp[:, m % 2, k, :], src, self.scale(kk), self.bias(kk),
                                                 ALU.mult, ALU.add)
                last.then_inc(turn_scaled, 1)
                if v:
                    low(v - 1)
            low(self.units - 1)

        def scalar(self, act):
            for v in range(self.units):
                n, m = self.at + v, self.at_split + v
                act.wait_ge(turn_scaled, n + 1)
                act.activation(self.hi[:, 2 * v:2 * v + 2, :], tmp[:, m % 2, :, :],
                               ACT.Copy).then_inc(turn_hi, 1)

    class Plain:

        def __init__(self, units):
            self.units, self.at = units, turns["n"]
            turns["n"] += len(units)

        def tensor(self, pe):
            for v, (ins, _) in enumerate(self.units):
                n = self.at + v
                pe.wait_ge(turn_scaled, n - 2)
                for src, rows_out, col in ins:
                    mm = pe.transpose(ps_turn[n % 3][0:rows_out, col:col + src.shape[0]], src,
                                      ident[0:src.shape[0], 0:src.shape[0]])
                mm.then_inc(turn_filled, 1)

        def vector(self, dve):
            for v, (_, copy) in enumerate(self.units):
                n = self.at + v
                dve.wait_ge(turn_filled, n + 1)
                copy(ps_turn[n % 3]).then_inc(turn_scaled, 1)

        @property
        def end(self):
            return self.at + len(self.units)

    turn_x = Turn(lambda k, t: xn[:, t, k * P:(k + 1) * P], KD, xt_hi, xt_lo,
                  scale=lambda k: scol[:, 0, k:k + 1], bias=lambda k: adacol[:, 0, k:k + 1])

    start_turned, start_cols, c_ready = sem("start_turned"), sem("start_cols"), sem("c_ready")
    ssq, root, inverse, xn_ready = sem("ssq"), sem("root"), sem("inverse"), sem("xn_ready")
    rms_n = dict(n=0)
    brd = place("brd", SM + 1600, [176])
    rope1 = place("rope1", SM + 2304, [2, T, 32])
    hstat = place("hstat", SM + 2816, [6, T * 8])
    posf = place("posf", SM + 3200, [2, T])
    posi = place("posi", SCR + 9216, [P], I32)
    posr = place("posr", SCR + 9728, [P])
    pesum = place("pesum", SM + 3296, [T])
    mst = place("mst", SM + 3328, [4, T * 8])
    adar = place("adar", SCR + 8192, [2, P])
    etmp = place("etmp", SCR + 9216, [CW])

    def rowcols(name, k=0):
        return cols[:, ROWS[name][0] + k:ROWS[name][0] + k + 1]

    class Rms:

        def __init__(self, srcs, width, junk, col):
            self.srcs, self.width, self.junk, self.col = srcs, width, junk, col
            self.n = rms_n["n"]
            rms_n["n"] += 1

        def scalar(self, act):
            m = len(self.srcs)
            for i, s in enumerate(self.srcs):
                last = act.activation(self.junk(i), s, ACT.Square,
                                      accum_out=stat[:, self.col + i:self.col + i + 1])
            last.then_inc(ssq, 1)
            act.wait_ge(ssq, self.n + 1)
            act.activation(stat[:, self.col + m:self.col + 2 * m], stat[:, self.col:self.col + m],
                           ACT.Sqrt, bias=epsc[:, 0:1], scale=1.0 / self.width).then_inc(root, 1)

        def vector(self, dve):
            m = len(self.srcs)
            dve.wait_ge(root, self.n + 1)
            dve.reciprocal(stat[:, self.col + 2 * m:self.col + 3 * m],
                           stat[:, self.col + m:self.col + 2 * m]).then_inc(inverse, 1)
            dve.wait_ge(inverse, self.n + 1)
            return lambda i: stat[:, self.col + 2 * m + i:self.col + 2 * m + i + 1]

    epsc = place("epsc", SM + 3264, [4])
    eps_set = sem("eps_set")
    rms_x = Rms([x[:, t, :] for t in range(T)], D, lambda i: xn[:, i, :], 0)
    adar_loaded, adar_turned, adacol_ready = sem("adar_loaded"), sem("adar_turned"), sem("adacol_ready")

    BL = 3 * P
    H = 8
    Q0, K0, V0, GA0, GB0 = 1088, 2112, 3136, 4160, 6208
    qsb = place("qsb", XT, [H, SEQ])
    ksb = place("ksb", XT + 8192, [H, SEQ])
    zs = place("zs", XT + 16384, [H, BL])
    ez = place("ez", 184832, [H, BL])
    mz = place("mz", GT2, [H, BL])
    sb_scale = 128 ** -0.5

    def sb_unit(dst, c0, u, scale):
        ins = [(proj[:, t, c0 + (2 * u + k) * P:c0 + (2 * u + k + 1) * P], P, k * SEQ + t * P)
               for k in range(2) for t in range(T)]

        def copy(bank):
            o = dst[:, 2 * u:2 * u + 2, :].rearrange("p a b -> p (a b)")
            return nc.vector.tensor_scalar(o, bank[:, :], scale, None, ALU.mult)
        return ins, copy
    turn_sb = Plain([sb_unit(d, c, u, s) for u in range(H // 2)
                     for d, c, s in ((qsb, Q0, sb_scale), (ksb, K0, 1.0))])
    z_filled, z_copied, z_abs, z_soft = sem("z_filled"), sem("z_copied"), sem("z_abs"), sem("z_soft")
    m_ready, lb_ready = sem("m_ready"), sem("lb_ready")
    tail_filled, arg_ready, a_ready = sem("tail_filled"), sem("arg_ready"), sem("a_ready")
    yb_filled, yb_hi, yb_lo = sem("yb_filled"), sem("yb_hi"), sem("yb_lo")
    gates_ready = sem("gates_ready")

    def keys_by_queries(pe, bank, lhs, rhs, start=True, stop=True):
        pe.matmul(bank[:, 0:SEQ], lhs(0), rhs(0, SEQ), start=start, stop=stop)
        return pe.matmul(bank[:, SEQ:BL], lhs(1), rhs(P, SEQ), start=start, stop=stop)

    def sb_tensor(pe):
        turn_sb.tensor(pe)
        masks = const[:, C_MASKS:C_MASKS + P]
        for h in range(H):
            pe.wait_ge(turn_scaled, turn_sb.at + 2 * (h // 2) + 2)
            if h - 3 > 0:
                pe.wait_ge(z_copied, h - 3)
            b = ps_gemm[h % 4]
            pe.matmul(b[:, 0:SEQ], ksb[:, h, 0:P], qsb[:, h, :], start=True, stop=False)
            pe.matmul(b[:, 0:P], ident, masks, start=False, stop=True)
            pe.matmul(b[:, SEQ:BL], ksb[:, h, P:SEQ], qsb[:, h, P:SEQ], start=True, stop=False)
            pe.matmul(b[:, SEQ:BL], ident, masks, start=False, stop=True).then_inc(z_filled, 1)
        after = const[:, C_AFTER:C_AFTER + P]
        for h in range(H):
            pe.wait_ge(m_ready, h // 4 + 1)
            pe.wait_ge(z_copied, H)
            if h - 3 > 0:
                pe.wait_ge(arg_ready, h - 3)
            b = ps_gemm[h % 4]
            pe.matmul(b[:, 0:SEQ], after, mz[:, h, 0:SEQ], start=True, stop=False)
            pe.matmul(b[:, P:SEQ], ones, mz[:, h, SEQ:BL], start=False, stop=True)
            pe.matmul(b[:, SEQ:BL], after, mz[:, h, SEQ:BL], start=True, stop=True).then_inc(tail_filled, 1)
        for h in range(H):
            pe.wait_ge(a_ready, h + 1)
            if h % 2 == 0:
                if h // 2 - 2 > 0:
                    pe.wait_ge(yb_lo, h // 2 - 2)
            b = ps_turn[(h // 2) % 3][:, (h % 2) * SEQ:(h % 2 + 1) * SEQ]
            v = lambda t: proj[:, t, V0 + h * P:V0 + (h + 1) * P]
            pe.matmul(b, v(0), zs[:, h, 0:SEQ], start=True, stop=False)
            mm = pe.matmul(b[:, P:SEQ], v(1), zs[:, h, SEQ:BL], start=False, stop=True)
            if h % 2:
                mm.then_inc(yb_filled, 1)

    def sb_vector(dve):
        turn_sb.vector(dve)
        for h in range(H):
            dve.wait_ge(z_filled, h + 1)
            dve.tensor_copy(zs[:, h, :], ps_gemm[h % 4][:, 0:BL]).then_inc(z_copied, 1)
        for f in range(2):
            zf, ef = (b[:, 4 * f:4 * f + 4, :].rearrange("p a b -> p (a b)") for b in (zs, ez))
            dve.wait_ge(z_copied, 4 * f + 4)
            dve.scalar_tensor_tensor(ef, zf, -1.0, zf, ALU.mult, ALU.max).then_inc(z_abs, 1)
        for f in range(2):
            zf, ef, mf = (b[:, 4 * f:4 * f + 4, :].rearrange("p a b -> p (a b)") for b in (zs, ez, mz))
            dve.wait_ge(z_soft, f + 1)
            dve.scalar_tensor_tensor(mf, zf, 0.0, ef, ALU.max, ALU.add).then_inc(m_ready, 1)
            dve.wait_ge(m_ready, f + 1)
            dve.scalar_tensor_tensor(zf, zf, 0.0, ef, ALU.min, ALU.subtract).then_inc(lb_ready, 1)
        for h in range(H):
            dve.wait_ge(lb_ready, h // 4 + 1)
            dve.wait_ge(tail_filled, h + 1)
            dve.tensor_tensor(zs[:, h, :], zs[:, h, :], ps_gemm[h % 4][:, 0:BL],
                              ALU.subtract).then_inc(arg_ready, 1)
        for u in range(H // 2):
            dve.wait_ge(yb_hi, u + 1)
            dve.tensor_tensor(yt_lo[:, 2 * u:2 * u + 2, :].rearrange("p a b -> p (a b)"), ps_turn[u % 3][:, :],
                              yt_hi[:, 2 * u:2 * u + 2, :].rearrange("p a b -> p (a b)").bitcast(F32),
                              ALU.subtract).then_inc(yb_lo, 1)

    def sb_scalar(act):
        for f in range(2):
            ef = ez[:, 4 * f:4 * f + 4, :].rearrange("p a b -> p (a b)")
            act.wait_ge(z_abs, f + 1)
            act.activation(ef, ef, ACT.Exp, scale=-1.0).then_inc(z_abs2, 1)
        for f in range(2):
            ef = ez[:, 4 * f:4 * f + 4, :].rearrange("p a b -> p (a b)")
            act.wait_ge(z_abs2, f + 1)
            act.activation(ef, ef, ACT.Ln, bias=ones[:, 0:1]).then_inc(z_soft, 1)
        for h in range(H):
            act.wait_ge(arg_ready, h + 1)
            act.activation(zs[:, h, :], zs[:, h, :], ACT.Exp).then_inc(a_ready, 1)
        for u in range(H // 2):
            act.wait_ge(yb_filled, u + 1)
            act.activation(yt_hi[:, 2 * u:2 * u + 2, :].rearrange("p a b -> p (a b)"), ps_turn[u % 3][:, :],
                           ACT.Copy).then_inc(yb_hi, 1)

    def gates_scalar(act):
        for t in range(T):
            act.activation(proj[:, t, GA0:NIN], proj[:, t, GA0:NIN], ACT.Sigmoid).then_inc(gates_ready, 1)
    z_abs2 = sem("z_exp")

    g_psb = Gemm(at, wview("w_proj_sb"), 8, 4, lhs_y)

    lat_sq = place("lat_sq", GT2, [4, CW])
    rms_lat = Rms([proj[:, t, L * CW:(L + 1) * CW] for L in range(2) for t in range(T)], CW,
                  lambda i: lat_sq[:, i, :], 8)
    lat = [(place(f"lat{L}_hi", XT + 8192 * L, [4, SEQ], F32R), place(f"lat{L}_lo", XT + 8192 * L + 4096, [4, SEQ], F32R))
           for L in range(2)]
    turn_lat = [Turn(lambda k, t, L=L: proj[:, t, L * CW + k * P:L * CW + (k + 1) * P], 4, *lat[L],
                     scale=lambda k, L=L: rowcols(("gql", "gkv")[L], k)) for L in range(2)]
    lat_scaled = sem("lat_scaled")
    g_uq = Gemm(at, wview("w_uq"), 4, 3, lambda part, k, t: lat[0][part][:, k, t * P:(t + 1) * P])
    g_ukv = Gemm(at, wview("w_ukv"), 4, 4, lambda part, k, t: lat[1][part][:, k, t * P:(t + 1) * P])
    kv = place("kv", XT + 16384, [T, 2048])
    qtm = lambda t, a, b: proj[:, t, Q0 + a:Q0 + b]
    HQ, ROPE = 192, 64
    qk_sq = place("qk_sq", GT2, [T, 1536])
    pe_in = place("pe_in", GT2, [T, 16, ROPE])
    pe_out = place("pe_out", GT2 + 8192, [T, 16, ROPE])
    pe_tmp = place("pe_tmp", ACC, [T, 16, 32])
    kT = place("kT", XT, [12, SEQ])
    qT = lambda m: proj[:, m // 6, 2624 + 256 * (m % 6):2624 + 256 * (m % 6 + 1)]

    pos_float = sem("pos_float")

    def start_tensor(pe):
        pe.wait_ge(start, 16 * NSTART)
        pe.transpose(ps_turn[0][:, 0:P], rows_in[:, 0, :], ident)
        pe.transpose(ps_turn[0][:, P:P + 62], rows_in[0:62, 1, :], ident[0:62, 0:62])
        pe.wait_ge(pos_float, 1)
        pe.transpose(ps_turn[0][:, 192:192 + T], posr[0:T, :], ident[0:T, 0:T]).then_inc(start_turned, 1)

    def start_vector(dve):
        dve.memset(epsc[:, :], EPS).then_inc(eps_set, 1)
        dve.wait_ge(start, 16 * NSTART)
        dve.tensor_copy(posr[0:T, :], posi[0:T, :]).then_inc(pos_float, 1)
        dve.wait_ge(start_turned, 1)
        dve.tensor_copy(cols[:, :], ps_turn[0][:, 0:P]).then_inc(start_cols, 1)
        dve.tensor_copy(posf[:, 0, :], ps_turn[0][:, 192:192 + T]).then_inc(start_cols, 1)
        dve.tensor_copy(colb[:, 0:62], ps_turn[0][:, P:P + 62]).then_inc(start_cols, 1)
        inv = rms_x.vector(dve)
        for t in range(T):
            dve.tensor_scalar(xn[:, t, :], x[:, t, :], inv(t), None, ALU.mult).then_inc(xn_ready, 1)
        dve.wait_ge(c_ready, 1)

    def start_scalar(act):
        for par in range(2):
            act.sem_inc(ada_stored[par], 16)
        act.wait_ge(start, 16 * NSTART)
        act.wait_ge(eps_set, 1)
        rms_x.scalar(act)
        act.wait_ge(start_cols, 3)
        act.activation(ccol[:, :], cols[:, ROWS["c"][0]:ROWS["c"][0] + 16], ACT.Silu).then_inc(c_ready, 1)

    adar_rows = dict(n=0)

    class AdaColumns:

        def __init__(self, first, gain, stored):
            self.first, self.gain, self.stored = first, gain, stored
            self.n = adar_rows["n"]
            adar_rows["n"] += 1

        def scalar(self, act):
            for par in range(2):
                act.wait_ge(ada_stored[par], 16 * (self.stored // 2) + 16)
            if self.n:
                act.wait_ge(adar_turned, self.n)
            for i, src in enumerate((scratch, A["b_ada"].rearrange("o n -> (o n)"))):
                act.dma_start(adar[0:32, i, :], src[self.first:self.first + 2 * D].rearrange("(r q) -> r q", q=P)
                              ).then_inc(adar_loaded, 16)

        def tensor(self, pe):
            pe.wait_ge(adar_loaded, 32 * (self.n + 1))
            pe.wait_ge(ada_evac, self.stored)
            pe.matmul(ps_ada[:, 0:32], adar[0:32, 0, :], ident[0:32, 0:32], start=True, stop=False)
            pe.matmul(ps_ada[:, 0:32], adar[0:32, 1, :], ident[0:32, 0:32], start=False,
                      stop=True).then_inc(adar_turned, 1)

        def vector(self, dve):
            dve.wait_ge(adar_turned, self.n + 1)
            dve.tensor_copy(adacol[:, 0, :], ps_ada[:, 0:16]).then_inc(adacol_ready, 1)
            dve.scalar_tensor_tensor(scol[:, 0, :], ps_ada[:, 16:32], 1.0,
                                     cols[:, ROWS[self.gain][0]:ROWS[self.gain][0] + 16],
                                     ALU.add, ALU.mult).then_inc(adacol_ready, 1)
            dve.wait_ge(adacol_ready, 2 * self.n + 2)

    ada1 = AdaColumns(0, "g1", 8)

    def turn_x_tensor(pe):
        pe.wait_ge(xn_ready, 2)
        pe.wait_ge(start_cols, 3)
        turn_x.tensor(pe)
        pe.wait_ge(turn_lo, turn_x.at_split + turn_x.units)

    def evac_proj(c, u, j):
        b = c % 2
        col = Count(CW * u, 2 * CW, j).value
        for t in range(T):
            last = nc.scalar.activation(proj[:, t, bass.ds(col, CW)], ps_gemm[2 * b + t][:, :], ACT.Copy)
        last.then_inc(evac_done, 1)

    def evac_proj_rest(c, u, j):
        b = c % 2
        for t in range(T):
            last = nc.scalar.activation(proj[:, t, 8192:NIN], ps_gemm[2 * b + t][:, 0:NIN - 8192], ACT.Copy)
        last.then_inc(evac_done, 1)


    def lat_vector(dve):
        inv = rms_lat.vector(dve)
        for i in range(4):
            L, t = divmod(i, T)
            c = proj[:, t, L * CW:(L + 1) * CW]
            dve.tensor_scalar(c, c, inv(i), None, ALU.mult).then_inc(lat_scaled, 1)
        for turn in turn_lat:
            turn.vector(dve)

    def lat_tensor(pe):
        pe.wait_ge(lat_scaled, 4)
        for turn in turn_lat:
            turn.tensor(pe)
        pe.wait_ge(turn_lo, turn_lat[1].at_split + 2)

    def rope1_vector(dve):
        two_pi = 2 * np.pi
        c1 = 6.28125
        c2 = float(np.float32(np.round((two_pi - c1) * 2 ** 22) / 2 ** 22))
        c3 = two_pi - c1 - c2
        magic = 1.5 * 2 ** 23
        pi = 3.1415925
        ang, turn_n = rope1[:, 0, :, :], rope1[:, 1, :, :]
        for t in range(T):
            dve.tensor_scalar(ang[:, t, :], const[:, C_FREQ:C_FREQ + 32], posf[:, 0, t:t + 1], None,
                              ALU.mult).then_inc(rope_step, 1)
        dve.wait_ge(rope_step, 2)
        steps = [lambda: dve.tensor_scalar(turn_n, ang, 1 / two_pi, magic, ALU.mult, ALU.add),
                 lambda: dve.tensor_scalar(turn_n, turn_n, magic, None, ALU.subtract)]
        steps += [lambda c=c: dve.scalar_tensor_tensor(ang, turn_n, -c, ang, ALU.mult, ALU.add) for c in (c1, c2, c3)]
        steps += [lambda: dve.tensor_scalar(ang, ang, -pi, pi, ALU.max, ALU.min),
                  lambda: dve.scalar_tensor_tensor(turn_n, ang, -1.0, ang, ALU.mult, ALU.max),
                  lambda: dve.tensor_scalar(turn_n, turn_n, -1.0, np.pi / 2, ALU.mult, ALU.add)]
        for n, step in enumerate(steps):
            step().then_inc(rope_step, 1)
            dve.wait_ge(rope_step, 3 + n)
    rope_step, rope_ready = sem("rope_step"), sem("rope_ready")
    ROPE_STEPS = 10

    def rope1_scalar(act):
        act.wait_ge(rope_step, ROPE_STEPS)
        for i in range(2):
            act.activation(rope1[:, i, :, :], rope1[:, i, :, :], ACT.Sin).then_inc(rope_ready, 1)
    sin1, cos1 = rope1[:, 0, :, :], rope1[:, 1, :, :]

    def evac_scalar_to(dst):
        def evac(c, u, j):
            col = Count(CW * u, 2 * CW, j).value
            for t in range(T):
                last = nc.scalar.activation(dst(t, col), ps_gemm[2 * (c % 2) + t][:, :], ACT.Copy)
            last.then_inc(evac_done, 1)
        return evac

    def evac_gate_b(c, u, j):
        col = Count(GB0 + CW * u, 2 * CW, j).value
        for t in range(T):
            g = proj[:, t, bass.ds(col, CW)]
            last = nc.vector.tensor_tensor(g, ps_gemm[2 * (c % 2) + t][:, :], g, ALU.mult)
        last.then_inc(evac_done, 1)

    sq_ready, sq_used, hn = sem("sq_ready"), sem("sq_used"), sem("head_norm")
    hroot, qk_ready = sem("head_root"), sem("qk_ready")
    q4 = proj[:, :, Q0:Q0 + 1536].rearrange("p t (h d) -> p t h d", d=HQ)
    k4 = kv[:, :, :].rearrange("p t (h d) -> p t h d", d=256)[:, :, :, 0:P]
    sq_q = qk_sq[:, :, :].rearrange("p t (h d) -> p t h d", d=HQ)
    sq_k = place("k_sq", GT2, [T, 8, P])

    def heads_scalar(act):
        act.wait_ge(evac_done, g_ukv.c + 4)
        act.activation(sq_q, q4, ACT.Square).then_inc(sq_ready, 1)
        for t in range(T):
            act.activation(etmp[:, t * 64:(t + 1) * 64], proj[:, t, 1024:1088], ACT.Square,
                           accum_out=pesum[:, t:t + 1])
        act.wait_ge(sq_used, 1)
        act.activation(sq_k[:, :, :, :], k4, ACT.Square).then_inc(sq_ready, 1)
        act.wait_ge(hn, 2)
        act.activation(hstat[:, 2:4, :], hstat[:, 0:2, :], ACT.Sqrt, bias=epsc[:, 0:1],
                       scale=1.0 / HQ).then_inc(hroot, 1)

    def heads_vector(dve):
        hs = lambda i: hstat[:, i, :].rearrange("p (t h) -> p t h", t=T)
        dve.wait_ge(sq_ready, 1)
        dve.tensor_reduce(hs(0), sq_q, AX_X, ALU.add).then_inc(sq_used, 1)
        dve.wait_ge(sq_ready, 2)
        dve.tensor_reduce(hs(1), sq_k[:, :, :, :], AX_X, ALU.add).then_inc(sq_used, 1)
        dve.wait_ge(sq_used, 2)
        for t in range(T):
            dve.tensor_scalar(hs(1)[:, t, :], hs(1)[:, t, :], pesum[:, t:t + 1], None, ALU.add).then_inc(hn, 1)
        dve.wait_ge(hroot, 1)
        dve.reciprocal(hstat[:, 4:6, :], hstat[:, 2:4, :]).then_inc(hn, 1)
        dve.wait_ge(hn, 3)
        iq, ik = hs(4), hs(5)
        dve.tensor_tensor(q4, q4, iq[:, :, :, None].broadcast_to([P, T, 8, HQ]), ALU.mult).then_inc(hn, 1)
        dve.tensor_tensor(k4, k4, ik[:, :, :, None].broadcast_to([P, T, 8, P]), ALU.mult).then_inc(hn, 1)
        kpe = proj[:, :, 1024:1088][:, :, None, :].broadcast_to([P, T, 8, ROPE])
        dve.tensor_tensor(pe_in[:, :, 8:16, :], kpe, ik[:, :, :, None].broadcast_to([P, T, 8, ROPE]),
                          ALU.mult).then_inc(hn, 1)
        dve.wait_ge(hn, 6)
        gq = brd[:, 0:64][:, None, None, :].broadcast_to([P, T, 8, ROPE])
        gk = brd[:, 64:128][:, None, None, :].broadcast_to([P, T, 8, ROPE])
        dve.tensor_tensor(pe_in[:, :, 0:8, :], q4[:, :, :, P:HQ], gq, ALU.mult).then_inc(hn, 1)
        dve.tensor_tensor(pe_in[:, :, 8:16, :], pe_in[:, :, 8:16, :], gk, ALU.mult).then_inc(hn, 1)
        dve.wait_ge(hn, 8)
        dve.wait_ge(rope_ready, 2)
        x1, x2 = pe_in[:, :, :, 0:32], pe_in[:, :, :, 32:64]
        o1, o2 = pe_out[:, :, :, 0:32], pe_out[:, :, :, 32:64]
        cb, sb = (a[:, :, None, :].broadcast_to([P, T, 16, 32]) for a in (cos1, sin1))
        n = 8
        for o, a, b, op in ((o1, cb, sb, ALU.subtract), (o2, sb, cb, ALU.add)):
            dve.tensor_tensor(o, x1, a, ALU.mult).then_inc(hn, 1)
            dve.tensor_tensor(pe_tmp[:, :, :, :], x2, b, ALU.mult).then_inc(hn, 1)
            dve.wait_ge(hn, n + 2)
            dve.tensor_tensor(o, o, pe_tmp[:, :, :, :], op).then_inc(hn, 1)
            n += 3
            dve.wait_ge(hn, n)
        turn_qk.vector(dve)

    def qk_unit(dst, src, u, scale):
        ins = [(src(t, 2 * u + k), P, k * SEQ + t * P) for k in range(2) for t in range(T)]

        def copy(bank):
            if scale is None:
                return nc.vector.tensor_copy(dst(u), bank[:, :])
            return nc.vector.tensor_scalar(dst(u), bank[:, :], scale, None, ALU.mult)
        return ins, copy
    q_dst = lambda u: proj[:, u // 3, 2624 + CW * (u % 3):2624 + CW * (u % 3 + 1)]
    k_dst = lambda u: kT[:, 2 * u:2 * u + 2, :].rearrange("p a b -> p (a b)")
    qn_src = lambda t, h: proj[:, t, Q0 + HQ * h:Q0 + HQ * h + P]
    kn_src = lambda t, h: kv[:, t, 256 * h:256 * h + P]
    pe_src = lambda first: (lambda t, m: pe_out[:, t, first + 2 * (m - 8):first + 2 * (m - 8) + 2, :])
    turn_qk = Plain([qk_unit(q_dst, qn_src, u, colb[:, 60:61]) for u in range(4)]
                    + [qk_unit(k_dst, kn_src, u, colb[:, 61:62]) for u in range(4)]
                    + [qk_unit(q_dst, pe_src(0), u, None) for u in (4, 5)]
                    + [qk_unit(k_dst, pe_src(8), u, None) for u in (4, 5)])

    pbuf = place("pbuf", SCR, [2, BL])
    ptb = place("ptb", GT2, [2, BL])
    mla_scale = HQ ** -0.5
    s_filled, s_max, p_exp, p_ready = sem("s_filled"), sem("s_max"), sem("p_exp"), sem("p_ready")
    p_inv, pt_filled, pt_ready = sem("p_inv"), sem("pt_filled"), sem("pt_ready")
    ya_filled, ya_hi, ya_lo = sem("ya_filled"), sem("ya_hi"), sem("ya_lo")
    SPAN = ((0, P), (P, BL))

    def mla_tensor(pe):
        pe.wait_ge(hn, 14)
        turn_qk.tensor(pe)
        pe.wait_ge(turn_scaled, turn_qk.end)
        for i in range(H + 2):
            if i < H:
                h = i
                if 2 * (h - 1) > 0:
                    pe.wait_ge(p_exp, 2 * (h - 1))
                b, r = ps_gemm[h % 2], slice(64 * (h % 2), 64 * (h % 2) + 64)
                for t, (lo, up) in enumerate(SPAN):
                    pe.matmul(b[:, lo:up], qT(h)[:, t * P:(t + 1) * P], kT[:, h, 0:(t + 1) * P],
                              start=True, stop=False)
                    pe.matmul(b[:, lo:up], qT(8 + h // 2)[r, t * P:(t + 1) * P],
                              kT[r, 8 + h // 2, 0:(t + 1) * P], start=False, stop=False)
                    mm = pe.matmul(b[:, up - P:up], ident, const[:, C_MASKQ:C_MASKQ + P], start=False, stop=True)
                mm.then_inc(s_filled, 1)
            if 1 <= i <= H:
                h = i - 1
                pe.wait_ge(p_ready, h + 1)
                if h - 1 > 0:
                    pe.wait_ge(pt_ready, h - 1)
                b = ps_gemm[2 + h % 2]
                for k in range(3):
                    mm = pe.transpose(b[:, k * P:(k + 1) * P], pbuf[:, h % 2, k * P:(k + 1) * P], ident)
                mm.then_inc(pt_filled, 1)
            if i >= 2:
                h = i - 2
                pe.wait_ge(pt_ready, h + 1)
                if h % 2 == 0:
                    if h // 2 - 2 > 0:
                        pe.wait_ge(ya_lo, h // 2 - 2)
                b = ps_turn[(h // 2) % 3][:, (h % 2) * SEQ:(h % 2 + 1) * SEQ]
                v = lambda t: kv[:, t, 256 * h + P:256 * (h + 1)]
                pe.matmul(b, v(0), ptb[:, h % 2, 0:SEQ], start=True, stop=False)
                mm = pe.matmul(b[:, P:SEQ], v(1), ptb[:, h % 2, SEQ:BL], start=False, stop=True)
                if h % 2:
                    mm.then_inc(ya_filled, 1)

    def mla_vector(dve):
        def low(u):
            dve.wait_ge(ya_hi, u + 1)
            dve.tensor_tensor(yt_lo[:, 2 * u:2 * u + 2, :].rearrange("p a b -> p (a b)"), ps_turn[u % 3][:, :],
                              yt_hi[:, 2 * u:2 * u + 2, :].rearrange("p a b -> p (a b)").bitcast(F32),
                              ALU.subtract).then_inc(ya_lo, 1)
        for i in range(H + 1):
            if i < H:
                h = i
                dve.wait_ge(s_filled, h + 1)
                for t, (lo, up) in enumerate(SPAN):
                    dve.tensor_reduce(mst[:, 0, 2 * h + t:2 * h + t + 1], ps_gemm[h % 2][:, lo:up],
                                      AX_X, ALU.max).then_inc(s_max, 1)
                dve.wait_ge(s_max, 3 * h + 2)
                dve.tensor_scalar(mst[:, 1, 2 * h:2 * h + 2], mst[:, 0, 2 * h:2 * h + 2], -mla_scale, None,
                                  ALU.mult).then_inc(s_max, 1)
            if i >= 1:
                h = i - 1
                dve.wait_ge(p_exp, 2 * h + 2)
                dve.reciprocal(mst[:, 3, 2 * h:2 * h + 2], mst[:, 2, 2 * h:2 * h + 2]).then_inc(p_inv, 1)
                dve.wait_ge(p_inv, h + 1)
                for t, (lo, up) in enumerate(SPAN):
                    last = dve.tensor_scalar(pbuf[:, h % 2, lo:up], pbuf[:, h % 2, lo:up],
                                             mst[:, 3, 2 * h + t:2 * h + t + 1], None, ALU.mult)
                last.then_inc(p_ready, 1)
            if i >= 5 and i % 2:
                low((i - 5) // 2)
        low(2)
        low(3)

    def mla_scalar(act):
        for par in range(2):
            act.wait_ge(ada_stored[par], 16 * 13)
        def high(u):
            act.wait_ge(ya_filled, u + 1)
            act.activation(yt_hi[:, 2 * u:2 * u + 2, :].rearrange("p a b -> p (a b)"), ps_turn[u % 3][:, :],
                           ACT.Copy).then_inc(ya_hi, 1)
        for i in range(H + 1):
            if i < H:
                h = i
                act.wait_ge(s_max, 3 * h + 3)
                if h - 1 > 0:
                    act.wait_ge(pt_filled, h - 1)
                for t, (lo, up) in enumerate(SPAN):
                    act.activation(pbuf[:, h % 2, lo:up], ps_gemm[h % 2][:, lo:up], ACT.Exp,
                                   bias=mst[:, 1, 2 * h + t:2 * h + t + 1], scale=mla_scale,
                                   accum_out=mst[:, 2, 2 * h + t:2 * h + t + 1]).then_inc(p_exp, 1)
            if i >= 1:
                h = i - 1
                act.wait_ge(pt_filled, h + 1)
                act.activation(ptb[:, h % 2, :], ps_gemm[2 + h % 2][:, 0:BL], ACT.Copy).then_inc(pt_ready, 1)
            if i >= 4 and i % 2 == 0:
                high((i - 4) // 2)
        high(3)

    gtr = place("gtr", ACC, [2, CW])
    gt_loaded, gt_filled, gt_ready = sem("gt_loaded"), sem("gt_filled"), sem("gt_ready")

    def gt_scalar(act):
        act.wait_ge(turn_scaled, turn_qk.end)
        for i, src in enumerate((scratch, A["b_ada"].rearrange("o n -> (o n)"))):
            for g in range(2):
                a = (2 + 3 * g) * D
                act.dma_start(gtr[4 * g:4 * g + 4, i, :], src[a:a + D].rearrange("(r q) -> r q", q=CW)
                              ).then_inc(gt_loaded, 16)

    def gt_tensor(pe):
        pe.wait_ge(gt_loaded, 16 * 4)
        for r in range(8):
            if r - 3 > 0:
                pe.wait_ge(gt_ready, r - 3)
            b = ps_gemm[r % 4]
            sel = ident[0:8, r:r + 1].broadcast_to([8, P])
            for i in range(2):
                mm = pe.matmul(b[:, :], sel, gtr[0:8, i, :], start=(i == 0), stop=(i == 1))
            mm.then_inc(gt_filled, 1)

    def gt_vector(dve):
        for r in range(8):
            dve.wait_ge(gt_filled, r + 1)
            g = (gt1, gt2)[r // 4]
            dve.tensor_copy(g[:, CW * (r % 4):CW * (r % 4 + 1)], ps_gemm[r % 4][:, :]).then_inc(gt_ready, 1)

    g_pmla = Gemm(at, wview("w_proj_mla"), 8, 4, lhs_y)
    merge_step = sem("merge_step")

    def evac_merge(c, u, j):
        for t in range(T):
            g = proj[:, t, bass.ds(Count(GA0 + CW * u, 2 * CW, j).value, CW)]
            nc.vector.tensor_tensor(g, ps_gemm[2 * (c % 2) + t][:, :], g, ALU.mult).then_inc(merge_step, 1)
        nc.vector.wait_ge(merge_step, Count(2 * u + 2, 4, j).value)
        for t in range(T):
            g = proj[:, t, bass.ds(Count(GA0 + CW * u, 2 * CW, j).value, CW)]
            gb = proj[:, t, bass.ds(Count(GB0 + CW * u, 2 * CW, j).value, CW)]
            last = nc.vector.tensor_tensor(g, g, gb, ALU.add)
        last.then_inc(evac_done, 1)

    turn_m = Turn(lambda k, t: proj[:, t, GA0 + k * P:GA0 + (k + 1) * P], KD, xt_hi, xt_lo)

    def turn_after(turn, g):
        def tensor(pe):
            pe.wait_ge(evac_done, g.c + g.n)
            turn.tensor(pe)
            pe.wait_ge(turn_lo, turn.at_split + turn.units)
        return tensor

    g_out = Gemm(at, wview("w_out"), KD, 4, lhs_x)
    restmp = place("restmp", SCR, [T, CW])
    res_step = sem("res_step")
    res_n = dict(n=0)

    def evac_residual(g, gate):
        first = res_n["n"]
        res_n["n"] += g.n * T if gate is not None else 0

        def evac(c, u, j):
            col = Count(CW * u, 2 * CW, j).value
            if gate is not None:
                for t in range(T):
                    nc.vector.tensor_tensor(restmp[:, t, :], ps_gemm[2 * (c % 2) + t][:, :],
                                            gate[:, bass.ds(col, CW)], ALU.mult).then_inc(res_step, 1)
                nc.vector.wait_ge(res_step, Count(first + 2 * u + 2, 4, j).value)
            for t in range(T):
                src = restmp[:, t, :] if gate is not None else ps_gemm[2 * (c % 2) + t][:, :]
                xc = x[:, t, bass.ds(col, CW)]
                last = nc.vector.tensor_tensor(xc, xc, src, ALU.add)
            last.then_inc(evac_done, 1)
        return evac
    evac_out = evac_residual(g_out, gt1)

    KF = 5632 // P
    ht_hi = place("ht_hi", GT1, [KF, SEQ], F32R)
    ht_lo = place("ht_lo", GT1 + KF * SEQ * 4, [KF, SEQ], F32R)
    ftmp = place("ftmp", GT1 + 2 * KF * SEQ * 4, [T, CW])
    hbuf = place("hbuf", GT1 + 2 * KF * SEQ * 4 + 4096, [T, CW])
    assert GT1 + 2 * KF * SEQ * 4 + 8192 <= SCR + 4096
    lhs_h = lambda part, k, t: (ht_lo if part else ht_hi)[:, k, t * P:(t + 1) * P]
    silu_done = sem("silu_done")

    class Ffn:

        def __init__(self, name, w_gate, w_up, up0, w_down, scale, bias, gate):
            at_pair = lambda u: ((u % 2) * up0 + CW * (u // 2), CW)
            self.silu0 = silu_n["n"]
            silu_n["n"] += KF // 4
            self.rms = Rms([x[:, t, :] for t in range(T)], D, lambda i: xn[:, i, :], 0)
            self.xn0 = xn_n["n"]
            xn_n["n"] += T
            self.turn = Turn(lambda k, t: xn[:, t, k * P:(k + 1) * P], KD, xt_hi, xt_lo, scale, bias)
            self.g = Gemm(at, None, KD, 2 * KF // 4, lhs_x, cols=at_pair, peeled=2)
            self.g.by_half = (w_gate, w_up)
            self.at, self.at_split = turns["n"], turns["split"]
            turns["n"] += KF // 2
            turns["split"] += KF // 2
            self.down = Gemm(at, w_down, KF, 4, lhs_h)
            self.evac_down = evac_residual(self.down, gate)

        def scalar(self, act, more=lambda act: None):
            act.wait_ge(evac_done, self.before)
            self.rms.scalar(act)
            more(act)
            self.turn.scalar(act)

            def evac(c, u, j):
                if u % 2 == 0:
                    pair = Count(u // 2, 1, j)
                    act.wait_ge(evac_done, c.value)
                    for t in range(T):
                        last = act.activation(ftmp[:, t, :], ps_gemm[2 * (c % 2) + t][:, :], ACT.Silu)
                    last.then_inc(evac_done, 1)
                elif j is not None or u > 1:
                    self.high(act, Count(u // 2 - 1, 1, j))
            scalar_gemm(act, self.g, evac)
            self.high(act, Count(KF // 4 - 1))
            scalar_gemm(act, self.down, None)

        def high(self, act, pair):
            for v in range(2):
                m = Count(self.at_split + 2 * pair.first + v, 2 * pair.per, pair.j)
                n = Count(self.at + 2 * pair.first + v, 2 * pair.per, pair.j)
                act.wait_ge(turn_scaled, (n + 1).value)
                k = Count(4 * pair.first + 2 * v, 4 * pair.per, pair.j).value
                act.activation(ht_hi[:, bass.ds(k, 2), :], tmp[:, v, :, :], ACT.Copy).then_inc(turn_hi, 1)

        def vector(self, dve, more=lambda dve: None):
            inv = self.rms.vector(dve)
            for t in range(T):
                dve.tensor_scalar(xn[:, t, :], x[:, t, :], inv(t), None, ALU.mult).then_inc(xn_ready, 1)
            more(dve)
            self.turn.vector(dve)

            def turned(pair):
                for v in range(2):
                    m = Count(self.at_split + 2 * pair.first + v, 2 * pair.per, pair.j)
                    n = Count(self.at + 2 * pair.first + v, 2 * pair.per, pair.j)
                    dve.wait_ge(turn_filled, (n + 1).value)
                    dve.wait_ge(turn_lo, (m - v).value)
                    dve.tensor_copy(tmp[:, v, :, :].rearrange("p a b -> p (a b)"),
                                    ps_turn[v][:, :]).then_inc(turn_scaled, 1)
                for v in range(2):
                    m = Count(self.at_split + 2 * pair.first + v, 2 * pair.per, pair.j)
                    k = Count(4 * pair.first + 2 * v, 4 * pair.per, pair.j).value
                    dve.wait_ge(turn_hi, (m + 1).value)
                    dve.tensor_tensor(ht_lo[:, bass.ds(k, 2), :], tmp[:, v, :, :],
                                      ht_hi[:, bass.ds(k, 2), :].bitcast(F32), ALU.subtract).then_inc(turn_lo, 1)

            def evac(c, u, j):
                if u % 2 == 0:
                    return
                if j is not None or u > 1:
                    turned(Count(u // 2 - 1, 1, j))
                dve.wait_ge(evac_done, c.value)
                for t in range(T):
                    last = dve.tensor_tensor(hbuf[:, t, :], ps_gemm[2 * (c % 2) + t][:, :], ftmp[:, t, :],
                                             ALU.mult)
                last.then_inc(evac_done, 1)
            vector_gemm(dve, self.g, evac)
            turned(Count(KF // 4 - 1))
            vector_gemm(dve, self.down, self.evac_down)

        def tensor(self, pe, more=lambda pe: None):
            pe.wait_ge(xn_ready, self.xn0 + T + 2)
            more(pe)
            self.turn.tensor(pe)
            pe.wait_ge(turn_lo, self.turn.at_split + self.turn.units)

            def fill(pair, c_end):
                pe.wait_ge(evac_done, c_end.value)
                for v in range(2):
                    n = Count(self.at + 2 * pair.first + v, 2 * pair.per, pair.j)
                    pe.wait_ge(turn_scaled, (n - v).value)
                    for k in range(2):
                        for t in range(T):
                            mm = pe.transpose(ps_turn[v][:, k * SEQ + t * P:k * SEQ + (t + 1) * P],
                                              hbuf[:, t, (2 * v + k) * P:(2 * v + k + 1) * P], ident)
                    mm.then_inc(turn_filled, 1)

            def middle(u, j):
                if u % 2 == 0 and (j is not None or u > 0):
                    fill(Count(u // 2 - 1, 1, j), Count(self.g.c + u, 2, j))
            tensor_gemm(pe, self.g, middle)
            fill(Count(KF // 4 - 1), Count(self.g.c + self.g.n))
            pe.wait_ge(turn_lo, self.at_split + KF // 2)
            tensor_gemm(pe, self.down)
    silu_n, xn_n = dict(n=0), dict(n=0)

    def halves(g, u):
        return g.by_half[u % 2] if g.weights is None else g.weights

    w_f1 = wview("w_ffn_in")
    ada2 = AdaColumns(3 * D, "g2", 24)
    ffn1 = Ffn("ffn1", w_f1, w_f1, 5632, wview("w_ffn_out"),
               lambda k: scol[:, 0, k:k + 1], lambda k: adacol[:, 0, k:k + 1], gt2)
    ffn1.before = g_out.c + g_out.n


    NIN2 = 5184
    XBC, DT, QN, KC0, VC0, KS0, VS0, KW0, VW0, GN = 1024, 2560, 2576, 3600, 3856, 4112, 4368, 4624, 4880, 5136
    P2 = 131072
    proj2 = place("proj2", P2, [T, NIN2])
    w1 = [place("w1k", GT2, [16, 256]), place("w1v", P2 + 41472, [16, 256])]
    SM2 = 197120
    adt = place("adt", SM2, [T, 16])
    dtv = place("dtv", SM2 + 128, [T, 16])
    dtl = place("dtl", SM2 + 256, [T, 16])
    bias3 = place("bias3", SM2 + 384, [3, 16])
    gate2 = place("gate2", SM2 + 576, [T, 16, 3])
    hidT = place("hidT", SM2 + 1024, [4, 60])
    w2 = [place("w2k", SM2 + 2048, [2, 64]), place("w2v", SM2 + 2560, [2, 64])]
    kcmp = place("kcmp", SM2 + 3072, [2, 2, 15])
    cst = place("cst", SM2 + 3328, [4, T * 16])
    ea = place("ea", SM2 + 3840, [16])
    pe_odd = place("pe_odd", SM2 + 3904, [32])

    rms_a = Rms([x[:, t, :] for t in range(T)], D, lambda i: xn[:, i, :], 0)
    xn_a = xn_n["n"]
    xn_n["n"] += T
    turn_a = Turn(lambda k, t: xn[:, t, k * P:(k + 1) * P], KD, xt_hi, xt_lo, lambda k: rowcols("ga", k))
    g_b = Gemm(at, wview("w_in_2"), KD, 10, lhs_x)
    g_b2 = Gemm(at, wview("w_in_2"), KD, 1, lhs_x, col0=5120, width=64)
    w1_loaded = sem("w1_loaded")

    def norm_a_scalar(act):
        act.wait_ge(evac_done, ffn1.down.c + 4)
        for i, kv_ in enumerate("kv"):
            act.dma_start(w1[i][:, :, :], A[f"cmp_w1_{kv_}_2"].rearrange("o (u p) n -> p (o u) n", p=P)
                          ).then_inc(w1_loaded, 16)
            act.dma_start(w2[i][:, :, :], A[f"cmp_w2_{kv_}_2"].rearrange("o (u p) n -> p (o u) n", p=P)
                          ).then_inc(w1_loaded, 16)
        rms_a.scalar(act)
        turn_a.scalar(act)

    def norm_a_vector(dve):
        inv = rms_a.vector(dve)
        for t in range(T):
            dve.tensor_scalar(xn[:, t, :], x[:, t, :], inv(t), None, ALU.mult).then_inc(xn_ready, 1)
        turn_a.vector(dve)

    def norm_a_tensor(pe):
        pe.wait_ge(xn_ready, xn_a + T + 2)
        turn_a.tensor(pe)
        pe.wait_ge(turn_lo, turn_a.at_split + turn_a.units)

    def evac_rest2(c, u, j):
        for t in range(T):
            last = nc.scalar.activation(proj2[:, t, 5120:NIN2], ps_gemm[2 * (c % 2) + t][:, 0:64], ACT.Copy)
        last.then_inc(evac_done, 1)

    PADW = 3 + SEQ
    xbcT = place("xbcT", XT, [12, PADW])
    xc = place("xc", XT + 12544, [12, SEQ])
    gT = place("gT", XT + 24832, [2, BL])
    decay = place("decay", XT + 27904, [3, BL])
    xs = place("xs", PROJ, [T, 1024])
    xdt = place("xdt", PROJ + 8192, [T, 1024])
    ys = place("ys", 188928, [T, 1024])
    turn_xbc = Plain([([(proj2[:, t, XBC + (2 * u + k) * P:XBC + (2 * u + k + 1) * P], P, k * SEQ + t * P)
                        for k in range(2) for t in range(T)],
                       lambda bank, u=u: nc.vector.tensor_copy(xbcT[:, 2 * u:2 * u + 2, 3:PADW],
                                                               bank[:, :].rearrange("p (a b) -> p a b", a=2)))
                      for u in (4, 5, 0, 1, 2, 3)])
    turn_xs = Plain([([(xc[:, 4 * m + k, t * P:(t + 1) * P], P, k * P) for k in range(4)],
                      lambda bank, t=t, m=m: nc.vector.tensor_copy(xs[:, t, 512 * m:512 * (m + 1)], bank[:, :]))
                     for m in range(2) for t in range(T)])
    CONV = [8, 9, 10, 11, 0, 1, 2, 3, 4, 5, 6, 7]
    conv, xc_ready = sem("conv"), sem("xc_ready")
    ssd_v, ssd_v_at = sem("ssd_vector"), steps("pad", "shifted", "abs", "dt", "decay_rate", "bias0", "bias1", "bias2",
                   "g0", "g1", "xdt0", "xdt1")
    ssd_a, ssd_a_at = sem("ssd_scalar"), steps("exp_alog", "exp", "log", "z0", "z1")
    ssd_p, ssd_p_at = sem("ssd_tensor"), steps("sums", "g0", "g1")
    seg_filled, decay_ready, m2_ready, y_filled = sem("seg_filled"), sem("decay_ready"), sem("m2_ready"), sem("y_filled")
    y_step = sem("y_step")
    ps_y, ps_seg = ps[0:4], ps[4:7]
    HS = 16

    def ssd_tensor(pe):
        pe.wait_ge(evac_done, g_b2.c + 1)
        turn_xbc.tensor(pe)
        pe.wait_ge(ssd_v, ssd_v_at["decay_rate"])
        cum, after, maskt = (const[:, c:c + P] for c in (C_CUM, C_AFTER, C_MASKT))
        b = ps[7]
        pe.wait_ge(turn_scaled, turn_xbc.end)
        pe.matmul(b[:, 0:16], cum, adt[:, 0, :], start=True, stop=True)
        pe.matmul(b[:, 16:32], after, adt[:, 0, :], start=True, stop=True)
        pe.matmul(b[:, 32:48], cum, adt[:, 1, :], start=True, stop=True).then_inc(ssd_p, 1)
        for g in range(2):
            pe.wait_ge(xc_ready, 4)
            keys_by_queries(pe, ps_gemm[g], lambda kt: xc[:, 8 + g, kt * P:(kt + 1) * P],
                                         lambda a, z: xc[:, 10 + g, a:z]).then_inc(ssd_p, 1)
        pe.wait_ge(xc_ready, 12)
        pe.wait_ge(ssd_v, ssd_v_at["bias2"])
        turn_xs.tensor(pe)
        pe.wait_ge(ssd_v, ssd_v_at["xdt1"])
        for i in range(HS + 2):
            if i < HS:
                h = i
                if 3 * (h - 2) > 0:
                    pe.wait_ge(decay_ready, 3 * (h - 2))
                b = ps_seg[h % 3]
                rate = lambda t: adt[:, t, h:h + 1].broadcast_to([P, P])
                pe.matmul(b[:, 0:P], rate(0), cum, start=True, stop=False)
                pe.matmul(b[:, 0:P], ident, maskt, start=False, stop=True)
                pe.matmul(b[:, P:BL], rate(1), cum[:, None, :].broadcast_to([P, 2, P]), start=True, stop=False)
                pe.matmul(b[:, 2 * P:BL], ident, maskt, start=False, stop=True).then_inc(seg_filled, 1)
            if i >= 2:
                h = i - 2
                pe.wait_ge(m2_ready, h + 1)
                o = lambda t: ps_y[2 * t + h // 8][:, (h % 8) * 64:(h % 8 + 1) * 64]
                m = lambda k: decay[:, h % 3, k * P:(k + 1) * P]
                v = lambda t: xdt[:, t, h * 64:(h + 1) * 64]
                pe.matmul(o(0), m(0), v(0), start=True, stop=True)
                pe.matmul(o(1), m(1), v(0), start=True, stop=False)
                pe.matmul(o(1), m(2), v(1), start=False, stop=True).then_inc(y_filled, 1)

    def ssd_vector(dve):
        dve.wait_ge(evac_done, g_b2.c + 1)
        dve.memset(xbcT[:, :, 0:3], 0.0).then_inc(ssd_v, 1)
        bc = lambda a: a[:, None, :].broadcast_to([P, T, 16])
        dve.tensor_tensor(dtv[:, :, :], proj2[:, :, DT:DT + 16], bc(brd[:, 128:144]), ALU.add).then_inc(ssd_v, 1)
        dve.wait_ge(ssd_v, ssd_v_at["shifted"])
        dve.scalar_tensor_tensor(dtl[:, :, :], dtv[:, :, :], -1.0, dtv[:, :, :], ALU.mult, ALU.max).then_inc(ssd_v, 1)
        dve.wait_ge(ssd_a, ssd_a_at["log"])
        dve.scalar_tensor_tensor(dtv[:, :, :], dtv[:, :, :], 0.0, dtl[:, :, :], ALU.max, ALU.add).then_inc(ssd_v, 1)
        dve.wait_ge(ssd_v, ssd_v_at["dt"])
        dve.scalar_tensor_tensor(adt[:, :, :], dtv[:, :, :], -1.0, bc(ea[:, :]), ALU.mult, ALU.mult).then_inc(ssd_v, 1)
        turn_xbc.vector(dve)
        for j in range(4):
            for n, c in enumerate(CONV):
                w = colb[:, 12 + 12 * j + c:13 + 12 * j + c]
                src = xbcT[:, c, j:j + SEQ]
                if j == 0:
                    dve.wait_ge(turn_scaled, turn_xbc.at + n // 2 + 1)
                    dve.tensor_scalar(xc[:, c, :], src, w, None, ALU.mult).then_inc(conv, 1)
                else:
                    dve.wait_ge(conv, 12 * (j - 1) + n + 1)
                    dve.scalar_tensor_tensor(xc[:, c, :], src, w, xc[:, c, :], ALU.mult,
                                             ALU.add).then_inc(conv, 1)
        dve.wait_ge(ssd_p, ssd_p_at["sums"])
        b = ps[7]
        dve.tensor_scalar(bias3[:, 0, :], b[:, 0:16], -1.0, None, ALU.mult).then_inc(ssd_v, 1)
        dve.tensor_copy(bias3[:, 1, :], b[:, 16:32]).then_inc(ssd_v, 1)
        dve.tensor_scalar(bias3[:, 2, :], b[:, 32:48], -1.0, None, ALU.mult).then_inc(ssd_v, 1)
        for g in range(2):
            dve.wait_ge(ssd_p, ssd_p_at[f"g{g}"])
            dve.tensor_copy(gT[:, g, :], ps_gemm[g][:, 0:BL]).then_inc(ssd_v, 1)
        turn_xs.vector(dve)
        dve.wait_ge(turn_scaled, turn_xs.end)
        for t in range(T):
            dve.tensor_tensor(xdt[:, t, :].rearrange("p (h d) -> p h d", d=64),
                                           xs[:, t, :].rearrange("p (h d) -> p h d", d=64),
                                           dtv[:, t, :, None].broadcast_to([P, 16, 64]), ALU.mult).then_inc(ssd_v, 1)
        for h in range(HS):
            dve.wait_ge(decay_ready, 3 * h + 3)
            d = decay[:, h % 3, :]
            dve.tensor_tensor(d, d, gT[:, h // 8, :], ALU.mult).then_inc(m2_ready, 1)
        n = 0
        for t in range(T):
            dve.tensor_tensor(ys[:, t, :].rearrange("p (h d) -> p h d", d=64),
                              xs[:, t, :].rearrange("p (h d) -> p h d", d=64),
                              brd[:, 160:176][:, :, None].broadcast_to([P, 16, 64]), ALU.mult).then_inc(y_step, 1)
        dve.wait_ge(y_step, 2)
        dve.wait_ge(y_filled, HS)
        for t in range(T):
            for f in range(2):
                o = ys[:, t, 512 * f:512 * (f + 1)]
                dve.tensor_tensor(o, o, ps_y[2 * t + f][:, :], ALU.add).then_inc(y_step, 1)
        dve.wait_ge(y_step, 6)
        dve.wait_ge(ssd_a, ssd_a_at["z1"])
        for t in range(T):
            dve.tensor_tensor(ys[:, t, :], ys[:, t, :], proj2[:, t, 0:1024], ALU.mult).then_inc(y_step, 1)
        inv = rms_s.vector(dve)
        for t in range(T):
            dve.tensor_scalar(ys[:, t, :], ys[:, t, :], inv(t), None, ALU.mult).then_inc(y_step, 1)

    rms_s = Rms([ys[:, t, :] for t in range(T)], 1024, lambda i: xdt[:, i, :], 0)

    def ssd_scalar(act):
        act.wait_ge(start, 16 * NSTART)
        act.activation(ea[:, :], brd[:, 144:160], ACT.Exp).then_inc(ssd_a, 1)
        act.wait_ge(ssd_v, ssd_v_at["abs"])
        act.activation(dtl[:, :, :], dtl[:, :, :], ACT.Exp, scale=-1.0).then_inc(ssd_a, 1)
        act.wait_ge(ssd_a, ssd_a_at["exp"])
        act.activation(dtl[:, :, :], dtl[:, :, :], ACT.Ln, bias=ones[:, 0:1]).then_inc(ssd_a, 1)
        for n, c in enumerate(CONV):
            act.wait_ge(conv, 36 + n + 1)
            act.activation(xc[:, c, :], xc[:, c, :], ACT.Silu, bias=colb[:, c:c + 1]).then_inc(xc_ready, 1)
        for t in range(T):
            act.activation(proj2[:, t, 0:1024], proj2[:, t, 0:1024], ACT.Silu).then_inc(ssd_a, 1)
        act.wait_ge(ssd_v, ssd_v_at["bias2"])
        for h in range(HS):
            act.wait_ge(seg_filled, h + 1)
            if h - 2 > 0:
                act.wait_ge(y_filled, h - 2)
            for k in range(3):
                act.activation(decay[:, h % 3, k * P:(k + 1) * P], ps_seg[h % 3][:, k * P:(k + 1) * P], ACT.Exp,
                               bias=bias3[:, k, h:h + 1]).then_inc(decay_ready, 1)
        act.wait_ge(y_step, 8)
        rms_s.scalar(act)

    qu = place("qu", XT, [8, SEQ])
    qrT = place("qrT", XT + 8192, [8, SEQ])
    ksw = [proj2[:, br, 0:1024].rearrange("p (a b s) -> p a b s", a=2, b=2) for br in range(2)]
    vcmp = proj2[:, 0, 1024:2048].rearrange("p (g j d) -> p g j d", g=4, j=4)
    fl = [place("flk", XT + 20480, [16, 4, 15]), place("flv", XT + 24320, [16, 4, 15])]
    pc = place("pc", XT + 28160, [T, 16, 32])
    qr = place("qr", PROJ, [T, 1024])
    qp = place("qp", PROJ + 8192, [T, 1024])
    yatt = place("yatt", PROJ + 8192, [T, 1024])
    rt = place("rt", SCR, [4, T, 16, 8])
    hid = place("hid", SCR + 9216, [2, 256])
    pcT = place("pcT", GT2, [8, P])
    cs = place("cs", GT2 + 5120, [T, 16, 15])
    nst = place("nst", GT2 + 8192, [5, 64])
    pb2 = place("pb2", SCR, [2, BL])
    pt2 = place("pt2", SCR + 3072, [4, BL])
    cos2 = const[:, C_COS2:C_COS2 + 16].rearrange("p (t d) -> p t d", t=T)
    sin2 = const[:, C_SIN2:C_SIN2 + 16].rearrange("p (t d) -> p t d", t=T)
    rot = sem("rot")

    def q_unit(dst, src, u):
        ins = [(src[:, t, (2 * u + k) * P:(2 * u + k + 1) * P], P, k * SEQ + t * P)
               for k in range(2) for t in range(T)]
        return ins, lambda bank: nc.vector.tensor_copy(dst[:, 2 * u:2 * u + 2, :].rearrange("p a b -> p (a b)"),
                                                       bank[:, :])

    def k_unit(dst, c0):
        ins = [(proj2[:, t, c0 + k * P:c0 + (k + 1) * P], P, k * SEQ + t * P) for k in range(2) for t in range(T)]

        def copy(bank):
            for b in range(2):
                r = slice(64 * b, 64 * b + 64)
                last = nc.vector.tensor_copy(dst[r, :, b, :], bank[r, :].rearrange("p (a s) -> p a s", a=2))
            return last
        return ins, copy
    turn_nq = Plain([q_unit(qu, qp, u) for u in range(4)]
                    + [q_unit(qrT, qr, u) for u in range(4)]
                    + [k_unit(ksw[0], KS0), k_unit(ksw[1], KW0)])
    cmp_v, cmp_v_at = sem("cmp_vector"), steps("zeros", "pe_odd", *(f"f{n}" for n in range(8)), "hidT", "kc0", "kc1",
                   *(f"vc{j}" for j in range(4)), "cs0", "cs1", "max", "sub", "sum", "inv", "coef", "masked",
                   "pc", "pcT0", "pcT1")
    cmp_a, cmp_a_at = sem("cmp_scalar"), steps("hid0", "hid1", "gates", "exp")
    cmp_p, cmp_p_at = sem("cmp_tensor"), steps("t0", "t1", "t2", "t3", "hid0", "hid1", "hidT", "kc", "vc", "cs0", "cs1",
                   "pcT0", "pcT1")
    nsa_scale = 64 ** -0.5
    n_filled, n_max, n_exp, n_inv, n_ready = (sem(f"nsa_{n}") for n in ("filled", "max", "exp", "inverse", "ready"))
    npt_filled, npt_ready, o_filled, o_ready = (sem(f"nsa_{n}") for n in ("pt_filled", "pt_ready", "o_filled", "o_ready"))
    UN = 32

    def cmp_tensor(pe):
        pe.wait_ge(rot, 14)
        turn_nq.tensor(pe)
        pe.wait_ge(turn_scaled, turn_nq.end)
        pe.wait_ge(y_step, 6)
        for n in range(4):
            c0 = (KC0, VC0)[n // 2] + P * (n % 2)
            for k in range(2):
                for t in range(T):
                    mm = pe.transpose(ps[n][0:64, k * SEQ + t * P:k * SEQ + (t + 1) * P],
                                      proj2[:, t, c0 + 64 * k:c0 + 64 * (k + 1)], ident)
            mm.then_inc(cmp_p, 1)
        pe.wait_ge(w1_loaded, 64)
        for i in range(2):
            pe.wait_ge(cmp_v, cmp_v_at[f"f{4 * i + 3}"])
            for u in range(16):
                mm = pe.matmul(ps[4 + i][0:60, 0:256], fl[i][:, u, :, :].rearrange("p h i -> p (h i)"),
                               w1[i][:, u, :], start=(u == 0), stop=(u == 15))
            mm.then_inc(cmp_p, 1)
        pe.wait_ge(cmp_a, cmp_a_at["hid1"])
        for i in range(2):
            for f in range(2):
                mm = pe.transpose(ps[6][:, 60 * (2 * i + f):60 * (2 * i + f + 1)], hid[0:60, i, f * P:(f + 1) * P],
                                  ident[0:60, 0:60])
        mm.then_inc(cmp_p, 1)
        pe.wait_ge(cmp_v, cmp_v_at["hidT"])
        for f in range(2):
            mm = pe.matmul(ps[7][0:64, 0:60], w2[0][:, f, :], hidT[:, f, :], start=(f == 0), stop=(f == 1))
        mm.then_inc(cmp_p, 1)
        pe.wait_ge(cmp_v, cmp_v_at["hidT"])
        for g in range(4):
            for f in range(2):
                mm = pe.matmul(ps[6][0:15, 256 + 64 * g:256 + 64 * (g + 1)], hidT[:, 2 + f, 15 * g:15 * (g + 1)],
                               w2[1][:, f, :], start=(f == 0), stop=(f == 1))
        mm.then_inc(cmp_p, 1)
        pe.wait_ge(cmp_v, cmp_v_at["kc1"])
        for t in range(T):
            for n in range(8):
                a, i = n // 4, n % 4
                o = ps[4 + t][:, 0:240].rearrange("p (a b i k) -> p a b i k", a=2, b=2, i=4)
                mm = pe.matmul(o[:, a, :, i, :], qu[:, 4 * a + i, t * P:(t + 1) * P], kcmp[:, a, :, :],
                               start=True, stop=True)
            mm.then_inc(cmp_p, 1)
        pe.wait_ge(cmp_v, cmp_v_at["pc"])
        for t in range(T):
            for m in range(4):
                mm = pe.transpose(ps[6 + t][:, m * P:(m + 1) * P],
                                  pc[:, t, 4 * m:4 * m + 4, :].rearrange("p n i -> p (n i)"), ident)
            mm.then_inc(cmp_p, 1)

    def rope2_vector(dve):
        dve.wait_ge(y_step, 10)
        for t in range(T):
            for dst in (qp, qr):
                for a in range(2):
                    at_a = slice(512 * a, 512 * (a + 1))
                    dve.tensor_copy(dst[:, t, at_a].rearrange("p (i b d) -> p i b d", i=4, b=2),
                                    proj2[:, t, QN:QN + 1024][:, at_a].rearrange("p (b i d) -> p i b d", i=4, b=2)
                                    ).then_inc(rot, 1)
        dve.wait_ge(rot, 8)
        n = 8
        jobs = [(qr[:, :, :], 16), (proj2[:, :, KS0:KS0 + 256], 4), (proj2[:, :, KW0:KW0 + 256], 4)]
        for src, heads in jobs:
            v = src.rearrange("p t (h d) -> p t h d", d=64)
            x1, x2 = v[:, :, :, 0:8], v[:, :, :, 8:16]
            c, s = (a[:, :, None, :].broadcast_to([P, T, heads, 8]) for a in (cos2, sin2))
            o = [rt[:, i, :, 0:heads, :] for i in range(4)]
            for dst, a, b in ((o[0], x1, c), (o[1], x2, s), (o[2], x2, c), (o[3], x1, s)):
                last = dve.tensor_tensor(dst, a, b, ALU.mult)
            last.then_inc(rot, 1)
            n += 1
            dve.wait_ge(rot, n)
            dve.tensor_tensor(x1, o[0], o[1], ALU.subtract)
            dve.tensor_tensor(x2, o[2], o[3], ALU.add).then_inc(rot, 1)
            n += 1
            dve.wait_ge(rot, n)
        assert n == 14

    def cmp_vector(dve):
        dve.memset(pc[:, :, :, :], 0.0)
        dve.memset(kcmp[:, :, :, :], 0.0)
        dve.memset(vcmp, 0.0)
        for br in range(2):
            for b in range(2):
                last = dve.memset(ksw[br][64 - 64 * b:P - 64 * b, :, b, :], 0.0)
        last.then_inc(cmp_v, 1)
        r = ROWS["pek"][0]
        dve.tensor_copy(pe_odd[0:64, :], cols[64:P, r:r + 32]).then_inc(cmp_v, 1)
        turn_nq.vector(dve)
        dve.wait_ge(cmp_v, cmp_v_at["pe_odd"])
        for n in range(4):
            dve.wait_ge(cmp_p, cmp_p_at[f"t{n}"])
            i, pair = divmod(n, 2)
            for odd in range(2):
                bank = ps[n][0:64, :]
                for f in range(1):
                    pe_ = (pe_odd[0:64, 16 * i:16 * i + 16] if odd
                           else cols[0:64, r + 16 * i:r + 16 * i + 16])
                    src = bank.rearrange("p (h b u r) -> p r u h b", h=2, b=16, u=8)[:, odd, :, :, :]
                    for half in range(2):
                        last = dve.tensor_tensor(
                            fl[i][64 * odd:64 * odd + 64, 8 * half:8 * half + 8, 2 * pair:2 * pair + 2, :],
                            src[:, :, :, half:half + 15],
                            pe_[:, 8 * half:8 * half + 8][:, :, None, None].broadcast_to([64, 8, 2, 15]), ALU.add)
                last.then_inc(cmp_v, 1)
        dve.wait_ge(cmp_p, cmp_p_at["hidT"])
        dve.tensor_copy(hidT[:, :, :].rearrange("p a b -> p (a b)"), ps[6][:, 0:240]).then_inc(cmp_v, 1)
        dve.wait_ge(cmp_p, cmp_p_at["kc"])
        for b in range(2):
            dve.tensor_copy(kcmp[64 * b:64 * b + 64, :, b, :],
                                         ps[7][0:64, 0:60].rearrange("p (a b i) -> p b a i", a=2, b=2)[:, b, :, :]).then_inc(cmp_v, 1)
        dve.wait_ge(cmp_p, cmp_p_at["vc"])
        for j in range(4):
            dve.tensor_copy(vcmp[32 * j:32 * j + 15, :, j, :],
                                         ps[6][0:15, 256:512].rearrange("p (g d) -> p g d", g=4)).then_inc(cmp_v, 1)
        for t in range(T):
            dve.wait_ge(cmp_p, cmp_p_at[f"cs{t}"])
            madd = const[:, C_CMPADD + 15 * t:C_CMPADD + 15 * (t + 1)]
            dve.scalar_tensor_tensor(cs[:, t, :, :], ps[4 + t][:, 0:240].rearrange("p (n i) -> p n i", n=16),
                                                  nsa_scale, madd[:, None, :].broadcast_to([P, 16, 15]),
                                                  ALU.mult, ALU.add).then_inc(cmp_v, 1)
        st = lambda i: cst[:, i, :].rearrange("p (t n) -> p t n", t=T)
        wide = lambda i: st(i)[:, :, :, None].broadcast_to([P, T, 16, 15])
        dve.wait_ge(cmp_v, cmp_v_at["cs1"])
        dve.tensor_reduce(st(0), cs[:, :, :, :], AX_X, ALU.max).then_inc(cmp_v, 1)
        dve.wait_ge(cmp_v, cmp_v_at["max"])
        dve.tensor_tensor(cs[:, :, :, :], cs[:, :, :, :], wide(0), ALU.subtract).then_inc(cmp_v, 1)
        dve.wait_ge(cmp_a, cmp_a_at["exp"])
        dve.tensor_reduce(st(1), cs[:, :, :, :], AX_X, ALU.add).then_inc(cmp_v, 1)
        dve.wait_ge(cmp_v, cmp_v_at["sum"])
        dve.reciprocal(st(2), st(1)).then_inc(cmp_v, 1)
        dve.wait_ge(cmp_v, cmp_v_at["inv"])
        dve.wait_ge(cmp_a, cmp_a_at["gates"])
        dve.tensor_tensor(st(3), st(2), gate2[:, :, :, 0], ALU.mult).then_inc(cmp_v, 1)
        mmul = const[:, C_CMPMUL:C_CMPMUL + 30].rearrange("p (t i) -> p t i", t=T)
        dve.tensor_tensor(cs[:, :, :, :], cs[:, :, :, :],
                                       mmul[:, :, None, :].broadcast_to([P, T, 16, 15]), ALU.mult).then_inc(cmp_v, 1)
        dve.wait_ge(cmp_v, cmp_v_at["masked"])
        dve.tensor_tensor(pc[:, :, :, 0:15], cs[:, :, :, :], wide(3), ALU.mult).then_inc(cmp_v, 1)
        for t in range(T):
            dve.wait_ge(cmp_p, cmp_p_at[f"pcT{t}"])
            dve.tensor_copy(pcT[:, 4 * t:4 * t + 4, :].rearrange("p a b -> p (a b)"), ps[6 + t][:, :]).then_inc(cmp_v, 1)

    def cmp_scalar(act):
        for i in range(2):
            act.wait_ge(cmp_p, cmp_p_at[f"hid{i}"])
            act.activation(hid[0:60, i, :], ps[4 + i][0:60, 0:256], ACT.Silu).then_inc(cmp_a, 1)
        act.activation(gate2[:, :, :, :].rearrange("p t n b -> p t (n b)"), proj2[:, :, GN:NIN2],
                                    ACT.Sigmoid).then_inc(cmp_a, 1)
        act.wait_ge(cmp_v, cmp_v_at["sub"])
        act.activation(cs[:, :, :, :].rearrange("p t n i -> p (t n i)"),
                                    cs[:, :, :, :].rearrange("p t n i -> p (t n i)"), ACT.Exp).then_inc(cmp_a, 1)

    ps_o, ps_s, ps_pt = ps[0:4], ps[4:6], ps[6:8]

    def nsa_tensor(pe):
        pe.wait_ge(cmp_v, cmp_v_at["pcT1"])
        for i in range(UN + 3):
            if i < UN:
                n, br = divmod(i, 2)
                a, b, m = n // 8, n // 4 % 2, n % 4
                if 2 * (i - 1) > 0:
                    pe.wait_ge(n_exp, 2 * (i - 1))
                bank = ps_s[i % 2]
                for t, (lo, up) in enumerate(SPAN):
                    pe.matmul(bank[:, lo:up], qrT[:, 4 * a + m, t * P:(t + 1) * P],
                              ksw[br][:, a, b, 0:(t + 1) * P],
                              start=True, stop=False)
                    mm = pe.matmul(bank[:, up - P:up], ident, const[:, C_MASKQ:C_MASKQ + P], start=False, stop=True)
                mm.then_inc(n_filled, 1)
            if 1 <= i <= UN:
                w = i - 1
                pe.wait_ge(n_ready, w + 1)
                if w - 1 > 0:
                    pe.wait_ge(npt_ready, w - 1)
                for k in range(3):
                    mm = pe.transpose(ps_pt[w % 2][:, k * P:(k + 1) * P], pb2[:, w % 2, k * P:(k + 1) * P], ident)
                mm.then_inc(npt_filled, 1)
            if i >= 3 and i % 2 == 1:
                n = (i - 3) // 2
                pe.wait_ge(npt_ready, 2 * n + 2)
                g, j = n // 4, n % 4
                for t in range(T):
                    bank = ps_o[2 * t + n // 8]
                    if j == 0:
                        pe.matmul(bank[:, (n % 8) * 64:(n % 8 + 4) * 64], pcT[:, 4 * t + g, :],
                                  vcmp[:, g, :, :].rearrange("p j d -> p (j d)"), start=True, stop=False)
                    o = bank[:, (n % 8) * 64:(n % 8 + 1) * 64]
                    for br, v0 in enumerate((VS0, VW0)):
                        pt = pt2[:, (2 * n + br) % 4, :]
                        v = lambda k: proj2[:, k, v0 + 64 * g:v0 + 64 * (g + 1)]
                        last = br == 1 and j == 3
                        mm = pe.matmul(o, pt[:, t * P:(t + 1) * P], v(0), start=False, stop=(last and t == 0))
                        if t == 1:
                            mm = pe.matmul(o, pt[:, 2 * P:BL], v(1), start=False, stop=last)
                mm.then_inc(o_filled, 1)

    def nsa_vector(dve):
        for i in range(UN + 1):
            if i < UN:
                dve.wait_ge(n_filled, i + 1)
                for t, (lo, up) in enumerate(SPAN):
                    dve.tensor_reduce(nst[:, 0, 2 * i + t:2 * i + t + 1], ps_s[i % 2][:, lo:up], AX_X,
                                      ALU.max).then_inc(n_max, 1)
                dve.wait_ge(n_max, 3 * i + 2)
                dve.tensor_scalar(nst[:, 1, 2 * i:2 * i + 2], nst[:, 0, 2 * i:2 * i + 2], -nsa_scale, None,
                                  ALU.mult).then_inc(n_max, 1)
            if i >= 1:
                w = i - 1
                n, br = divmod(w, 2)
                dve.wait_ge(n_exp, 2 * w + 2)
                dve.reciprocal(nst[:, 3, 2 * w:2 * w + 2], nst[:, 2, 2 * w:2 * w + 2]).then_inc(n_inv, 1)
                dve.wait_ge(n_inv, 2 * w + 1)
                dve.tensor_tensor(nst[:, 4, 2 * w:2 * w + 2], nst[:, 3, 2 * w:2 * w + 2], gate2[:, :, n, 1 + br],
                                  ALU.mult).then_inc(n_inv, 1)
                dve.wait_ge(n_inv, 2 * w + 2)
                for t, (lo, up) in enumerate(SPAN):
                    last = dve.tensor_scalar(pb2[:, w % 2, lo:up], pb2[:, w % 2, lo:up],
                                             nst[:, 4, 2 * w + t:2 * w + t + 1], None, ALU.mult)
                last.then_inc(n_ready, 1)
        dve.wait_ge(o_filled, 16)
        for t in range(T):
            for f in range(2):
                dve.tensor_copy(yatt[:, t, 512 * f:512 * (f + 1)], ps_o[2 * t + f][:, :]).then_inc(o_ready, 1)

    def nsa_scalar(act):
        for i in range(UN + 1):
            if i < UN:
                act.wait_ge(n_max, 3 * i + 3)
                if i - 1 > 0:
                    act.wait_ge(npt_filled, i - 1)
                for t, (lo, up) in enumerate(SPAN):
                    act.activation(pb2[:, i % 2, lo:up], ps_s[i % 2][:, lo:up], ACT.Exp,
                                   bias=nst[:, 1, 2 * i + t:2 * i + t + 1], scale=nsa_scale,
                                   accum_out=nst[:, 2, 2 * i + t:2 * i + t + 1]).then_inc(n_exp, 1)
            if i >= 1:
                w = i - 1
                act.wait_ge(npt_filled, w + 1)
                if (w - 4) // 2 + 1 > 0:
                    act.wait_ge(o_filled, (w - 4) // 2 + 1)
                act.activation(pt2[:, w % 4, :], ps_pt[w % 2][:, 0:BL], ACT.Copy).then_inc(npt_ready, 1)

    turn_mix = Turn(lambda k, t: (ys if k < 8 else yatt)[:, t, (k % 8) * P:(k % 8 + 1) * P], KD, xt_hi, xt_lo,
                    lambda k: rowcols("gs", k) if k < 8 else ones[:, 0:1])

    def mix_tensor(pe):
        pe.wait_ge(o_ready, 4)
        turn_mix.tensor(pe)
        pe.wait_ge(turn_lo, turn_mix.at_split + turn_mix.units)

    g_out2 = Gemm(at, wview("w_out_2"), KD, 4, lhs_x)
    evac_out2 = evac_residual(g_out2, None)
    ffn2 = Ffn("ffn2", wview("w_gate_2"), wview("w_up_2"), 0, wview("w_down_2"), lambda k: rowcols("gf", k),
               None, None)
    ffn2.before = g_out2.c + 4

    rms_f = Rms([x[:, t, :] for t in range(T)], D, lambda i: xn[:, i, :], 0)
    fw = place("fw", GT2, [D])
    fw_loaded, final = sem("fw_loaded"), sem("final")

    def final_scalar(act):
        act.wait_ge(evac_done, ffn2.down.c + 4)
        act.dma_start(fw[:, :], A["final_norm_w_2"].rearrange("(o n) -> o n", o=1).broadcast_to([P, D])
                      ).then_inc(fw_loaded, 16)
        rms_f.scalar(act)

    def final_vector(dve):
        inv = rms_f.vector(dve)
        dve.wait_ge(fw_loaded, 16)
        for t in range(T):
            dve.scalar_tensor_tensor(x[:, t, :], x[:, t, :], inv(t), fw[:, :], ALU.mult, ALU.mult).then_inc(final, 1)

    def sp_end(sp):
        sp.wait_ge(final, 2)
        sp.dma_start(out.rearrange("o (t p) d -> p (o t) d", p=P), x[:, :, :]).then_inc(sem("out"), 16)
        sp.wait_ge(sem("out"), 16)

    def start_loads(sp):
        sp.dma_start(const[:, :], A["const"]).then_inc(start, 16)
        for name, src in (("g1", A["g_norm1"]), ("g2", A["g_norm2"]), ("gql", A["g_q_latent"]),
                          ("gkv", A["g_kv_latent"]), ("ga", A["attn_norm_w_2"]), ("gs", A["ssd_norm_w_2"]),
                          ("gf", A["ffn_norm_w_2"]), ("pek", A["cmp_pe_k_2"].rearrange("o a b -> o (a b)")),
                          ("pev", A["cmp_pe_v_2"].rearrange("o a b -> o (a b)")), ("c", A["c"])):
            r, n = ROWS[name]
            sp.dma_start(rows_in[r:r + n, 0, :], src.rearrange("o (r q) -> (o r) q", q=P)).then_inc(start, 16)
        sp.dma_start(rows_in[0:12, 1, :], A["conv_b_2"].rearrange("o (r q) -> (o r) q", q=P)).then_inc(start, 16)
        sp.dma_start(rows_in[12:60, 1, :], A["conv_w_2"].rearrange("o w (r q) -> (o w r) q", q=P)).then_inc(start, 16)
        sp.dma_start(rows_in[60:61, 1, :], A["g_q_head"][:, 0:P]).then_inc(start, 16)
        sp.dma_start(rows_in[61:62, 1, :], A["g_k_head"][:, 0:P]).then_inc(start, 16)
        sp.dma_start(x[:, :, :], A["x"].rearrange("o (t p) d -> p (o t) d", p=P)).then_inc(start, 16)
        sp.dma_start(posi[0:T, :], A["positions"].rearrange("o (t p) -> (o t) p", p=P)).then_inc(start, 16)
        for src, a, n in ((A["g_q_head"][:, P:HQ], 0, 64), (A["g_k_head"][:, P:HQ], 64, 64),
                          (A["dt_bias_2"], 128, 16), (A["a_log_2"], 144, 16), (A["d_skip_2"], 160, 16)):
            sp.dma_start(brd[:, a:a + n], src.broadcast_to([P, n])).then_inc(start, 16)
    NSTART = 1 + 10 + 4 + 2 + 5

    block = nc.Block()
    with block:
        @block.sync
        def _(sp):
            start_loads(sp)
            sync_gemm(sp, g_ada)
            sync_gemm(sp, g_in)
            sync_gemm(sp, g_in2)
            sync_gemm(sp, g_psb)
            sync_gemm(sp, g_uq)
            sync_gemm(sp, g_ukv)
            sync_gemm(sp, g_pmla)
            sync_gemm(sp, g_out)
            sync_gemm(sp, ffn1.g)
            sync_gemm(sp, ffn1.down)
            sync_gemm(sp, g_b)
            sync_gemm(sp, g_b2)
            sync_gemm(sp, g_out2)
            sync_gemm(sp, ffn2.g)
            sync_gemm(sp, ffn2.down)
            sp_end(sp)

        @block.scalar
        def _(act):
            start_scalar(act)
            scalar_gemm(act, g_ada, None)
            ada1.scalar(act)
            turn_x.scalar(act)
            scalar_gemm(act, g_in, evac_proj)
            scalar_gemm(act, g_in2, evac_proj_rest)
            sb_scalar(act)
            rms_lat.scalar(act)
            turn_lat[0].scalar(act)
            turn_lat[1].scalar(act)
            gates_scalar(act)
            scalar_gemm(act, g_psb, None)
            scalar_gemm(act, g_uq, evac_scalar_to(lambda t, c: proj[:, t, bass.ds(Q0 + c, CW)]))
            scalar_gemm(act, g_ukv, evac_scalar_to(lambda t, c: kv[:, t, bass.ds(c, CW)]))
            rope1_scalar(act)
            heads_scalar(act)
            mla_scalar(act)
            gt_scalar(act)
            scalar_gemm(act, g_pmla, None)
            turn_m.scalar(act)
            scalar_gemm(act, g_out, None)
            ffn1.scalar(act, ada2.scalar)
            norm_a_scalar(act)
            scalar_gemm(act, g_b, evac_scalar_to(lambda t, c: proj2[:, t, bass.ds(c, CW)]))
            scalar_gemm(act, g_b2, evac_rest2)
            ssd_scalar(act)
            cmp_scalar(act)
            nsa_scalar(act)
            turn_mix.scalar(act)
            scalar_gemm(act, g_out2, None)
            ffn2.scalar(act)
            final_scalar(act)

        @block.vector
        def _(dve):
            start_vector(dve)
            rope1_vector(dve)
            vector_gemm(dve, g_ada)
            ada1.vector(dve)
            turn_x.vector(dve)
            vector_gemm(dve, g_in)
            vector_gemm(dve, g_in2)
            sb_vector(dve)
            lat_vector(dve)
            dve.wait_ge(gates_ready, 2)
            vector_gemm(dve, g_psb, evac_gate_b)
            vector_gemm(dve, g_uq)
            vector_gemm(dve, g_ukv)
            heads_vector(dve)
            mla_vector(dve)
            gt_vector(dve)
            vector_gemm(dve, g_pmla, evac_merge)
            turn_m.vector(dve)
            vector_gemm(dve, g_out, evac_out)
            ffn1.vector(dve, ada2.vector)
            norm_a_vector(dve)
            vector_gemm(dve, g_b)
            vector_gemm(dve, g_b2)
            ssd_vector(dve)
            rope2_vector(dve)
            cmp_vector(dve)
            nsa_vector(dve)
            turn_mix.vector(dve)
            vector_gemm(dve, g_out2, evac_out2)
            ffn2.vector(dve)
            final_vector(dve)

        @block.tensor
        def _(pe):
            start_tensor(pe)
            tensor_gemm(pe, g_ada)
            ada1.tensor(pe)
            turn_x_tensor(pe)
            tensor_gemm(pe, g_in)
            tensor_gemm(pe, g_in2)
            pe.wait_ge(evac_done, g_in2.c + 1)
            sb_tensor(pe)
            lat_tensor(pe)
            pe.wait_ge(yb_lo, 4)
            tensor_gemm(pe, g_psb)
            tensor_gemm(pe, g_uq)
            tensor_gemm(pe, g_ukv)
            mla_tensor(pe)
            gt_tensor(pe)
            pe.wait_ge(ya_lo, 4)
            tensor_gemm(pe, g_pmla)
            turn_after(turn_m, g_pmla)(pe)
            tensor_gemm(pe, g_out)
            ffn1.tensor(pe, ada2.tensor)
            norm_a_tensor(pe)
            tensor_gemm(pe, g_b)
            tensor_gemm(pe, g_b2)
            ssd_tensor(pe)
            cmp_tensor(pe)
            nsa_tensor(pe)
            mix_tensor(pe)
            tensor_gemm(pe, g_out2)
            ffn2.tensor(pe)
    return names


def kernel(**inputs):
    import numpy as _np
    import concourse.bacc as _bacc
    from concourse import mybir as _mybir
    from concourse.bass_utils import run_bass_kernel_spmd as _run

    nc = _bacc.Bacc("TRN2", target_bir_lowering=False, num_devices=1)
    arrays, aps = {}, {}
    given = {name: _np.ascontiguousarray(value) for name, value in inputs.items()}
    given["const"] = constants()
    for name, a in given.items():
        arrays[f"in_{name}"] = a
        aps[name] = nc.dram_tensor(f"in_{name}", a.shape, _mybir.dt.from_np(a.dtype), kind="ExternalInput").ap()
    out = nc.dram_tensor("out", (1, SEQ, D), F32, kind="ExternalOutput").ap()
    program(nc, aps, out)
    r = _run(nc, [arrays], core_ids=[0])
    return r.results[0]["out"]
```

```python
import numpy as np

import concourse.bass as bass
from concourse import mybir

F32 = mybir.dt.float32
F32R = mybir.dt.float32r
I32 = mybir.dt.int32
ALU = mybir.AluOpType
ACT = mybir.ActivationFunctionType
AX_X = mybir.AxisListType.X

P = 128
SEQ = 256
T = SEQ // P
D = 2048
KD = D // P
CW = 512
RAW, HI, LO = 4, 4, 2
ADA = 4
PEELED = 1
NEG = -1e30
EPS = 1e-6


class Gemm:

    def __init__(self, at, weights, k, n, lhs, col0=0, ada=(0, 0), width=CW, cols=None,
                 peeled=PEELED):
        self.turn = None
        self.weights, self.n, self.lhs, self.width = weights, n, lhs, width
        self.peeled = peeled
        self.S = k // 2
        self.ada, self.ada_width = ada
        self.ada_k = KD // self.ada if self.ada else 0
        self.col = cols or (lambda u: (col0 + CW * u, 2 * CW))
        self.v, self.w, self.c, self.a = at["v"], at["w"], at["c"], at["a"]
        at["v"] += n * self.ada
        at["w"] += n * self.S
        at["c"] += n if k else 0
        self.ada_steps = self.ada * (self.ada_k - 1)
        self.steps, self.ada_col = at["steps"], at["ada_col"]
        at["steps"] += n * self.ada_steps
        at["ada_col"] += n * self.ada_width
        self.r = at["r"]
        at["a"] += n if self.ada else 0
        at["r"] += n if self.ada and k else 0
        assert self.ada % 2 == 0 and self.S % 2 == 0

    def ada_columns(self, u, j):
        return Count(self.ada_col + u * self.ada_width, 2 * self.ada_width, j).value

    def order(self):
        if not self.S:
            return [("ada", s) for s in range(self.ada)]
        both = [(("w", s), ("ada", s)) for s in range(self.S)]
        return [x for pair in both for x in pair if x[0] == "w" or self.ada]

    def slots(self, u, j):
        for kind, s in self.order():
            first, per = (self.w, self.S) if kind == "w" else (self.v, self.ada)
            yield kind, s, Count(first + u * per + s, 2 * per, j)


class Count:

    def __init__(self, first, per=0, j=None):
        self.first, self.per, self.j = first, per, j

    def __add__(self, n):
        return Count(self.first + n, self.per, self.j)

    def __sub__(self, n):
        return self + -n

    def __mod__(self, n):
        assert self.j is None or self.per % n == 0
        return self.first % n

    def times(self, n, of=1):
        assert self.j is None or self.per % of == 0
        return Count(self.first // of * n, self.per // of * n, self.j)

    @property
    def above_zero(self):
        assert self.j is None or self.first + self.per * PEELED > 0
        return self.j is not None or self.first > 0

    @property
    def value(self):
        return self.first if self.j is None else self.first + self.per * self.j


def in_pairs(eng, g, chunk, tail):
    for u in range(min(g.n, 2 * g.peeled)):
        chunk(u, None, u > 0)
    if g.n // 2 > g.peeled:
        with eng.Fori(g.peeled, g.n // 2) as j:
            chunk(0, j, True)
            chunk(1, j, True)
    if g.n % 2 and g.n > 2 * g.peeled:
        chunk(g.n - 1, None, True)
    tail(g.n)


def steps(*names):
    return {name: n + 1 for n, name in enumerate(names)}


C_IDENT, C_ONES, C_MASKQ, C_MASKT, C_MASKS, C_CUM, C_AFTER = (i * P for i in range(7))
C_FREQ = 7 * P
C_COS2, C_SIN2 = C_FREQ + 32, C_FREQ + 48
C_CMPADD, C_CMPMUL = C_FREQ + 64, C_FREQ + 94
NCONST = 1024


def constants():
    k = np.zeros((P, NCONST), np.float32)
    row, col = np.arange(P)[:, None], np.arange(P)[None, :]
    k[:, C_IDENT:C_IDENT + P] = row == col
    k[:, C_ONES:C_ONES + P] = 1.0
    k[:, C_MASKQ:C_MASKQ + P] = np.where(col <= row, 0.0, NEG)
    k[:, C_MASKT:C_MASKT + P] = np.where(row <= col, 0.0, NEG)
    k[:, C_MASKS:C_MASKS + P] = np.where(row < col, 0.0, NEG)
    k[:, C_CUM:C_CUM + P] = row <= col
    k[:, C_AFTER:C_AFTER + P] = row > col
    f32 = np.float32
    k[:, C_FREQ:C_FREQ + 32] = f32(10000.0) ** (-np.arange(32, dtype=f32) / f32(32))
    inv = f32(1.0) / (f32(500000.0) ** (np.arange(0, 16, 2, dtype=f32) / f32(16)))
    ang = (np.arange(SEQ, dtype=f32)[:, None] * inv[None, :]).reshape(T, P, 8)
    k[:, C_COS2:C_COS2 + 16] = np.cos(ang).transpose(1, 0, 2).reshape(P, 16)
    k[:, C_SIN2:C_SIN2 + 16] = np.sin(ang).transpose(1, 0, 2).reshape(P, 16)
    seen = (16 * np.arange(15) + 31)[None, None, :] <= np.arange(SEQ).reshape(T, P).T[:, :, None]
    k[:, C_CMPADD:C_CMPADD + 30] = np.where(seen, 0.0, NEG).reshape(P, 30)
    k[:, C_CMPMUL:C_CMPMUL + 30] = seen.reshape(P, 30)
    return k


ROWS = {}
for _name, _n in (("g1", 16), ("g2", 16), ("gql", 4), ("gkv", 4), ("ga", 16), ("gs", 8), ("gf", 16),
                  ("pek", 16), ("pev", 16), ("c", 16)):
    ROWS[_name] = (sum(n for _, n in ROWS.values()), _n)


def program(nc, A, out):
    base = (nc.sbuf_base + 63) // 64 * 64
    slab = nc.alloc_sbuf_tensor("slab", [P, (nc.sbuf_bytes_remaining - 64) // 4], F32)
    names = {}

    def place(name, at, shape, dt=F32):
        t = nc.alloc_sbuf_tensor_at(name, [P] + shape, dt, offset=base + at)
        names[name] = t.name
        return t

    x = place("x", 0, [T, D])
    raw = place("raw", 16384, [RAW, 2, CW])
    w_hi = place("w_hi", 32768, [HI, 2, CW], F32R)
    w_lo = place("w_lo", 49152, [LO, 2, CW], F32R)
    XT = 57344
    xt_hi = place("xt_hi", XT, [KD, SEQ], F32R)
    xt_lo = place("xt_lo", XT + 16384, [KD, SEQ], F32R)
    const = place("const", 90112, [NCONST])
    SM = 94208
    cols = place("cols", SM, [P])
    colb = place("colb", SM + 512, [64])
    adacol = place("adacol", SM + 768, [4, KD])
    ccol = place("ccol", SM + 1024, [KD])
    scol = place("scol", SM + 1088, [4, KD])
    stat = place("stat", SM + 1344, [64])
    GT2, GT1, PROJ = 98304, 106496, 114688
    ada_raw = place("ada_raw", GT2, [ADA, 2 * CW])
    gt2 = place("gt2", GT2, [D])
    gt1 = place("gt1", GT1, [D])
    NIN = 8256
    proj = place("proj", PROJ, [T, NIN])
    xn = place("xn", PROJ, [T, D])
    rows_in = place("rows_in", PROJ + 16384, [2, P])
    ACC = 180736
    acc = place("acc", ACC, [2, CW])
    yt_hi = place("yt_hi", 184832, [8, SEQ], F32R)
    yt_lo = place("yt_lo", 193024, [8, SEQ], F32R)
    SCR = 201216
    arow = place("arow", SCR, [2, CW])
    tmp = place("tmp", SCR + 4096, [2, 2, SEQ])
    ident = const[:, C_IDENT:C_IDENT + P]
    ones = const[:, C_ONES:C_ONES + P]

    ps = [nc.alloc_psum_tensor(f"ps{i}", [P, CW], F32) for i in range(8)]
    ps_gemm = ps[0:4]
    ps_ada = ps[4]
    ps_turn = ps[5:8]

    scratch = nc.dram_tensor("ada_scratch", [6 * D], F32, kind="Internal").ap()

    sems = {}

    def sem(name):
        if name not in sems:
            sems[name] = nc.alloc_semaphore(name)
        return sems[name]

    loaded = [sem(f"loaded{i}") for i in range(RAW)]
    ada_loaded = [sem(f"ada_loaded{i}") for i in range(ADA)]
    ada_used = sem("ada_used")
    raw_used, hi_ready, w_used = sem("raw_used"), sem("hi_ready"), sem("w_used")
    evac_done = sem("evac_done")
    ada_step, ada_summed, ada_evac = sem("ada_step"), sem("ada_summed"), sem("ada_evac")
    ada_stored = [sem("ada_stored0"), sem("ada_stored1")]
    turn_filled, turn_scaled = sem("turn_filled"), sem("turn_scaled")
    turn_hi, turn_lo = sem("turn_hi"), sem("turn_lo")
    start = sem("start_loaded")

    def wview(name):
        return A[name].rearrange("o (c p) n -> p (o c) n", p=P)

    at = dict(v=0, w=0, c=0, a=0, r=0, steps=0, ada_col=0)
    g_ada = Gemm(at, None, 0, 2 * D // CW, None, ada=(KD // 2, CW))
    lhs_x = lambda part, k, t: (xt_lo if part else xt_hi)[:, k, t * P:(t + 1) * P]
    lhs_y = lambda part, k, t: (yt_lo if part else yt_hi)[:, k, t * P:(t + 1) * P]
    g_in = Gemm(at, wview("w_in"), KD, 16, lhs_x, ada=(KD // 2, 3 * D // 16))

    narrow_n = dict(n=0)
    narrow_loaded, narrow_hi, narrow_lo, narrow_done, narrow_copied = (
        sem(f"narrow_{n}") for n in ("loaded", "hi", "lo", "done", "copied"))

    class Narrow:

        def __init__(self, name, at, weights, col0, places):
            self.weights, self.col0 = weights, col0
            self.raw, self.hi, self.lo = (place(f"{name}_{part}", where, [KD, 64], dt)
                                          for part, where, dt in zip(("raw", "hi", "lo"), places, (F32, F32R, F32R)))
            self.turned = place(f"{name}_turned", places[0], [SEQ])
            self.c = at["c"]
            self.banks = ps_gemm[2 * (self.c % 2):2 * (self.c % 2) + 2]
            at["c"] += 1
            self.n = narrow_n["n"]
            narrow_n["n"] += 1

        def load(self, q):
            q.dma_start(self.raw[:, :, :], self.weights[:, :, self.col0:self.col0 + 64]).then_inc(narrow_loaded, 16)

        def high(self, act):
            act.wait_ge(narrow_loaded, 16 * (self.n + 1))
            act.activation(self.hi[:, :, :], self.raw[:, :, :], ACT.Copy).then_inc(narrow_hi, 1)

        def scalar(self, act, dst):
            act.wait_ge(narrow_done, 2 * self.n + 1)
            act.activation(self.turned[0:64, :], self.banks[0][0:64, 0:SEQ], ACT.Copy).then_inc(narrow_copied, 1)
            act.wait_ge(narrow_done, 2 * self.n + 2)
            for t in range(T):
                last = act.activation(dst(t), self.banks[1][:, 64 * t:64 * (t + 1)], ACT.Copy)
            last.then_inc(evac_done, 1)

        def vector(self, dve):
            dve.wait_ge(narrow_hi, self.n + 1)
            dve.tensor_tensor(self.lo[:, :, :], self.raw[:, :, :], self.hi[:, :, :].bitcast(F32),
                              ALU.subtract).then_inc(narrow_lo, 1)

        def tensor(self, pe):
            pe.wait_ge(narrow_lo, self.n + 1)
            pe.wait_ge(evac_done, self.c - 1)
            for k in range(KD):
                for i, (part, weights) in enumerate(((0, self.hi), (0, self.lo), (1, self.hi))):
                    mm = pe.matmul(self.banks[0][0:64, 0:SEQ], weights[:, k, :], (xt_lo if part else xt_hi)[:, k, :],
                                   start=(k == 0 and i == 0), stop=(k == KD - 1 and i == 2))
            mm.then_inc(narrow_done, 1)
            pe.wait_ge(narrow_copied, self.n + 1)
            for t in range(T):
                mm = pe.transpose(self.banks[1][:, 64 * t:64 * (t + 1)], self.turned[0:64, t * P:(t + 1) * P],
                                  ident[0:64, 0:64])
            mm.then_inc(narrow_done, 1)

    g_in2 = Narrow("w_in_rest", at, wview("w_in"), 8192, (184832, 184832 + 4096, 184832 + 8192))

    def ada_slot(g, v):
        return ada_raw[:, v % ADA, 0:g.ada_k * g.ada_width].rearrange("p (k n) -> p k n", k=g.ada_k)

    def sync_gemm(sp, g, place_free=None):
        w_ada = wview("w_ada")

        def chunk(u, j, before):
            for kind, s, w in g.slots(u, j):
                if kind == "ada":
                    if u == 0 and j is None and s == 0 and place_free:
                        sp.wait_ge(place_free[0], place_free[1])
                    if (w + (1 - ADA)).above_zero:
                        sp.wait_ge(ada_used, (w + (1 - ADA)).value)
                    src = w_ada[:, g.ada_k * s:g.ada_k * (s + 1), bass.ds(g.ada_columns(u, j), g.ada_width)]
                    sp.dma_start(ada_slot(g, w), src).then_inc(ada_loaded[w % ADA], 16)
                else:
                    if (w + (1 - RAW)).above_zero:
                        sp.wait_ge(raw_used, (w + (1 - RAW)).value)
                    first, step = g.col(u)
                    src = halves(g, u)[:, 2 * s:2 * s + 2, bass.ds(Count(first, step, j).value, g.width)]
                    sp.dma_start(raw[:, w % RAW, :, 0:g.width], src).then_inc(loaded[w % RAW], 16)
        in_pairs(sp, g, chunk, lambda n: None)

    def scalar_gemm(act, g, evac):
        def hook(u, j):
            if g.S and evac:
                c = Count(g.c + u, 2, j)
                act.wait_ge(w_used, Count(g.w + (u + 1) * g.S, 2 * g.S, j).value)
                evac(c, u, j)
            if g.ada and g.S:
                a, row = Count(g.a + u, 2, j), Count(g.r + u, 2, j)
                par = row % 2
                act.wait_ge(ada_summed, (a + 1).value)
                act.wait_ge(ada_stored[par], ((row if par == 0 else row - 1).times(16, 2) + 16).value)
                act.activation(arow[0:1, par, 0:g.ada_width], ps_ada[0:1, 0:g.ada_width],
                               ACT.Copy).then_inc(ada_evac, 1)
                act.wait_ge(ada_evac, (row + 1).value)
                act.dma_start(scratch[bass.ds(g.ada_columns(u, j), g.ada_width)].rearrange("(o n) -> o n", o=1),
                              arow[0:1, par, 0:g.ada_width]).then_inc(ada_stored[par], 16)

        def chunk(u, j, before):
            for n, (kind, s, w) in enumerate(g.slots(u, j)):
                if n == 3 * (g.S + g.ada) // 4 and before and g.S != 2:
                    hook(u - 1, j)
                if kind == "w":
                    if g.turn and not before:
                        g.turn.high(act, s)
                    act.wait_ge(loaded[w % RAW], (w.times(16, RAW) + 16).value)
                    if (w + (1 - HI)).above_zero:
                        act.wait_ge(w_used, (w + (1 - HI)).value)
                    act.activation(w_hi[:, w % HI, :, 0:g.width], raw[:, w % RAW, :, 0:g.width],
                                   ACT.Copy).then_inc(hi_ready, 1)
            if g.S == 2 and before:
                hook(u - 1, j)
        in_pairs(act, g, chunk, lambda n: hook(n - 1, None))

    def vector_gemm(dve, g, evac=None):
        def hook(u, j):
            if evac:
                dve.wait_ge(w_used, Count(g.w + (u + 1) * g.S, 2 * g.S, j).value)
                evac(Count(g.c + u, 2, j), u, j)

        def chunk(u, j, before):
            for n, (kind, s, w) in enumerate(g.slots(u, j)):
                if n == 3 * (g.S + g.ada) // 4 and before and g.S != 2:
                    hook(u - 1, j)
                if kind == "w":
                    if g.turn and not before:
                        if s == 0:
                            g.turn.scaled(dve, 0)
                        if s + 1 < g.S:
                            g.turn.scaled(dve, s + 1)
                        g.turn.low(dve, s)
                    dve.wait_ge(hi_ready, (w + 1).value)
                    if (w + (1 - LO)).above_zero:
                        dve.wait_ge(w_used, (w + (1 - LO)).value)
                    dve.tensor_tensor(w_lo[:, w % LO, :, 0:g.width], raw[:, w % RAW, :, 0:g.width],
                                      w_hi[:, w % HI, :, 0:g.width].bitcast(F32),
                                      ALU.subtract).then_inc(raw_used, 1)
                else:
                    a = Count(g.a + u, 2, j)
                    part = acc[:, a % 2, 0:g.ada_width]
                    rows = ada_slot(g, w)
                    done = Count(g.steps + u * g.ada_steps + s * (g.ada_k - 1), 2 * g.ada_steps, j)
                    dve.wait_ge(ada_loaded[w % ADA], (w.times(16, ADA) + 16).value)
                    for k in range(g.ada_k):
                        weight = ccol[:, g.ada_k * s + k:g.ada_k * s + k + 1]
                        if s == 0 and k == 0:
                            if (a - 1).above_zero:
                                dve.wait_ge(ada_summed, (a - 1).value)
                            dve.tensor_scalar(part, rows[:, 0, :], weight, None, ALU.mult).then_inc(ada_step, 1)
                            continue
                        if k == 0:
                            dve.wait_ge(ada_used, w.value)
                        else:
                            dve.wait_ge(ada_step, (done + k).value)
                        ins = dve.scalar_tensor_tensor(part, rows[:, k, :], weight, part, ALU.mult, ALU.add)
                        if k < g.ada_k - 1:
                            ins.then_inc(ada_step, 1)
                        else:
                            ins.then_inc(ada_used, 1)
            if g.S == 2 and before:
                hook(u - 1, j)
        in_pairs(dve, g, chunk, lambda n: hook(n - 1, None))

    def tensor_gemm(pe, g, middle=None):
        def hook(u, j):
            if g.ada:
                a, row = Count(g.a + u, 2, j), Count(g.r + u, 2, j)
                pe.wait_ge(ada_used, Count(g.v + (u + 1) * g.ada, 2 * g.ada, j).value)
                part = acc[:, a % 2, :]
                if g.S:
                    if row.above_zero:
                        pe.wait_ge(ada_evac, row.value)
                    pe.matmul(ps_ada[0:1, 0:g.ada_width], ones[:, 0:1], part[:, 0:g.ada_width], start=True,
                              stop=True).then_inc(ada_summed, 1)
                else:
                    for i in range(CW // P):
                        column = ps_ada[:, bass.ds(Count(4 * u + i, 8, j).value, 1)]
                        mm = pe.matmul(column, part[:, i * P:(i + 1) * P], ones[:, 0:1], start=True, stop=True)
                    mm.then_inc(ada_summed, 1)
            if middle:
                middle(u, j)

        def chunk(u, j, before):
            c = Count(g.c + u, 2, j)
            bank = ps_gemm[2 * (c % 2):2 * (c % 2) + 2]
            if g.S:
                if (c - 1).above_zero:
                    pe.wait_ge(evac_done, (c - 1).value)
            for n, (kind, s, w) in enumerate(g.slots(u, j)):
                if n == (g.S + g.ada) // 4 and before:
                    hook(u - 1, j)
                if kind != "w":
                    continue
                if g.turn and not before:
                    for v in ([0, 1, 2] if s == 0 else [s + 2] if s + 2 < g.S else []):
                        g.turn.fill(pe, v)
                    pe.wait_ge(turn_lo, g.turn.at_split + s + 1)
                pe.wait_ge(raw_used, (w + 1).value)
                for k in range(2):
                    for t in range(T):
                        for n3, (part, weights) in enumerate(((0, w_hi[:, w % HI]), (0, w_lo[:, w % LO]),
                                                              (1, w_hi[:, w % HI]))):
                            mm = pe.matmul(bank[t][:, 0:g.width], g.lhs(part, 2 * s + k, t),
                                           weights[:, k, 0:g.width],
                                           start=(s == 0 and k == 0 and n3 == 0),
                                           stop=(s == g.S - 1 and k == 1 and n3 == 2))
                mm.then_inc(w_used, 1)
        in_pairs(pe, g, chunk, lambda n: hook(n - 1, None))

    turns = dict(n=0, split=0)

    class Turn:

        def __init__(self, src, k, hi, lo, scale=None, bias=None):
            self.src, self.units, self.hi, self.lo, self.scale, self.bias = src, k // 2, hi, lo, scale, bias
            self.at, self.at_split = turns["n"], turns["split"]
            turns["n"] += self.units
            turns["split"] += self.units

        def fill(self, pe, v):
            n = self.at + v
            if n - 2 > 0:
                pe.wait_ge(turn_scaled, n - 2)
            for k in range(2):
                for t in range(T):
                    mm = pe.transpose(ps_turn[n % 3][:, k * SEQ + t * P:k * SEQ + (t + 1) * P],
                                      self.src(2 * v + k, t), ident)
            mm.then_inc(turn_filled, 1)

        def scaled(self, dve, v):
            n, m = self.at + v, self.at_split + v
            dve.wait_ge(turn_filled, n + 1)
            if m - 1 > 0:
                dve.wait_ge(turn_lo, m - 1)
            for k in range(2):
                kk = 2 * v + k
                src = ps_turn[n % 3][:, k * SEQ:(k + 1) * SEQ]
                if self.scale is None:
                    last = dve.tensor_copy(tmp[:, m % 2, k, :], src)
                elif self.bias is None:
                    last = dve.tensor_scalar(tmp[:, m % 2, k, :], src, self.scale(kk), None, ALU.mult)
                else:
                    last = dve.tensor_scalar(tmp[:, m % 2, k, :], src, self.scale(kk), self.bias(kk),
                                             ALU.mult, ALU.add)
            last.then_inc(turn_scaled, 1)

        def low(self, dve, v):
            n = self.at_split + v
            dve.wait_ge(turn_hi, n + 1)
            dve.tensor_tensor(self.lo[:, 2 * v:2 * v + 2, :], tmp[:, n % 2, :, :],
                              self.hi[:, 2 * v:2 * v + 2, :].bitcast(F32),
                              ALU.subtract).then_inc(turn_lo, 1)

        def high(self, act, v):
            n, m = self.at + v, self.at_split + v
            act.wait_ge(turn_scaled, n + 1)
            act.activation(self.hi[:, 2 * v:2 * v + 2, :], tmp[:, m % 2, :, :],
                           ACT.Copy).then_inc(turn_hi, 1)

        def tensor(self, pe):
            for v in range(self.units):
                self.fill(pe, v)

        def vector(self, dve):
            for v in range(self.units):
                self.scaled(dve, v)
                if v:
                    self.low(dve, v - 1)
            self.low(dve, self.units - 1)

        def scalar(self, act):
            for v in range(self.units):
                self.high(act, v)

    class Plain:

        def __init__(self, units):
            self.units, self.at = units, turns["n"]
            turns["n"] += len(units)

        def tensor(self, pe):
            for v, (ins, _) in enumerate(self.units):
                n = self.at + v
                pe.wait_ge(turn_scaled, n - 2)
                for src, rows_out, col in ins:
                    mm = pe.transpose(ps_turn[n % 3][0:rows_out, col:col + src.shape[0]], src,
                                      ident[0:src.shape[0], 0:src.shape[0]])
                mm.then_inc(turn_filled, 1)

        def vector(self, dve):
            for v, (_, copy) in enumerate(self.units):
                n = self.at + v
                dve.wait_ge(turn_filled, n + 1)
                copy(ps_turn[n % 3]).then_inc(turn_scaled, 1)

        @property
        def end(self):
            return self.at + len(self.units)

    turn_x = Turn(lambda k, t: xn[:, t, k * P:(k + 1) * P], KD, xt_hi, xt_lo,
                  scale=lambda k: scol[:, 0, k:k + 1], bias=lambda k: adacol[:, 0, k:k + 1])

    start_turned, start_cols, c_ready = sem("start_turned"), sem("start_cols"), sem("c_ready")
    ssq, root, inverse, xn_ready = sem("ssq"), sem("root"), sem("inverse"), sem("xn_ready")
    rms_n = dict(n=0)
    brd = place("brd", SM + 1600, [176])
    rope1 = place("rope1", SM + 2304, [2, T, 32])
    hstat = place("hstat", SM + 2816, [6, T * 8])
    posf = place("posf", SM + 3200, [2, T])
    posi = place("posi", SCR + 9216, [P], I32)
    posr = place("posr", SCR + 9728, [P])
    pesum = place("pesum", SM + 3296, [T])
    mst = place("mst", SM + 3328, [4, T * 8])
    adar = place("adar", SCR + 8192, [2, P])
    etmp = place("etmp", SCR + 9216, [CW])

    def rowcols(name, k=0):
        return cols[:, ROWS[name][0] + k:ROWS[name][0] + k + 1]

    class Rms:

        def __init__(self, srcs, width, junk, col):
            self.srcs, self.width, self.junk, self.col = srcs, width, junk, col
            self.n = rms_n["n"]
            rms_n["n"] += 1

        def scalar(self, act):
            m = len(self.srcs)
            for i, s in enumerate(self.srcs):
                last = act.activation(self.junk(i), s, ACT.Square,
                                      accum_out=stat[:, self.col + i:self.col + i + 1])
            last.then_inc(ssq, 1)
            act.wait_ge(ssq, self.n + 1)
            act.activation(stat[:, self.col + m:self.col + 2 * m], stat[:, self.col:self.col + m],
                           ACT.Sqrt, bias=epsc[:, 0:1], scale=1.0 / self.width).then_inc(root, 1)

        def vector(self, dve):
            m = len(self.srcs)
            dve.wait_ge(root, self.n + 1)
            dve.reciprocal(stat[:, self.col + 2 * m:self.col + 3 * m],
                           stat[:, self.col + m:self.col + 2 * m]).then_inc(inverse, 1)
            dve.wait_ge(inverse, self.n + 1)
            return lambda i: stat[:, self.col + 2 * m + i:self.col + 2 * m + i + 1]

    epsc = place("epsc", SM + 3264, [4])
    eps_set = sem("eps_set")
    rms_x = Rms([x[:, t, :] for t in range(T)], D, lambda i: xn[:, i, :], 0)
    adar_loaded, adar_turned, adacol_ready = sem("adar_loaded"), sem("adar_turned"), sem("adacol_ready")

    BL = 3 * P
    H = 8
    Q0, K0, V0, GA0, GB0 = 1088, 2112, 3136, 4160, 6208
    qsb = place("qsb", XT, [H, SEQ])
    ksb = place("ksb", XT + 8192, [H, SEQ])
    zs = place("zs", XT + 16384, [H, BL])
    ez = place("ez", 184832, [H, BL])
    mz = place("mz", GT2, [H, BL])
    sb_scale = 128 ** -0.5

    def sb_unit(dst, c0, u, scale):
        ins = [(proj[:, t, c0 + (2 * u + k) * P:c0 + (2 * u + k + 1) * P], P, k * SEQ + t * P)
               for k in range(2) for t in range(T)]

        def copy(bank):
            o = dst[:, 2 * u:2 * u + 2, :].rearrange("p a b -> p (a b)")
            return nc.vector.tensor_scalar(o, bank[:, :], scale, None, ALU.mult)
        return ins, copy
    turn_sb = Plain([sb_unit(d, c, u, s) for u in range(H // 2)
                     for d, c, s in ((qsb, Q0, sb_scale), (ksb, K0, 1.0))])
    z_filled, z_copied, z_abs, z_soft = sem("z_filled"), sem("z_copied"), sem("z_abs"), sem("z_soft")
    m_ready, lb_ready = sem("m_ready"), sem("lb_ready")
    tail_filled, arg_ready, a_ready = sem("tail_filled"), sem("arg_ready"), sem("a_ready")
    yb_filled, yb_hi, yb_lo = sem("yb_filled"), sem("yb_hi"), sem("yb_lo")
    gates_ready = sem("gates_ready")

    def keys_by_queries(pe, bank, lhs, rhs, start=True, stop=True):
        pe.matmul(bank[:, 0:SEQ], lhs(0), rhs(0, SEQ), start=start, stop=stop)
        return pe.matmul(bank[:, SEQ:BL], lhs(1), rhs(P, SEQ), start=start, stop=stop)

    def sb_tensor(pe):
        turn_sb.tensor(pe)
        masks = const[:, C_MASKS:C_MASKS + P]
        for h in range(H):
            pe.wait_ge(turn_scaled, turn_sb.at + 2 * (h // 2) + 2)
            if h - 3 > 0:
                pe.wait_ge(z_copied, h - 3)
            b = ps_gemm[h % 4]
            pe.matmul(b[:, 0:SEQ], ksb[:, h, 0:P], qsb[:, h, :], start=True, stop=False)
            pe.matmul(b[:, 0:P], ident, masks, start=False, stop=True)
            pe.matmul(b[:, SEQ:BL], ksb[:, h, P:SEQ], qsb[:, h, P:SEQ], start=True, stop=False)
            pe.matmul(b[:, SEQ:BL], ident, masks, start=False, stop=True).then_inc(z_filled, 1)
        after = const[:, C_AFTER:C_AFTER + P]
        for h in range(H):
            pe.wait_ge(m_ready, h // 4 + 1)
            pe.wait_ge(z_copied, H)
            if h - 3 > 0:
                pe.wait_ge(arg_ready, h - 3)
            b = ps_gemm[h % 4]
            pe.matmul(b[:, 0:SEQ], after, mz[:, h, 0:SEQ], start=True, stop=False)
            pe.matmul(b[:, P:SEQ], ones, mz[:, h, SEQ:BL], start=False, stop=True)
            pe.matmul(b[:, SEQ:BL], after, mz[:, h, SEQ:BL], start=True, stop=True).then_inc(tail_filled, 1)
        for h in range(H):
            pe.wait_ge(a_ready, h + 1)
            if h % 2 == 0:
                if h // 2 - 2 > 0:
                    pe.wait_ge(yb_lo, h // 2 - 2)
            b = ps_turn[(h // 2) % 3][:, (h % 2) * SEQ:(h % 2 + 1) * SEQ]
            v = lambda t: proj[:, t, V0 + h * P:V0 + (h + 1) * P]
            pe.matmul(b, v(0), zs[:, h, 0:SEQ], start=True, stop=False)
            mm = pe.matmul(b[:, P:SEQ], v(1), zs[:, h, SEQ:BL], start=False, stop=True)
            if h % 2:
                mm.then_inc(yb_filled, 1)

    def sb_vector(dve):
        turn_sb.vector(dve)
        for h in range(H):
            dve.wait_ge(z_filled, h + 1)
            dve.tensor_copy(zs[:, h, :], ps_gemm[h % 4][:, 0:BL]).then_inc(z_copied, 1)
        for f in range(2):
            zf, ef = (b[:, 4 * f:4 * f + 4, :].rearrange("p a b -> p (a b)") for b in (zs, ez))
            dve.wait_ge(z_copied, 4 * f + 4)
            dve.scalar_tensor_tensor(ef, zf, -1.0, zf, ALU.mult, ALU.max).then_inc(z_abs, 1)
        for f in range(2):
            zf, ef, mf = (b[:, 4 * f:4 * f + 4, :].rearrange("p a b -> p (a b)") for b in (zs, ez, mz))
            dve.wait_ge(z_soft, f + 1)
            dve.scalar_tensor_tensor(mf, zf, 0.0, ef, ALU.max, ALU.add).then_inc(m_ready, 1)
            dve.wait_ge(m_ready, f + 1)
            dve.scalar_tensor_tensor(zf, zf, 0.0, ef, ALU.min, ALU.subtract).then_inc(lb_ready, 1)
        for h in range(H):
            dve.wait_ge(lb_ready, h // 4 + 1)
            dve.wait_ge(tail_filled, h + 1)
            dve.tensor_tensor(zs[:, h, :], zs[:, h, :], ps_gemm[h % 4][:, 0:BL],
                              ALU.subtract).then_inc(arg_ready, 1)
        for u in range(H // 2):
            dve.wait_ge(yb_hi, u + 1)
            dve.tensor_tensor(yt_lo[:, 2 * u:2 * u + 2, :].rearrange("p a b -> p (a b)"), ps_turn[u % 3][:, :],
                              yt_hi[:, 2 * u:2 * u + 2, :].rearrange("p a b -> p (a b)").bitcast(F32),
                              ALU.subtract).then_inc(yb_lo, 1)

    def sb_scalar(act):
        for f in range(2):
            ef = ez[:, 4 * f:4 * f + 4, :].rearrange("p a b -> p (a b)")
            act.wait_ge(z_abs, f + 1)
            act.activation(ef, ef, ACT.Exp, scale=-1.0).then_inc(z_abs2, 1)
        for f in range(2):
            ef = ez[:, 4 * f:4 * f + 4, :].rearrange("p a b -> p (a b)")
            act.wait_ge(z_abs2, f + 1)
            act.activation(ef, ef, ACT.Ln, bias=ones[:, 0:1]).then_inc(z_soft, 1)
        for h in range(H):
            act.wait_ge(arg_ready, h + 1)
            act.activation(zs[:, h, :], zs[:, h, :], ACT.Exp).then_inc(a_ready, 1)
        for u in range(H // 2):
            act.wait_ge(yb_filled, u + 1)
            act.activation(yt_hi[:, 2 * u:2 * u + 2, :].rearrange("p a b -> p (a b)"), ps_turn[u % 3][:, :],
                           ACT.Copy).then_inc(yb_hi, 1)

    def gates_scalar(act):
        act.wait_ge(evac_done, g_in2.c + 1)
        for t in range(T):
            act.activation(proj[:, t, GA0:NIN], proj[:, t, GA0:NIN], ACT.Sigmoid).then_inc(gates_ready, 1)
    z_abs2 = sem("z_exp")

    g_psb = Gemm(at, wview("w_proj_sb"), 8, 4, lhs_y, ada=(4, D // 8))

    lat_sq = place("lat_sq", GT2, [4, CW])
    rms_lat = Rms([proj[:, t, L * CW:(L + 1) * CW] for L in range(2) for t in range(T)], CW,
                  lambda i: lat_sq[:, i, :], 8)
    lat = [(place(f"lat{L}_hi", XT + 8192 * L, [4, SEQ], F32R), place(f"lat{L}_lo", XT + 8192 * L + 4096, [4, SEQ], F32R))
           for L in range(2)]
    turn_lat = [Turn(lambda k, t, L=L: proj[:, t, L * CW + k * P:L * CW + (k + 1) * P], 4, *lat[L],
                     scale=lambda k, L=L: rowcols(("gql", "gkv")[L], k)) for L in range(2)]
    lat_scaled = sem("lat_scaled")
    g_uq = Gemm(at, wview("w_uq"), 4, 3, lambda part, k, t: lat[0][part][:, k, t * P:(t + 1) * P])
    g_ukv = Gemm(at, wview("w_ukv"), 4, 4, lambda part, k, t: lat[1][part][:, k, t * P:(t + 1) * P],
                 peeled=2)
    kv = place("kv", XT + 16384, [T, 2048])
    HQ, ROPE = 192, 64
    qk_sq = place("qk_sq", GT2, [T, 1536])
    pe_in = place("pe_in", GT2, [T, 16, ROPE])
    pe_out = place("pe_out", GT2 + 8192, [T, 16, ROPE])
    pe_tmp = place("pe_tmp", ACC, [T, 16, 32])
    kT = place("kT", XT, [12, SEQ])
    qT = lambda m: proj[:, m // 6, 2624 + 256 * (m % 6):2624 + 256 * (m % 6 + 1)]

    pos_float = sem("pos_float")

    crow = place("crow", SCR + 10240, [P])
    c_loaded, c_turned = sem("c_loaded"), sem("c_turned")

    def start_tensor(pe):
        pe.wait_ge(c_loaded, 32)
        pe.transpose(ps_turn[1][:, 0:KD], crow[0:KD, :], ident[0:KD, 0:KD]).then_inc(c_turned, 1)

    def small_tensor(pe):
        pe.wait_ge(start, 16 * NSTART)
        pe.transpose(ps_turn[0][:, 0:P], rows_in[:, 0, :], ident)
        pe.transpose(ps_turn[0][:, P:P + 94], rows_in[0:94, 1, :], ident[0:94, 0:94])
        pe.wait_ge(pos_float, 1)
        pe.transpose(ps_turn[0][:, SEQ:SEQ + T], posr[0:T, :], ident[0:T, 0:T]).then_inc(start_turned, 1)

    def start_vector(dve):
        dve.memset(epsc[:, :], EPS).then_inc(eps_set, 1)
        dve.wait_ge(c_ready, 1)

    def small_vector(dve):
        dve.wait_ge(start, 16 * NSTART)
        dve.tensor_copy(posr[0:T, :], posi[0:T, :]).then_inc(pos_float, 1)
        dve.wait_ge(start_turned, 1)
        dve.tensor_copy(cols[:, :], ps_turn[0][:, 0:P]).then_inc(start_cols, 1)
        dve.tensor_copy(posf[:, 0, :], ps_turn[0][:, SEQ:SEQ + T]).then_inc(start_cols, 1)
        dve.tensor_copy(colb[:, 0:62], ps_turn[0][:, P:P + 62]).then_inc(start_cols, 1)
        dve.tensor_copy(adacol[:, 1:3, :].rearrange("p a b -> p (a b)"),
                        ps_turn[0][:, P + 62:P + 94]).then_inc(start_cols, 1)
        rms_x.vector(dve)

    def start_scalar(act):
        for par in range(2):
            act.sem_inc(ada_stored[par], 16)
        act.wait_ge(c_turned, 1)
        act.activation(ccol[:, :], ps_turn[1][:, 0:KD], ACT.Silu).then_inc(c_ready, 1)
        start_loads(act)
        g_in2.load(act)
        act.wait_ge(start, 16 * NSTART)
        act.wait_ge(eps_set, 1)
        rms_x.scalar(act)
        act.wait_ge(inverse, 1)
        for t in range(T):
            act.activation(xn[:, t, :], x[:, t, :], ACT.Copy, scale=stat[:, 4 + t:5 + t]).then_inc(xn_ready, 1)

    def rowcols16(name):
        return cols[:, ROWS[name][0]:ROWS[name][0] + KD]

    adar_rows = dict(n=0)

    class AdaColumns:

        def __init__(self, first, gain, stored, summed):
            self.first, self.gain, self.stored, self.summed = first, gain, stored, summed
            self.n = adar_rows["n"]
            adar_rows["n"] += 1

        def scalar(self, act):
            for par in range(2):
                act.wait_ge(ada_stored[par], 16 * (self.stored // 2) + 16)
            if self.n:
                act.wait_ge(adar_turned, self.n)
            for i, src in enumerate((scratch, A["b_ada"].rearrange("o n -> (o n)"))):
                act.dma_start(adar[0:32, i, :], src[self.first:self.first + 2 * D].rearrange("(r q) -> r q", q=P)
                              ).then_inc(adar_loaded, 16)

        def tensor(self, pe):
            pe.wait_ge(adar_loaded, 32 * (self.n + 1))
            pe.wait_ge(ada_evac, self.summed)
            pe.matmul(ps_ada[:, 0:32], adar[0:32, 0, :], ident[0:32, 0:32], start=True, stop=False)
            pe.matmul(ps_ada[:, 0:32], adar[0:32, 1, :], ident[0:32, 0:32], start=False,
                      stop=True).then_inc(adar_turned, 1)

        def vector(self, dve):
            dve.wait_ge(adar_turned, self.n + 1)
            dve.tensor_copy(adacol[:, 0, :], ps_ada[:, 0:16]).then_inc(adacol_ready, 1)
            dve.scalar_tensor_tensor(scol[:, 0, :], ps_ada[:, 16:32], 1.0,
                                     cols[:, ROWS[self.gain][0]:ROWS[self.gain][0] + 16],
                                     ALU.add, ALU.mult).then_inc(adacol_ready, 1)
            dve.wait_ge(adacol_ready, 2 * self.n + 2)

    shifted1 = sem("shift_scale_1")

    def ada1_vector(dve):
        dve.wait_ge(ada_summed, 2 * D // CW)
        dve.tensor_tensor(adacol[:, 0, :], ps_ada[:, 0:KD], adacol[:, 1, :], ALU.add).then_inc(shifted1, 1)
        dve.tensor_tensor(scol[:, 0, :], ps_ada[:, KD:2 * KD], adacol[:, 2, :], ALU.add).then_inc(shifted1, 1)
        dve.wait_ge(shifted1, 2)
        dve.scalar_tensor_tensor(scol[:, 0, :], scol[:, 0, :], 1.0, rowcols16("g1"), ALU.add,
                                 ALU.mult).then_inc(shifted1, 1)
        dve.wait_ge(shifted1, 3)

    def turn_x_tensor(pe):
        pe.wait_ge(xn_ready, 2)
        pe.wait_ge(start_cols, 4)
    g_in.turn = turn_x

    def prepare_rest(c, u, j):
        if u == 0 and j is None:
            g_in2.vector(nc.vector)
            rope1_vector(nc.vector)

    def evac_proj(c, u, j):
        if u == 0 and j is None:
            g_in2.high(nc.scalar)
        b = c % 2
        col = Count(CW * u, 2 * CW, j).value
        for t in range(T):
            last = nc.scalar.activation(proj[:, t, bass.ds(col, CW)], ps_gemm[2 * b + t][:, :], ACT.Copy)
        last.then_inc(evac_done, 1)


    def lat_vector(dve):
        inv = rms_lat.vector(dve)
        for i in range(4):
            L, t = divmod(i, T)
            c = proj[:, t, L * CW:(L + 1) * CW]
            dve.tensor_scalar(c, c, inv(i), None, ALU.mult).then_inc(lat_scaled, 1)
        for turn in turn_lat:
            turn.vector(dve)

    def lat_tensor(pe):
        pe.wait_ge(lat_scaled, 4)
        for turn in turn_lat:
            turn.tensor(pe)
        pe.wait_ge(turn_lo, turn_lat[1].at_split + 2)

    def rope1_vector(dve):
        two_pi = 2 * np.pi
        c1 = 6.28125
        c2 = float(np.float32(np.round((two_pi - c1) * 2 ** 22) / 2 ** 22))
        c3 = two_pi - c1 - c2
        magic = 1.5 * 2 ** 23
        pi = 3.1415925
        ang, turn_n = rope1[:, 0, :, :], rope1[:, 1, :, :]
        for t in range(T):
            dve.tensor_scalar(ang[:, t, :], const[:, C_FREQ:C_FREQ + 32], posf[:, 0, t:t + 1], None,
                              ALU.mult).then_inc(rope_step, 1)
        dve.wait_ge(rope_step, 2)
        steps = [lambda: dve.tensor_scalar(turn_n, ang, 1 / two_pi, magic, ALU.mult, ALU.add),
                 lambda: dve.tensor_scalar(turn_n, turn_n, magic, None, ALU.subtract)]
        steps += [lambda c=c: dve.scalar_tensor_tensor(ang, turn_n, -c, ang, ALU.mult, ALU.add) for c in (c1, c2, c3)]
        steps += [lambda: dve.tensor_scalar(ang, ang, -pi, pi, ALU.max, ALU.min),
                  lambda: dve.scalar_tensor_tensor(turn_n, ang, -1.0, ang, ALU.mult, ALU.max),
                  lambda: dve.tensor_scalar(turn_n, turn_n, -1.0, np.pi / 2, ALU.mult, ALU.add)]
        for n, step in enumerate(steps):
            step().then_inc(rope_step, 1)
            dve.wait_ge(rope_step, 3 + n)
    rope_step, rope_ready = sem("rope_step"), sem("rope_ready")
    ROPE_STEPS = 10

    def rope1_scalar(act):
        act.wait_ge(rope_step, ROPE_STEPS)
        for i in range(2):
            act.activation(rope1[:, i, :, :], rope1[:, i, :, :], ACT.Sin).then_inc(rope_ready, 1)
    sin1, cos1 = rope1[:, 0, :, :], rope1[:, 1, :, :]

    def evac_scalar_to(dst):
        def evac(c, u, j):
            col = Count(CW * u, 2 * CW, j).value
            for t in range(T):
                last = nc.scalar.activation(dst(t, col), ps_gemm[2 * (c % 2) + t][:, :], ACT.Copy)
            last.then_inc(evac_done, 1)
        return evac

    def evac_gate_b(c, u, j):
        col = Count(GB0 + CW * u, 2 * CW, j).value
        for t in range(T):
            g = proj[:, t, bass.ds(col, CW)]
            last = nc.vector.tensor_tensor(g, ps_gemm[2 * (c % 2) + t][:, :], g, ALU.mult)
        last.then_inc(evac_done, 1)

    sq_ready, sq_used, hn = sem("sq_ready"), sem("sq_used"), sem("head_norm")
    hroot, qk_ready = sem("head_root"), sem("qk_ready")
    q4 = proj[:, :, Q0:Q0 + 1536].rearrange("p t (h d) -> p t h d", d=HQ)
    k4 = kv[:, :, :].rearrange("p t (h d) -> p t h d", d=256)[:, :, :, 0:P]
    sq_q = qk_sq[:, :, :].rearrange("p t (h d) -> p t h d", d=HQ)
    sq_k = place("k_sq", GT2, [T, 8, P])

    def q_squares(act):
        act.wait_ge(evac_done, g_uq.c + g_uq.n)
        act.activation(sq_q, q4, ACT.Square).then_inc(sq_ready, 1)
        for t in range(T):
            act.activation(etmp[:, t * 64:(t + 1) * 64], proj[:, t, 1024:1088], ACT.Square,
                           accum_out=pesum[:, t:t + 1])

    def q_sums(dve):
        dve.wait_ge(sq_ready, 1)
        dve.tensor_reduce(hstat[:, 0, :].rearrange("p (t h) -> p t h", t=T), sq_q, AX_X, ALU.add).then_inc(sq_used, 1)

    def evac_kv(c, u, j):
        evac_to_kv(c, u, j)
        if u == 0:
            q_squares(nc.scalar)
    evac_to_kv = evac_scalar_to(lambda t, c: kv[:, t, bass.ds(c, CW)])

    def beside_kv(c, u, j):
        if u == 1:
            q_sums(nc.vector)

    def heads_scalar(act):
        act.wait_ge(evac_done, g_ukv.c + 4)
        act.wait_ge(sq_used, 1)
        act.activation(sq_k[:, :, :, :], k4, ACT.Square).then_inc(sq_ready, 1)
        act.wait_ge(hn, 2)
        act.activation(hstat[:, 2:4, :], hstat[:, 0:2, :], ACT.Sqrt, bias=epsc[:, 0:1],
                       scale=1.0 / HQ).then_inc(hroot, 1)

    def heads_vector(dve):
        hs = lambda i: hstat[:, i, :].rearrange("p (t h) -> p t h", t=T)
        dve.wait_ge(sq_ready, 2)
        dve.tensor_reduce(hs(1), sq_k[:, :, :, :], AX_X, ALU.add).then_inc(sq_used, 1)
        dve.wait_ge(sq_used, 2)
        for t in range(T):
            dve.tensor_scalar(hs(1)[:, t, :], hs(1)[:, t, :], pesum[:, t:t + 1], None, ALU.add).then_inc(hn, 1)
        dve.wait_ge(hroot, 1)
        dve.reciprocal(hstat[:, 4:6, :], hstat[:, 2:4, :]).then_inc(hn, 1)
        dve.wait_ge(hn, 3)
        iq, ik = hs(4), hs(5)
        dve.tensor_tensor(q4, q4, iq[:, :, :, None].broadcast_to([P, T, 8, HQ]), ALU.mult).then_inc(hn, 1)
        dve.tensor_tensor(k4, k4, ik[:, :, :, None].broadcast_to([P, T, 8, P]), ALU.mult).then_inc(hn, 1)
        kpe = proj[:, :, 1024:1088][:, :, None, :].broadcast_to([P, T, 8, ROPE])
        dve.tensor_tensor(pe_in[:, :, 8:16, :], kpe, ik[:, :, :, None].broadcast_to([P, T, 8, ROPE]),
                          ALU.mult).then_inc(hn, 1)
        dve.wait_ge(hn, 6)
        gq = brd[:, 0:64][:, None, None, :].broadcast_to([P, T, 8, ROPE])
        gk = brd[:, 64:128][:, None, None, :].broadcast_to([P, T, 8, ROPE])
        dve.tensor_tensor(pe_in[:, :, 0:8, :], q4[:, :, :, P:HQ], gq, ALU.mult).then_inc(hn, 1)
        dve.tensor_tensor(pe_in[:, :, 8:16, :], pe_in[:, :, 8:16, :], gk, ALU.mult).then_inc(hn, 1)
        dve.wait_ge(hn, 8)
        dve.wait_ge(rope_ready, 2)
        x1, x2 = pe_in[:, :, :, 0:32], pe_in[:, :, :, 32:64]
        o1, o2 = pe_out[:, :, :, 0:32], pe_out[:, :, :, 32:64]
        cb, sb = (a[:, :, None, :].broadcast_to([P, T, 16, 32]) for a in (cos1, sin1))
        n = 8
        for o, a, b, op in ((o1, cb, sb, ALU.subtract), (o2, sb, cb, ALU.add)):
            dve.tensor_tensor(o, x1, a, ALU.mult).then_inc(hn, 1)
            dve.tensor_tensor(pe_tmp[:, :, :, :], x2, b, ALU.mult).then_inc(hn, 1)
            dve.wait_ge(hn, n + 2)
            dve.tensor_tensor(o, o, pe_tmp[:, :, :, :], op).then_inc(hn, 1)
            n += 3
            dve.wait_ge(hn, n)
        turn_qk.vector(dve)

    def qk_unit(dst, src, u, scale):
        ins = [(src(t, 2 * u + k), P, k * SEQ + t * P) for k in range(2) for t in range(T)]

        def copy(bank):
            if scale is None:
                return nc.vector.tensor_copy(dst(u), bank[:, :])
            return nc.vector.tensor_scalar(dst(u), bank[:, :], scale, None, ALU.mult)
        return ins, copy
    q_dst = lambda u: proj[:, u // 3, 2624 + CW * (u % 3):2624 + CW * (u % 3 + 1)]
    k_dst = lambda u: kT[:, 2 * u:2 * u + 2, :].rearrange("p a b -> p (a b)")
    qn_src = lambda t, h: proj[:, t, Q0 + HQ * h:Q0 + HQ * h + P]
    kn_src = lambda t, h: kv[:, t, 256 * h:256 * h + P]
    pe_src = lambda first: (lambda t, m: pe_out[:, t, first + 2 * (m - 8):first + 2 * (m - 8) + 2, :])
    turn_qk = Plain([qk_unit(q_dst, qn_src, u, colb[:, 60:61]) for u in range(4)]
                    + [qk_unit(k_dst, kn_src, u, colb[:, 61:62]) for u in range(4)]
                    + [qk_unit(q_dst, pe_src(0), u, None) for u in (4, 5)]
                    + [qk_unit(k_dst, pe_src(8), u, None) for u in (4, 5)])

    pbuf = place("pbuf", SCR, [3, BL])
    ptb = place("ptb", GT2, [2, BL])
    mla_scale = HQ ** -0.5
    s_filled, s_max, p_exp, p_ready = sem("s_filled"), sem("s_max"), sem("p_exp"), sem("p_ready")
    p_inv, pt_filled, pt_ready = sem("p_inv"), sem("pt_filled"), sem("pt_ready")
    ya_filled, ya_hi, ya_lo = sem("ya_filled"), sem("ya_hi"), sem("ya_lo")
    SPAN = ((0, P), (P, BL))

    def mla_tensor(pe):
        pe.wait_ge(hn, 14)
        turn_qk.tensor(pe)
        pe.wait_ge(turn_scaled, turn_qk.end)
        for i in range(H + 3):
            if i < H:
                h = i
                if 2 * (h - 2) > 0:
                    pe.wait_ge(p_exp, 2 * (h - 2))
                b, r = ps_gemm[h % 3], slice(64 * (h % 2), 64 * (h % 2) + 64)
                for t, (lo, up) in enumerate(SPAN):
                    pe.matmul(b[:, lo:up], qT(h)[:, t * P:(t + 1) * P], kT[:, h, 0:(t + 1) * P],
                              start=True, stop=False)
                    pe.matmul(b[:, lo:up], qT(8 + h // 2)[r, t * P:(t + 1) * P],
                              kT[r, 8 + h // 2, 0:(t + 1) * P], start=False, stop=False)
                    mm = pe.matmul(b[:, up - P:up], ident, const[:, C_MASKQ:C_MASKQ + P], start=False, stop=True)
                mm.then_inc(s_filled, 1)
            if 2 <= i < H + 2:
                h = i - 2
                pe.wait_ge(p_ready, h + 1)
                if h - 1 > 0:
                    pe.wait_ge(pt_ready, h - 1)
                b = ps[3 + h % 2]
                for k in range(3):
                    mm = pe.transpose(b[:, k * P:(k + 1) * P], pbuf[:, h % 3, k * P:(k + 1) * P], ident)
                mm.then_inc(pt_filled, 1)
            if i >= 3:
                h = i - 3
                pe.wait_ge(pt_ready, h + 1)
                if h % 2 == 0:
                    if h // 2 - 2 > 0:
                        pe.wait_ge(ya_lo, h // 2 - 2)
                b = ps_turn[(h // 2) % 3][:, (h % 2) * SEQ:(h % 2 + 1) * SEQ]
                v = lambda t: kv[:, t, 256 * h + P:256 * (h + 1)]
                pe.matmul(b, v(0), ptb[:, h % 2, 0:SEQ], start=True, stop=False)
                mm = pe.matmul(b[:, P:SEQ], v(1), ptb[:, h % 2, SEQ:BL], start=False, stop=True)
                if h % 2:
                    mm.then_inc(ya_filled, 1)

    def mla_vector(dve):
        def low(u):
            dve.wait_ge(ya_hi, u + 1)
            dve.tensor_tensor(yt_lo[:, 2 * u:2 * u + 2, :].rearrange("p a b -> p (a b)"), ps_turn[u % 3][:, :],
                              yt_hi[:, 2 * u:2 * u + 2, :].rearrange("p a b -> p (a b)").bitcast(F32),
                              ALU.subtract).then_inc(ya_lo, 1)
        for i in range(H + 1):
            if i < H:
                h = i
                dve.wait_ge(s_filled, h + 1)
                for t, (lo, up) in enumerate(SPAN):
                    dve.tensor_reduce(mst[:, 0, 2 * h + t:2 * h + t + 1], ps_gemm[h % 3][:, lo:up],
                                      AX_X, ALU.max).then_inc(s_max, 1)
                dve.wait_ge(s_max, 3 * h + 2)
                dve.tensor_scalar(mst[:, 1, 2 * h:2 * h + 2], mst[:, 0, 2 * h:2 * h + 2], -mla_scale, None,
                                  ALU.mult).then_inc(s_max, 1)
            if i >= 1:
                h = i - 1
                dve.wait_ge(p_exp, 2 * h + 2)
                dve.reciprocal(mst[:, 3, 2 * h:2 * h + 2], mst[:, 2, 2 * h:2 * h + 2]).then_inc(p_inv, 1)
                dve.wait_ge(p_inv, h + 1)
                for t, (lo, up) in enumerate(SPAN):
                    last = dve.tensor_scalar(pbuf[:, h % 3, lo:up], pbuf[:, h % 3, lo:up],
                                             mst[:, 3, 2 * h + t:2 * h + t + 1], None, ALU.mult)
                last.then_inc(p_ready, 1)
            if i >= 7 and i % 2:
                low((i - 7) // 2)
        low(1)
        low(2)
        low(3)

    def mla_scalar(act):
        for par in range(2):
            act.wait_ge(ada_stored[par], 16 * 11)
        def high(u):
            act.wait_ge(ya_filled, u + 1)
            act.activation(yt_hi[:, 2 * u:2 * u + 2, :].rearrange("p a b -> p (a b)"), ps_turn[u % 3][:, :],
                           ACT.Copy).then_inc(ya_hi, 1)
        for i in range(H + 2):
            if i < H:
                h = i
                act.wait_ge(s_max, 3 * h + 3)
                if h - 2 > 0:
                    act.wait_ge(pt_filled, h - 2)
                for t, (lo, up) in enumerate(SPAN):
                    act.activation(pbuf[:, h % 3, lo:up], ps_gemm[h % 3][:, lo:up], ACT.Exp,
                                   bias=mst[:, 1, 2 * h + t:2 * h + t + 1], scale=mla_scale,
                                   accum_out=mst[:, 2, 2 * h + t:2 * h + t + 1]).then_inc(p_exp, 1)
            if i >= 2:
                h = i - 2
                act.wait_ge(pt_filled, h + 1)
                act.activation(ptb[:, h % 2, :], ps[3 + h % 2][:, 0:BL], ACT.Copy).then_inc(pt_ready, 1)
            if i >= 6 and i % 2 == 0:
                high((i - 6) // 2)
        high(2)
        high(3)

    g_pmla = Gemm(at, wview("w_proj_mla"), 8, 4, lhs_y, ada=(4, D // 8))
    merge_step = sem("merge_step")

    def evac_merge(c, u, j):
        for t in range(T):
            g = proj[:, t, bass.ds(Count(GA0 + CW * u, 2 * CW, j).value, CW)]
            nc.vector.tensor_tensor(g, ps_gemm[2 * (c % 2) + t][:, :], g, ALU.mult).then_inc(merge_step, 1)
        nc.vector.wait_ge(merge_step, Count(2 * u + 2, 4, j).value)
        for t in range(T):
            g = proj[:, t, bass.ds(Count(GA0 + CW * u, 2 * CW, j).value, CW)]
            gb = proj[:, t, bass.ds(Count(GB0 + CW * u, 2 * CW, j).value, CW)]
            last = nc.vector.tensor_tensor(g, g, gb, ALU.add)
        last.then_inc(evac_done, 1)

    turn_m = Turn(lambda k, t: proj[:, t, GA0 + k * P:GA0 + (k + 1) * P], KD, xt_hi, xt_lo)

    gt_bias = proj[:, :, Q0:Q0 + D]
    gt_loaded, gt_ready = sem("gt_loaded"), sem("gt_ready")

    def gt_scalar(act):
        for par in range(2):
            act.wait_ge(ada_stored[par], 16 * 13)
        b_ada = A["b_ada"].rearrange("o n -> (o n)")
        for i, dst in enumerate((gt1, gt2)):
            a = (2 + 3 * i) * D
            act.dma_start(dst[:, :], scratch[a:a + D].rearrange("(o n) -> o n", o=1).broadcast_to([P, D])
                          ).then_inc(gt_loaded, 16)
            act.dma_start(gt_bias[:, i, :], b_ada[a:a + D].rearrange("(o n) -> o n", o=1).broadcast_to([P, D])
                          ).then_inc(gt_loaded, 16)

    def gt_vector(dve):
        dve.wait_ge(gt_loaded, 16 * 4)
        for i, dst in enumerate((gt1, gt2)):
            dve.tensor_tensor(dst[:, :], dst[:, :], gt_bias[:, i, :], ALU.add).then_inc(gt_ready, 1)
        dve.wait_ge(gt_ready, 2)

    g_out = Gemm(at, wview("w_out"), KD, 4, lhs_x)
    g_out.turn = turn_m
    restmp = place("restmp", SCR, [T, CW])
    res_step = sem("res_step")
    res_n = dict(n=0)

    def evac_residual(g, gate):
        first = res_n["n"]
        res_n["n"] += g.n * T if gate is not None else 0

        def evac(c, u, j):
            col = Count(CW * u, 2 * CW, j).value
            if gate is not None:
                for t in range(T):
                    nc.vector.tensor_tensor(restmp[:, t, :], ps_gemm[2 * (c % 2) + t][:, :],
                                            gate[:, bass.ds(col, CW)], ALU.mult).then_inc(res_step, 1)
                nc.vector.wait_ge(res_step, Count(first + 2 * u + 2, 4, j).value)
            for t in range(T):
                src = restmp[:, t, :] if gate is not None else ps_gemm[2 * (c % 2) + t][:, :]
                xc = x[:, t, bass.ds(col, CW)]
                last = nc.vector.tensor_tensor(xc, xc, src, ALU.add)
            last.then_inc(evac_done, 1)
        return evac
    evac_out1 = evac_residual(g_out, gt1)

    def evac_out(c, u, j):
        if u == 0 and j is None:
            gt_vector(nc.vector)
        evac_out1(c, u, j)

    KF = 5632 // P
    ht_hi = place("ht_hi", GT1, [KF, SEQ], F32R)
    ht_lo = place("ht_lo", GT1 + KF * SEQ * 4, [KF, SEQ], F32R)
    ftmp = place("ftmp", GT1 + 2 * KF * SEQ * 4, [T, CW])
    hbuf = place("hbuf", GT1 + 2 * KF * SEQ * 4 + 4096, [T, CW])
    assert GT1 + 2 * KF * SEQ * 4 + 8192 <= SCR + 4096
    lhs_h = lambda part, k, t: (ht_lo if part else ht_hi)[:, k, t * P:(t + 1) * P]
    silu_done = sem("silu_done")

    class Ffn:

        def __init__(self, name, w_gate, w_up, up0, w_down, scale, bias, gate):
            at_pair = lambda u: ((u % 2) * up0 + CW * (u // 2), CW)
            self.silu0 = silu_n["n"]
            silu_n["n"] += KF // 4
            self.rms = Rms([x[:, t, :] for t in range(T)], D, lambda i: xn[:, i, :], 0)
            self.xn0 = xn_n["n"]
            xn_n["n"] += T
            self.turn = Turn(lambda k, t: xn[:, t, k * P:(k + 1) * P], KD, xt_hi, xt_lo, scale, bias)
            self.g = Gemm(at, None, KD, 2 * KF // 4, lhs_x, cols=at_pair, peeled=2)
            self.g.by_half = (w_gate, w_up)
            self.g.turn = self.turn
            self.at, self.at_split = turns["n"], turns["split"]
            turns["n"] += KF // 2
            turns["split"] += KF // 2
            self.down = Gemm(at, w_down, KF, 4, lhs_h)
            self.evac_down = evac_residual(self.down, gate)

        def scalar(self, act, more=lambda act: None):
            act.wait_ge(evac_done, self.before)
            self.rms.scalar(act)
            more(act)

            def evac(c, u, j):
                if u % 2 == 0:
                    pair = Count(u // 2, 1, j)
                    act.wait_ge(evac_done, c.value)
                    for t in range(T):
                        last = act.activation(ftmp[:, t, :], ps_gemm[2 * (c % 2) + t][:, :], ACT.Silu)
                    last.then_inc(evac_done, 1)
                elif j is not None or u > 1:
                    self.high(act, Count(u // 2 - 1, 1, j))
            scalar_gemm(act, self.g, evac)
            self.high(act, Count(KF // 4 - 1))
            scalar_gemm(act, self.down, None)

        def high(self, act, pair):
            for v in range(2):
                m = Count(self.at_split + 2 * pair.first + v, 2 * pair.per, pair.j)
                n = Count(self.at + 2 * pair.first + v, 2 * pair.per, pair.j)
                act.wait_ge(turn_scaled, (n + 1).value)
                k = Count(4 * pair.first + 2 * v, 4 * pair.per, pair.j).value
                act.activation(ht_hi[:, bass.ds(k, 2), :], tmp[:, v, :, :], ACT.Copy).then_inc(turn_hi, 1)

        def vector(self, dve, more=lambda dve: None):
            inv = self.rms.vector(dve)
            for t in range(T):
                dve.tensor_scalar(xn[:, t, :], x[:, t, :], inv(t), None, ALU.mult).then_inc(xn_ready, 1)
            more(dve)

            def copied(pair):
                for v in range(2):
                    m = Count(self.at_split + 2 * pair.first + v, 2 * pair.per, pair.j)
                    n = Count(self.at + 2 * pair.first + v, 2 * pair.per, pair.j)
                    dve.wait_ge(turn_filled, (n + 1).value)
                    dve.wait_ge(turn_lo, (m - v).value)
                    dve.tensor_copy(tmp[:, v, :, :].rearrange("p a b -> p (a b)"),
                                    ps_turn[v][:, :]).then_inc(turn_scaled, 1)

            def low(pair):
                for v in range(2):
                    m = Count(self.at_split + 2 * pair.first + v, 2 * pair.per, pair.j)
                    k = Count(4 * pair.first + 2 * v, 4 * pair.per, pair.j).value
                    dve.wait_ge(turn_hi, (m + 1).value)
                    dve.tensor_tensor(ht_lo[:, bass.ds(k, 2), :], tmp[:, v, :, :],
                                      ht_hi[:, bass.ds(k, 2), :].bitcast(F32), ALU.subtract).then_inc(turn_lo, 1)

            def evac(c, u, j):
                if u % 2 == 0:
                    if j is not None or u > 2:
                        low(Count(u // 2 - 2, 1, j))
                    if j is not None or u > 0:
                        copied(Count(u // 2 - 1, 1, j))
                    return
                dve.wait_ge(evac_done, c.value)
                for t in range(T):
                    last = dve.tensor_tensor(hbuf[:, t, :], ps_gemm[2 * (c % 2) + t][:, :], ftmp[:, t, :],
                                             ALU.mult)
                last.then_inc(evac_done, 1)
            vector_gemm(dve, self.g, evac)
            low(Count(KF // 4 - 2))
            copied(Count(KF // 4 - 1))
            low(Count(KF // 4 - 1))
            vector_gemm(dve, self.down, self.evac_down)

        def tensor(self, pe, more=lambda pe: None):
            pe.wait_ge(xn_ready, self.xn0 + T + 2)
            more(pe)

            def fill(pair, c_end):
                pe.wait_ge(evac_done, c_end.value)
                for v in range(2):
                    n = Count(self.at + 2 * pair.first + v, 2 * pair.per, pair.j)
                    pe.wait_ge(turn_scaled, (n - v).value)
                    for k in range(2):
                        for t in range(T):
                            mm = pe.transpose(ps_turn[v][:, k * SEQ + t * P:k * SEQ + (t + 1) * P],
                                              hbuf[:, t, (2 * v + k) * P:(2 * v + k + 1) * P], ident)
                    mm.then_inc(turn_filled, 1)

            def middle(u, j):
                if u % 2 == 0 and (j is not None or u > 0):
                    fill(Count(u // 2 - 1, 1, j), Count(self.g.c + u, 2, j))
            tensor_gemm(pe, self.g, middle)
            fill(Count(KF // 4 - 1), Count(self.g.c + self.g.n))
            pe.wait_ge(turn_lo, self.at_split + KF // 2)
            tensor_gemm(pe, self.down)
    silu_n, xn_n = dict(n=0), dict(n=0)

    def halves(g, u):
        return g.by_half[u % 2] if g.weights is None else g.weights

    w_f1 = wview("w_ffn_in")
    ada2 = AdaColumns(3 * D, "g2", 16, 24)
    ffn1 = Ffn("ffn1", w_f1, w_f1, 5632, wview("w_ffn_out"),
               lambda k: scol[:, 0, k:k + 1], lambda k: adacol[:, 0, k:k + 1], gt2)
    ffn1.before = g_out.c + g_out.n


    NIN2 = 5184
    XBC, DT, QN, KC0, VC0, KS0, VS0, KW0, VW0, GN = 1024, 2560, 2576, 3600, 3856, 4112, 4368, 4624, 4880, 5136
    P2 = 131072
    proj2 = place("proj2", P2, [T, NIN2])
    w1 = [place("w1k", GT2, [16, 256]), place("w1v", P2 + 41472, [16, 256])]
    SM2 = 197120
    adt = place("adt", SM2, [T, 16])
    dtv = place("dtv", SM2 + 128, [T, 16])
    dtl = place("dtl", SM2 + 256, [T, 16])
    bias3 = place("bias3", SM2 + 384, [3, 16])
    gate2 = place("gate2", SM2 + 576, [T, 16, 3])
    hidT = place("hidT", SM2 + 1024, [4, 60])
    w2 = [place("w2k", SM2 + 2048, [2, 64]), place("w2v", SM2 + 2560, [2, 64])]
    kcmp = place("kcmp", SM2 + 3072, [2, 2, 15])
    cst = place("cst", SM2 + 3328, [4, T * 16])
    ea = place("ea", SM2 + 3840, [16])
    pe_odd = place("pe_odd", SM2 + 3904, [32])

    rms_a = Rms([x[:, t, :] for t in range(T)], D, lambda i: xn[:, i, :], 0)
    xn_a = xn_n["n"]
    xn_n["n"] += T
    turn_a = Turn(lambda k, t: xn[:, t, k * P:(k + 1) * P], KD, xt_hi, xt_lo, lambda k: rowcols("ga", k))
    g_b = Gemm(at, wview("w_in_2"), KD, 10, lhs_x)
    g_b.turn = turn_a
    g_b2 = Narrow("w_in_2_rest", at, wview("w_in_2"), 5120, (188928, 188928 + 4096, SCR))
    w1_loaded = sem("w1_loaded")

    def norm_a_scalar(act):
        act.wait_ge(evac_done, ffn1.down.c + 4)
        g_b2.load(act)
        for i, kv_ in enumerate("kv"):
            act.dma_start(w1[i][:, :, :], A[f"cmp_w1_{kv_}_2"].rearrange("o (u p) n -> p (o u) n", p=P)
                          ).then_inc(w1_loaded, 16)
            act.dma_start(w2[i][:, :, :], A[f"cmp_w2_{kv_}_2"].rearrange("o (u p) n -> p (o u) n", p=P)
                          ).then_inc(w1_loaded, 16)
        rms_a.scalar(act)

    def norm_a_vector(dve):
        inv = rms_a.vector(dve)
        for t in range(T):
            dve.tensor_scalar(xn[:, t, :], x[:, t, :], inv(t), None, ALU.mult).then_inc(xn_ready, 1)

    def norm_a_tensor(pe):
        pe.wait_ge(xn_ready, xn_a + T + 2)

    def evac_b(c, u, j):
        if u == 0 and j is None:
            g_b2.high(nc.scalar)
        evac_proj2(c, u, j)
    evac_proj2 = evac_scalar_to(lambda t, c: proj2[:, t, bass.ds(c, CW)])

    def prepare_rest2(c, u, j):
        if u == 0 and j is None:
            g_b2.vector(nc.vector)

    PADW = 3 + SEQ
    xbcT = place("xbcT", XT, [12, PADW])
    xc = place("xc", XT + 12544, [12, SEQ])
    gT = place("gT", XT + 24832, [2, BL])
    decay = place("decay", XT + 27904, [3, BL])
    xs = place("xs", PROJ, [T, 1024])
    xdt = place("xdt", PROJ + 8192, [T, 1024])
    ys = place("ys", 188928, [T, 1024])
    turn_xbc = Plain([([(proj2[:, t, XBC + (2 * u + k) * P:XBC + (2 * u + k + 1) * P], P, k * SEQ + t * P)
                        for k in range(2) for t in range(T)],
                       lambda bank, u=u: nc.vector.tensor_copy(xbcT[:, 2 * u:2 * u + 2, 3:PADW],
                                                               bank[:, :].rearrange("p (a b) -> p a b", a=2)))
                      for u in (4, 5, 0, 1, 2, 3)])
    turn_xs = Plain([([(xc[:, 4 * m + k, t * P:(t + 1) * P], P, k * P) for k in range(4)],
                      lambda bank, t=t, m=m: nc.vector.tensor_copy(xs[:, t, 512 * m:512 * (m + 1)], bank[:, :]))
                     for m in range(2) for t in range(T)])
    CONV = [8, 9, 10, 11, 0, 1, 2, 3, 4, 5, 6, 7]
    conv, xc_ready = sem("conv"), sem("xc_ready")
    ssd_v, ssd_v_at = sem("ssd_vector"), steps("pad", "shifted", "abs", "dt", "decay_rate", "bias0", "bias1", "bias2",
                   "g0", "g1", "xdt0", "xdt1")
    ssd_a, ssd_a_at = sem("ssd_scalar"), steps("exp_alog", "exp", "log", "z0", "z1")
    ssd_p, ssd_p_at = sem("ssd_tensor"), steps("sums", "g0", "g1")
    seg_filled, decay_ready, m2_ready, y_filled = sem("seg_filled"), sem("decay_ready"), sem("m2_ready"), sem("y_filled")
    y_step = sem("y_step")
    ps_y, ps_seg = ps[0:4], ps[4:7]
    HS = 16

    def ssd_tensor(pe):
        pe.wait_ge(evac_done, g_b2.c + 1)
        turn_xbc.tensor(pe)
        pe.wait_ge(ssd_v, ssd_v_at["decay_rate"])
        cum, after, maskt = (const[:, c:c + P] for c in (C_CUM, C_AFTER, C_MASKT))
        b = ps[7]
        pe.wait_ge(turn_scaled, turn_xbc.end)
        pe.matmul(b[:, 0:16], cum, adt[:, 0, :], start=True, stop=True)
        pe.matmul(b[:, 16:32], after, adt[:, 0, :], start=True, stop=True)
        pe.matmul(b[:, 32:48], cum, adt[:, 1, :], start=True, stop=True).then_inc(ssd_p, 1)
        for g in range(2):
            pe.wait_ge(xc_ready, 4)
            keys_by_queries(pe, ps_gemm[g], lambda kt: xc[:, 8 + g, kt * P:(kt + 1) * P],
                                         lambda a, z: xc[:, 10 + g, a:z]).then_inc(ssd_p, 1)
        pe.wait_ge(xc_ready, 12)
        pe.wait_ge(ssd_v, ssd_v_at["bias2"])
        turn_xs.tensor(pe)
        pe.wait_ge(ssd_v, ssd_v_at["xdt1"])
        for i in range(HS + 2):
            if i < HS:
                h = i
                if 3 * (h - 2) > 0:
                    pe.wait_ge(decay_ready, 3 * (h - 2))
                b = ps_seg[h % 3]
                rate = lambda t: adt[:, t, h:h + 1].broadcast_to([P, P])
                pe.matmul(b[:, 0:P], rate(0), cum, start=True, stop=False)
                pe.matmul(b[:, 0:P], ident, maskt, start=False, stop=True)
                pe.matmul(b[:, P:BL], rate(1), cum[:, None, :].broadcast_to([P, 2, P]), start=True, stop=False)
                pe.matmul(b[:, 2 * P:BL], ident, maskt, start=False, stop=True).then_inc(seg_filled, 1)
            if i >= 2:
                h = i - 2
                pe.wait_ge(m2_ready, h + 1)
                o = lambda t: ps_y[2 * t + h // 8][:, (h % 8) * 64:(h % 8 + 1) * 64]
                m = lambda k: decay[:, h % 3, k * P:(k + 1) * P]
                v = lambda t: xdt[:, t, h * 64:(h + 1) * 64]
                pe.matmul(o(0), m(0), v(0), start=True, stop=True)
                pe.matmul(o(1), m(1), v(0), start=True, stop=False)
                pe.matmul(o(1), m(2), v(1), start=False, stop=True).then_inc(y_filled, 1)

    def ssd_vector(dve):
        dve.wait_ge(evac_done, g_b2.c + 1)
        dve.memset(xbcT[:, :, 0:3], 0.0).then_inc(ssd_v, 1)
        bc = lambda a: a[:, None, :].broadcast_to([P, T, 16])
        dve.tensor_tensor(dtv[:, :, :], proj2[:, :, DT:DT + 16], bc(brd[:, 128:144]), ALU.add).then_inc(ssd_v, 1)
        dve.wait_ge(ssd_v, ssd_v_at["shifted"])
        dve.scalar_tensor_tensor(dtl[:, :, :], dtv[:, :, :], -1.0, dtv[:, :, :], ALU.mult, ALU.max).then_inc(ssd_v, 1)
        dve.wait_ge(ssd_a, ssd_a_at["log"])
        dve.scalar_tensor_tensor(dtv[:, :, :], dtv[:, :, :], 0.0, dtl[:, :, :], ALU.max, ALU.add).then_inc(ssd_v, 1)
        dve.wait_ge(ssd_v, ssd_v_at["dt"])
        dve.scalar_tensor_tensor(adt[:, :, :], dtv[:, :, :], -1.0, bc(ea[:, :]), ALU.mult, ALU.mult).then_inc(ssd_v, 1)
        turn_xbc.vector(dve)
        for j in range(4):
            for n, c in enumerate(CONV):
                w = colb[:, 12 + 12 * j + c:13 + 12 * j + c]
                src = xbcT[:, c, j:j + SEQ]
                if j == 0:
                    dve.wait_ge(turn_scaled, turn_xbc.at + n // 2 + 1)
                    dve.tensor_scalar(xc[:, c, :], src, w, None, ALU.mult).then_inc(conv, 1)
                else:
                    dve.wait_ge(conv, 12 * (j - 1) + n + 1)
                    dve.scalar_tensor_tensor(xc[:, c, :], src, w, xc[:, c, :], ALU.mult,
                                             ALU.add).then_inc(conv, 1)
        dve.wait_ge(ssd_p, ssd_p_at["sums"])
        b = ps[7]
        dve.tensor_scalar(bias3[:, 0, :], b[:, 0:16], -1.0, None, ALU.mult).then_inc(ssd_v, 1)
        dve.tensor_copy(bias3[:, 1, :], b[:, 16:32]).then_inc(ssd_v, 1)
        dve.tensor_scalar(bias3[:, 2, :], b[:, 32:48], -1.0, None, ALU.mult).then_inc(ssd_v, 1)
        for g in range(2):
            dve.wait_ge(ssd_p, ssd_p_at[f"g{g}"])
            dve.tensor_copy(gT[:, g, :], ps_gemm[g][:, 0:BL]).then_inc(ssd_v, 1)
        turn_xs.vector(dve)
        dve.wait_ge(turn_scaled, turn_xs.end)
        for t in range(T):
            dve.tensor_tensor(xdt[:, t, :].rearrange("p (h d) -> p h d", d=64),
                                           xs[:, t, :].rearrange("p (h d) -> p h d", d=64),
                                           dtv[:, t, :, None].broadcast_to([P, 16, 64]), ALU.mult).then_inc(ssd_v, 1)
        for h in range(HS):
            dve.wait_ge(decay_ready, 3 * h + 3)
            d = decay[:, h % 3, :]
            dve.tensor_tensor(d, d, gT[:, h // 8, :], ALU.mult).then_inc(m2_ready, 1)
        n = 0
        for t in range(T):
            dve.tensor_tensor(ys[:, t, :].rearrange("p (h d) -> p h d", d=64),
                              xs[:, t, :].rearrange("p (h d) -> p h d", d=64),
                              brd[:, 160:176][:, :, None].broadcast_to([P, 16, 64]), ALU.mult).then_inc(y_step, 1)
        dve.wait_ge(y_step, 2)
        dve.wait_ge(y_filled, HS)
        for t in range(T):
            for f in range(2):
                o = ys[:, t, 512 * f:512 * (f + 1)]
                dve.tensor_tensor(o, o, ps_y[2 * t + f][:, :], ALU.add).then_inc(y_step, 1)
        dve.wait_ge(y_step, 6)
        dve.wait_ge(ssd_a, ssd_a_at["z1"])
        for t in range(T):
            dve.tensor_tensor(ys[:, t, :], ys[:, t, :], proj2[:, t, 0:1024], ALU.mult).then_inc(y_step, 1)
        inv = rms_s.vector(dve)
        for t in range(T):
            dve.tensor_scalar(ys[:, t, :], ys[:, t, :], inv(t), None, ALU.mult).then_inc(y_step, 1)

    rms_s = Rms([ys[:, t, :] for t in range(T)], 1024, lambda i: xdt[:, i, :], 0)

    def ssd_scalar(act):
        act.wait_ge(start, 16 * NSTART)
        act.activation(ea[:, :], brd[:, 144:160], ACT.Exp).then_inc(ssd_a, 1)
        act.wait_ge(ssd_v, ssd_v_at["abs"])
        act.activation(dtl[:, :, :], dtl[:, :, :], ACT.Exp, scale=-1.0).then_inc(ssd_a, 1)
        act.wait_ge(ssd_a, ssd_a_at["exp"])
        act.activation(dtl[:, :, :], dtl[:, :, :], ACT.Ln, bias=ones[:, 0:1]).then_inc(ssd_a, 1)
        for n, c in enumerate(CONV):
            act.wait_ge(conv, 36 + n + 1)
            act.activation(xc[:, c, :], xc[:, c, :], ACT.Silu, bias=colb[:, c:c + 1]).then_inc(xc_ready, 1)
        for t in range(T):
            act.activation(proj2[:, t, 0:1024], proj2[:, t, 0:1024], ACT.Silu).then_inc(ssd_a, 1)
        act.wait_ge(ssd_v, ssd_v_at["bias2"])
        for h in range(HS):
            act.wait_ge(seg_filled, h + 1)
            if h - 2 > 0:
                act.wait_ge(y_filled, h - 2)
            for k in range(3):
                act.activation(decay[:, h % 3, k * P:(k + 1) * P], ps_seg[h % 3][:, k * P:(k + 1) * P], ACT.Exp,
                               bias=bias3[:, k, h:h + 1]).then_inc(decay_ready, 1)
        act.wait_ge(y_step, 8)
        rms_s.scalar(act)

    qu = place("qu", XT, [8, SEQ])
    qrT = place("qrT", XT + 8192, [8, SEQ])
    ksw = [proj2[:, br, 0:1024].rearrange("p (a b s) -> p a b s", a=2, b=2) for br in range(2)]
    vcmp = proj2[:, 0, 1024:2048].rearrange("p (g j d) -> p g j d", g=4, j=4)
    fl = [place("flk", XT + 20480, [16, 4, 15]), place("flv", XT + 24320, [16, 4, 15])]
    pc = place("pc", XT + 28160, [T, 16, 32])
    qr = place("qr", PROJ, [T, 1024])
    qp = place("qp", PROJ + 8192, [T, 1024])
    yatt = place("yatt", PROJ + 8192, [T, 1024])
    rt = place("rt", SCR, [4, T, 16, 8])
    hid = place("hid", SCR + 9216, [2, 256])
    pcT = place("pcT", GT2, [8, P])
    cs = place("cs", GT2 + 5120, [T, 16, 15])
    nst = place("nst", GT2 + 8192, [5, 64])
    pb2 = place("pb2", PROJ, [4, BL])
    pt2 = place("pt2", SCR + 3072, [4, BL])
    cos2 = const[:, C_COS2:C_COS2 + 16].rearrange("p (t d) -> p t d", t=T)
    sin2 = const[:, C_SIN2:C_SIN2 + 16].rearrange("p (t d) -> p t d", t=T)
    rot = sem("rot")

    def q_unit(dst, src, u):
        ins = [(src[:, t, (2 * u + k) * P:(2 * u + k + 1) * P], P, k * SEQ + t * P)
               for k in range(2) for t in range(T)]
        return ins, lambda bank: nc.vector.tensor_copy(dst[:, 2 * u:2 * u + 2, :].rearrange("p a b -> p (a b)"),
                                                       bank[:, :])

    def k_unit(dst, c0):
        ins = [(proj2[:, t, c0 + k * P:c0 + (k + 1) * P], P, k * SEQ + t * P) for k in range(2) for t in range(T)]

        def copy(bank):
            for b in range(2):
                r = slice(64 * b, 64 * b + 64)
                last = nc.vector.tensor_copy(dst[r, :, b, :], bank[r, :].rearrange("p (a s) -> p a s", a=2))
            return last
        return ins, copy
    turn_nq = Plain([q_unit(qu, qp, u) for u in range(4)]
                    + [q_unit(qrT, qr, u) for u in range(4)]
                    + [k_unit(ksw[0], KS0), k_unit(ksw[1], KW0)])
    cmp_v, cmp_v_at = sem("cmp_vector"), steps("zeros", "pe_odd", *(f"f{n}" for n in range(8)), "hidT", "kc0", "kc1",
                   *(f"vc{j}" for j in range(4)), "cs0", "cs1", "max", "sub", "sum", "inv", "coef", "masked",
                   "pc", "pcT0", "pcT1")
    cmp_a, cmp_a_at = sem("cmp_scalar"), steps("hid0", "hid1", "gates", "exp")
    cmp_p, cmp_p_at = sem("cmp_tensor"), steps("t0", "t1", "t2", "t3", "hid0", "hid1", "hidT", "kc", "vc", "cs0", "cs1",
                   "pcT0", "pcT1")
    nsa_scale = 64 ** -0.5
    n_filled, n_max, n_exp, n_inv, n_ready = (sem(f"nsa_{n}") for n in ("filled", "max", "exp", "inverse", "ready"))
    npt_filled, npt_ready, o_filled, o_ready = (sem(f"nsa_{n}") for n in ("pt_filled", "pt_ready", "o_filled", "o_ready"))
    UN = 32

    def cmp_tensor(pe):
        pe.wait_ge(rot, 14)
        turn_nq.tensor(pe)
        pe.wait_ge(turn_scaled, turn_nq.end)
        pe.wait_ge(y_step, 6)
        for n in range(4):
            c0 = (KC0, VC0)[n // 2] + P * (n % 2)
            for k in range(2):
                for t in range(T):
                    mm = pe.transpose(ps[n][0:64, k * SEQ + t * P:k * SEQ + (t + 1) * P],
                                      proj2[:, t, c0 + 64 * k:c0 + 64 * (k + 1)], ident)
            mm.then_inc(cmp_p, 1)
        pe.wait_ge(w1_loaded, 64)
        for i in range(2):
            pe.wait_ge(cmp_v, cmp_v_at[f"f{4 * i + 3}"])
            for u in range(16):
                mm = pe.matmul(ps[4 + i][0:60, 0:256], fl[i][:, u, :, :].rearrange("p h i -> p (h i)"),
                               w1[i][:, u, :], start=(u == 0), stop=(u == 15))
            mm.then_inc(cmp_p, 1)
        pe.wait_ge(cmp_a, cmp_a_at["hid1"])
        for i in range(2):
            for f in range(2):
                mm = pe.transpose(ps[6][:, 60 * (2 * i + f):60 * (2 * i + f + 1)], hid[0:60, i, f * P:(f + 1) * P],
                                  ident[0:60, 0:60])
        mm.then_inc(cmp_p, 1)
        pe.wait_ge(cmp_v, cmp_v_at["hidT"])
        for f in range(2):
            mm = pe.matmul(ps[7][0:64, 0:60], w2[0][:, f, :], hidT[:, f, :], start=(f == 0), stop=(f == 1))
        mm.then_inc(cmp_p, 1)
        pe.wait_ge(cmp_v, cmp_v_at["hidT"])
        for g in range(4):
            for f in range(2):
                mm = pe.matmul(ps[6][0:15, 256 + 64 * g:256 + 64 * (g + 1)], hidT[:, 2 + f, 15 * g:15 * (g + 1)],
                               w2[1][:, f, :], start=(f == 0), stop=(f == 1))
        mm.then_inc(cmp_p, 1)
        pe.wait_ge(cmp_v, cmp_v_at["kc1"])
        for t in range(T):
            for n in range(8):
                a, i = n // 4, n % 4
                o = ps[4 + t][:, 0:240].rearrange("p (a b i k) -> p a b i k", a=2, b=2, i=4)
                mm = pe.matmul(o[:, a, :, i, :], qu[:, 4 * a + i, t * P:(t + 1) * P], kcmp[:, a, :, :],
                               start=True, stop=True)
            mm.then_inc(cmp_p, 1)
        pe.wait_ge(cmp_v, cmp_v_at["pc"])
        for t in range(T):
            for m in range(4):
                mm = pe.transpose(ps[6 + t][:, m * P:(m + 1) * P],
                                  pc[:, t, 4 * m:4 * m + 4, :].rearrange("p n i -> p (n i)"), ident)
            mm.then_inc(cmp_p, 1)

    def rope2_vector(dve):
        dve.wait_ge(y_step, 10)
        for t in range(T):
            for dst in (qp, qr):
                for a in range(2):
                    at_a = slice(512 * a, 512 * (a + 1))
                    dve.tensor_copy(dst[:, t, at_a].rearrange("p (i b d) -> p i b d", i=4, b=2),
                                    proj2[:, t, QN:QN + 1024][:, at_a].rearrange("p (b i d) -> p i b d", i=4, b=2)
                                    ).then_inc(rot, 1)
        dve.wait_ge(rot, 8)
        n = 8
        jobs = [(qr[:, :, :], 16), (proj2[:, :, KS0:KS0 + 256], 4), (proj2[:, :, KW0:KW0 + 256], 4)]
        for src, heads in jobs:
            v = src.rearrange("p t (h d) -> p t h d", d=64)
            x1, x2 = v[:, :, :, 0:8], v[:, :, :, 8:16]
            c, s = (a[:, :, None, :].broadcast_to([P, T, heads, 8]) for a in (cos2, sin2))
            o = [rt[:, i, :, 0:heads, :] for i in range(4)]
            for dst, a, b in ((o[0], x1, c), (o[1], x2, s), (o[2], x2, c), (o[3], x1, s)):
                last = dve.tensor_tensor(dst, a, b, ALU.mult)
            last.then_inc(rot, 1)
            n += 1
            dve.wait_ge(rot, n)
            dve.tensor_tensor(x1, o[0], o[1], ALU.subtract)
            dve.tensor_tensor(x2, o[2], o[3], ALU.add).then_inc(rot, 1)
            n += 1
            dve.wait_ge(rot, n)
        assert n == 14

    def cmp_vector(dve):
        dve.memset(pc[:, :, :, :], 0.0)
        dve.memset(kcmp[:, :, :, :], 0.0)
        dve.memset(vcmp, 0.0)
        for br in range(2):
            for b in range(2):
                last = dve.memset(ksw[br][64 - 64 * b:P - 64 * b, :, b, :], 0.0)
        last.then_inc(cmp_v, 1)
        r = ROWS["pek"][0]
        dve.tensor_copy(pe_odd[0:64, :], cols[64:P, r:r + 32]).then_inc(cmp_v, 1)
        turn_nq.vector(dve)
        dve.wait_ge(cmp_v, cmp_v_at["pe_odd"])
        for n in range(4):
            dve.wait_ge(cmp_p, cmp_p_at[f"t{n}"])
            i, pair = divmod(n, 2)
            for odd in range(2):
                bank = ps[n][0:64, :]
                pe_ = (pe_odd[0:64, 16 * i:16 * i + 16] if odd
                       else cols[0:64, r + 16 * i:r + 16 * i + 16])
                src = bank.rearrange("p (h b u r) -> p r u h b", h=2, b=16, u=8)[:, odd, :, :, :]
                for half in range(2):
                    last = dve.tensor_tensor(
                        fl[i][64 * odd:64 * odd + 64, 8 * half:8 * half + 8, 2 * pair:2 * pair + 2, :],
                        src[:, :, :, half:half + 15],
                        pe_[:, 8 * half:8 * half + 8][:, :, None, None].broadcast_to([64, 8, 2, 15]), ALU.add)
                last.then_inc(cmp_v, 1)
        dve.wait_ge(cmp_p, cmp_p_at["hidT"])
        dve.tensor_copy(hidT[:, :, :].rearrange("p a b -> p (a b)"), ps[6][:, 0:240]).then_inc(cmp_v, 1)
        dve.wait_ge(cmp_p, cmp_p_at["kc"])
        for b in range(2):
            dve.tensor_copy(kcmp[64 * b:64 * b + 64, :, b, :],
                                         ps[7][0:64, 0:60].rearrange("p (a b i) -> p b a i", a=2, b=2)[:, b, :, :]).then_inc(cmp_v, 1)
        dve.wait_ge(cmp_p, cmp_p_at["vc"])
        for j in range(4):
            dve.tensor_copy(vcmp[32 * j:32 * j + 15, :, j, :],
                                         ps[6][0:15, 256:512].rearrange("p (g d) -> p g d", g=4)).then_inc(cmp_v, 1)
        for t in range(T):
            dve.wait_ge(cmp_p, cmp_p_at[f"cs{t}"])
            madd = const[:, C_CMPADD + 15 * t:C_CMPADD + 15 * (t + 1)]
            dve.scalar_tensor_tensor(cs[:, t, :, :], ps[4 + t][:, 0:240].rearrange("p (n i) -> p n i", n=16),
                                                  nsa_scale, madd[:, None, :].broadcast_to([P, 16, 15]),
                                                  ALU.mult, ALU.add).then_inc(cmp_v, 1)
        st = lambda i: cst[:, i, :].rearrange("p (t n) -> p t n", t=T)
        wide = lambda i: st(i)[:, :, :, None].broadcast_to([P, T, 16, 15])
        dve.wait_ge(cmp_v, cmp_v_at["cs1"])
        dve.tensor_reduce(st(0), cs[:, :, :, :], AX_X, ALU.max).then_inc(cmp_v, 1)
        dve.wait_ge(cmp_v, cmp_v_at["max"])
        dve.tensor_tensor(cs[:, :, :, :], cs[:, :, :, :], wide(0), ALU.subtract).then_inc(cmp_v, 1)
        dve.wait_ge(cmp_a, cmp_a_at["exp"])
        dve.tensor_reduce(st(1), cs[:, :, :, :], AX_X, ALU.add).then_inc(cmp_v, 1)
        dve.wait_ge(cmp_v, cmp_v_at["sum"])
        dve.reciprocal(st(2), st(1)).then_inc(cmp_v, 1)
        dve.wait_ge(cmp_v, cmp_v_at["inv"])
        dve.wait_ge(cmp_a, cmp_a_at["gates"])
        dve.tensor_tensor(st(3), st(2), gate2[:, :, :, 0], ALU.mult).then_inc(cmp_v, 1)
        mmul = const[:, C_CMPMUL:C_CMPMUL + 30].rearrange("p (t i) -> p t i", t=T)
        dve.tensor_tensor(cs[:, :, :, :], cs[:, :, :, :],
                                       mmul[:, :, None, :].broadcast_to([P, T, 16, 15]), ALU.mult).then_inc(cmp_v, 1)
        dve.wait_ge(cmp_v, cmp_v_at["masked"])
        dve.tensor_tensor(pc[:, :, :, 0:15], cs[:, :, :, :], wide(3), ALU.mult).then_inc(cmp_v, 1)
        for t in range(T):
            dve.wait_ge(cmp_p, cmp_p_at[f"pcT{t}"])
            dve.tensor_copy(pcT[:, 4 * t:4 * t + 4, :].rearrange("p a b -> p (a b)"), ps[6 + t][:, :]).then_inc(cmp_v, 1)

    def cmp_scalar(act):
        for i in range(2):
            act.wait_ge(cmp_p, cmp_p_at[f"hid{i}"])
            act.activation(hid[0:60, i, :], ps[4 + i][0:60, 0:256], ACT.Silu).then_inc(cmp_a, 1)
        act.activation(gate2[:, :, :, :].rearrange("p t n b -> p t (n b)"), proj2[:, :, GN:NIN2],
                                    ACT.Sigmoid).then_inc(cmp_a, 1)
        act.wait_ge(cmp_v, cmp_v_at["sub"])
        act.activation(cs[:, :, :, :].rearrange("p t n i -> p (t n i)"),
                                    cs[:, :, :, :].rearrange("p t n i -> p (t n i)"), ACT.Exp).then_inc(cmp_a, 1)

    ps_o, ps_s, ps_pt = ps[0:2], ps[2:6], ps[6:8]

    def nsa_tensor(pe):
        pe.wait_ge(cmp_v, cmp_v_at["pcT1"])
        for i in range(UN + 4):
            if i < UN:
                n, br = divmod(i, 2)
                a, b, m = n // 8, n // 4 % 2, n % 4
                if 2 * (i - 3) > 0:
                    pe.wait_ge(n_exp, 2 * (i - 3))
                bank = ps_s[i % 4]
                for t, (lo, up) in enumerate(SPAN):
                    pe.matmul(bank[:, lo:up], qrT[:, 4 * a + m, t * P:(t + 1) * P],
                              ksw[br][:, a, b, 0:(t + 1) * P],
                              start=True, stop=False)
                    mm = pe.matmul(bank[:, up - P:up], ident, const[:, C_MASKQ:C_MASKQ + P], start=False, stop=True)
                mm.then_inc(n_filled, 1)
            if 2 <= i < UN + 2:
                w = i - 2
                pe.wait_ge(n_ready, w + 1)
                if w - 1 > 0:
                    pe.wait_ge(npt_ready, w - 1)
                for k in range(3):
                    mm = pe.transpose(ps_pt[w % 2][:, k * P:(k + 1) * P], pb2[:, w % 4, k * P:(k + 1) * P], ident)
                mm.then_inc(npt_filled, 1)
            if i >= 5 and i % 2 == 1:
                n = (i - 5) // 2
                if n == 8:
                    pe.wait_ge(o_ready, 2)
                pe.wait_ge(npt_ready, 2 * n + 2)
                g, j = n // 4, n % 4
                for t in range(T):
                    bank = ps_o[t]
                    if j == 0:
                        pe.matmul(bank[:, (n % 8) * 64:(n % 8 + 4) * 64], pcT[:, 4 * t + g, :],
                                  vcmp[:, g, :, :].rearrange("p j d -> p (j d)"), start=True, stop=False)
                    o = bank[:, (n % 8) * 64:(n % 8 + 1) * 64]
                    for br, v0 in enumerate((VS0, VW0)):
                        pt = pt2[:, (2 * n + br) % 4, :]
                        v = lambda k: proj2[:, k, v0 + 64 * g:v0 + 64 * (g + 1)]
                        last = br == 1 and j == 3
                        mm = pe.matmul(o, pt[:, t * P:(t + 1) * P], v(0), start=False, stop=(last and t == 0))
                        if t == 1:
                            mm = pe.matmul(o, pt[:, 2 * P:BL], v(1), start=False, stop=last)
                mm.then_inc(o_filled, 1)

    def nsa_vector(dve):
        def take_out(f):
            dve.wait_ge(o_filled, 8 * (f + 1))
            for t in range(T):
                dve.tensor_copy(yatt[:, t, 512 * f:512 * (f + 1)], ps_o[t][:, :]).then_inc(o_ready, 1)
        for i in range(UN + 1):
            if i == 21:
                take_out(0)
            if i < UN:
                dve.wait_ge(n_filled, i + 1)
                for t, (lo, up) in enumerate(SPAN):
                    dve.tensor_reduce(nst[:, 0, 2 * i + t:2 * i + t + 1], ps_s[i % 4][:, lo:up], AX_X,
                                      ALU.max).then_inc(n_max, 1)
                dve.wait_ge(n_max, 3 * i + 2)
                dve.tensor_scalar(nst[:, 1, 2 * i:2 * i + 2], nst[:, 0, 2 * i:2 * i + 2], -nsa_scale, None,
                                  ALU.mult).then_inc(n_max, 1)
            if i >= 1:
                w = i - 1
                n, br = divmod(w, 2)
                dve.wait_ge(n_exp, 2 * w + 2)
                dve.reciprocal(nst[:, 3, 2 * w:2 * w + 2], nst[:, 2, 2 * w:2 * w + 2]).then_inc(n_inv, 1)
                dve.wait_ge(n_inv, 2 * w + 1)
                dve.tensor_tensor(nst[:, 4, 2 * w:2 * w + 2], nst[:, 3, 2 * w:2 * w + 2], gate2[:, :, n, 1 + br],
                                  ALU.mult).then_inc(n_inv, 1)
                dve.wait_ge(n_inv, 2 * w + 2)
                for t, (lo, up) in enumerate(SPAN):
                    last = dve.tensor_scalar(pb2[:, w % 4, lo:up], pb2[:, w % 4, lo:up],
                                             nst[:, 4, 2 * w + t:2 * w + t + 1], None, ALU.mult)
                last.then_inc(n_ready, 1)
        take_out(1)

    def nsa_scalar(act):
        for i in range(UN + 2):
            if i < UN:
                act.wait_ge(n_max, 3 * i + 3)
                if i - 3 > 0:
                    act.wait_ge(npt_filled, i - 3)
                for t, (lo, up) in enumerate(SPAN):
                    act.activation(pb2[:, i % 4, lo:up], ps_s[i % 4][:, lo:up], ACT.Exp,
                                   bias=nst[:, 1, 2 * i + t:2 * i + t + 1], scale=nsa_scale,
                                   accum_out=nst[:, 2, 2 * i + t:2 * i + t + 1]).then_inc(n_exp, 1)
            if i >= 2:
                w = i - 2
                act.wait_ge(npt_filled, w + 1)
                if (w - 4) // 2 + 1 > 0:
                    act.wait_ge(o_filled, (w - 4) // 2 + 1)
                act.activation(pt2[:, w % 4, :], ps_pt[w % 2][:, 0:BL], ACT.Copy).then_inc(npt_ready, 1)

    turn_mix = Turn(lambda k, t: (ys if k < 8 else yatt)[:, t, (k % 8) * P:(k % 8 + 1) * P], KD, xt_hi, xt_lo,
                    lambda k: rowcols("gs", k) if k < 8 else ones[:, 0:1])

    def mix_tensor(pe):
        pe.wait_ge(o_ready, 4)

    g_out2 = Gemm(at, wview("w_out_2"), KD, 4, lhs_x)
    g_out2.turn = turn_mix
    evac_out2 = evac_residual(g_out2, None)
    ffn2 = Ffn("ffn2", wview("w_gate_2"), wview("w_up_2"), 0, wview("w_down_2"), lambda k: rowcols("gf", k),
               None, None)
    ffn2.before = g_out2.c + 4

    rms_f = Rms([x[:, t, :] for t in range(T)], D, lambda i: xn[:, i, :], 0)
    fw = place("fw", GT2, [D])
    fw_loaded, final = sem("fw_loaded"), sem("final")

    def final_scalar(act):
        act.wait_ge(evac_done, ffn2.down.c + 4)
        act.dma_start(fw[:, :], A["final_norm_w_2"].rearrange("(o n) -> o n", o=1).broadcast_to([P, D])
                      ).then_inc(fw_loaded, 16)
        rms_f.scalar(act)

    def final_vector(dve):
        inv = rms_f.vector(dve)
        dve.wait_ge(fw_loaded, 16)
        for t in range(T):
            dve.scalar_tensor_tensor(x[:, t, :], x[:, t, :], inv(t), fw[:, :], ALU.mult, ALU.mult).then_inc(final, 1)

    def sp_end(sp):
        sp.wait_ge(final, 2)
        sp.dma_start(out.rearrange("o (t p) d -> p (o t) d", p=P), x[:, :, :]).then_inc(sem("out"), 16)
        sp.wait_ge(sem("out"), 16)

    def first_loads(q):
        q.dma_start(crow[0:KD, :], A["c"].rearrange("o (r q) -> (o r) q", q=P)).then_inc(c_loaded, 16)
        q.dma_start(const[:, :], A["const"]).then_inc(c_loaded, 16)

    def start_loads(q):
        q.dma_start(x[:, :, :], A["x"].rearrange("o (t p) d -> p (o t) d", p=P)).then_inc(start, 16)
        for name, src in (("g1", A["g_norm1"]), ("g2", A["g_norm2"]), ("gql", A["g_q_latent"]),
                          ("gkv", A["g_kv_latent"]), ("ga", A["attn_norm_w_2"]), ("gs", A["ssd_norm_w_2"]),
                          ("gf", A["ffn_norm_w_2"]), ("pek", A["cmp_pe_k_2"].rearrange("o a b -> o (a b)")),
                          ("pev", A["cmp_pe_v_2"].rearrange("o a b -> o (a b)")), ("c", A["c"])):
            r, n = ROWS[name]
            q.dma_start(rows_in[r:r + n, 0, :], src.rearrange("o (r q) -> (o r) q", q=P)).then_inc(start, 16)
        q.dma_start(rows_in[0:12, 1, :], A["conv_b_2"].rearrange("o (r q) -> (o r) q", q=P)).then_inc(start, 16)
        q.dma_start(rows_in[12:60, 1, :], A["conv_w_2"].rearrange("o w (r q) -> (o w r) q", q=P)).then_inc(start, 16)
        q.dma_start(rows_in[60:61, 1, :], A["g_q_head"][:, 0:P]).then_inc(start, 16)
        q.dma_start(rows_in[61:62, 1, :], A["g_k_head"][:, 0:P]).then_inc(start, 16)
        q.dma_start(rows_in[62:94, 1, :], A["b_ada"][:, 0:2 * D].rearrange("o (r q) -> (o r) q", q=P)
                     ).then_inc(start, 16)
        q.dma_start(posi[0:T, :], A["positions"].rearrange("o (t p) -> (o t) p", p=P)).then_inc(start, 16)
        for src, a, n in ((A["g_q_head"][:, P:HQ], 0, 64), (A["g_k_head"][:, P:HQ], 64, 64),
                          (A["dt_bias_2"], 128, 16), (A["a_log_2"], 144, 16), (A["d_skip_2"], 160, 16)):
            q.dma_start(brd[:, a:a + n], src.broadcast_to([P, n])).then_inc(start, 16)
    NSTART = 1 + 10 + 5 + 1 + 5

    block = nc.Block()
    with block:
        @block.sync
        def _(sp):
            first_loads(sp)
            sync_gemm(sp, g_ada)
            sync_gemm(sp, g_in)
            sync_gemm(sp, g_psb, (lat_scaled, 4))
            sync_gemm(sp, g_uq)
            sync_gemm(sp, g_ukv)
            sync_gemm(sp, g_pmla, (ya_lo, 4))
            sync_gemm(sp, g_out)
            sync_gemm(sp, ffn1.g)
            sync_gemm(sp, ffn1.down)
            sync_gemm(sp, g_b)
            sync_gemm(sp, g_out2)
            sync_gemm(sp, ffn2.g)
            sync_gemm(sp, ffn2.down)
            sp_end(sp)

        @block.scalar
        def _(act):
            start_scalar(act)
            scalar_gemm(act, g_ada, None)
            scalar_gemm(act, g_in, evac_proj)
            g_in2.scalar(act, lambda t: proj[:, t, 8192:NIN])
            gates_scalar(act)
            sb_scalar(act)
            rms_lat.scalar(act)
            turn_lat[0].scalar(act)
            turn_lat[1].scalar(act)
            scalar_gemm(act, g_psb, None)
            scalar_gemm(act, g_uq, evac_scalar_to(lambda t, c: proj[:, t, bass.ds(Q0 + c, CW)]))
            scalar_gemm(act, g_ukv, evac_kv)
            rope1_scalar(act)
            heads_scalar(act)
            mla_scalar(act)
            scalar_gemm(act, g_pmla, None)
            gt_scalar(act)
            scalar_gemm(act, g_out, None)
            ffn1.scalar(act, ada2.scalar)
            norm_a_scalar(act)
            scalar_gemm(act, g_b, evac_b)
            g_b2.scalar(act, lambda t: proj2[:, t, 5120:NIN2])
            ssd_scalar(act)
            cmp_scalar(act)
            nsa_scalar(act)
            scalar_gemm(act, g_out2, None)
            ffn2.scalar(act)
            final_scalar(act)

        @block.vector
        def _(dve):
            start_vector(dve)
            vector_gemm(dve, g_ada)
            small_vector(dve)
            ada1_vector(dve)
            vector_gemm(dve, g_in, prepare_rest)
            sb_vector(dve)
            lat_vector(dve)
            dve.wait_ge(gates_ready, 2)
            vector_gemm(dve, g_psb, evac_gate_b)
            vector_gemm(dve, g_uq)
            vector_gemm(dve, g_ukv, beside_kv)
            heads_vector(dve)
            mla_vector(dve)
            vector_gemm(dve, g_pmla, evac_merge)
            vector_gemm(dve, g_out, evac_out)
            ffn1.vector(dve, ada2.vector)
            norm_a_vector(dve)
            vector_gemm(dve, g_b, prepare_rest2)
            ssd_vector(dve)
            rope2_vector(dve)
            cmp_vector(dve)
            nsa_vector(dve)
            vector_gemm(dve, g_out2, evac_out2)
            ffn2.vector(dve)
            final_vector(dve)

        @block.tensor
        def _(pe):
            start_tensor(pe)
            tensor_gemm(pe, g_ada)
            small_tensor(pe)
            turn_x_tensor(pe)
            tensor_gemm(pe, g_in)
            g_in2.tensor(pe)
            pe.wait_ge(evac_done, g_in2.c + 1)
            sb_tensor(pe)
            lat_tensor(pe)
            pe.wait_ge(yb_lo, 4)
            tensor_gemm(pe, g_psb)
            tensor_gemm(pe, g_uq)
            tensor_gemm(pe, g_ukv)
            mla_tensor(pe)
            pe.wait_ge(ya_lo, 4)
            tensor_gemm(pe, g_pmla)
            pe.wait_ge(evac_done, g_pmla.c + g_pmla.n)
            tensor_gemm(pe, g_out)
            ffn1.tensor(pe, ada2.tensor)
            norm_a_tensor(pe)
            tensor_gemm(pe, g_b)
            g_b2.tensor(pe)
            ssd_tensor(pe)
            cmp_tensor(pe)
            nsa_tensor(pe)
            mix_tensor(pe)
            tensor_gemm(pe, g_out2)
            ffn2.tensor(pe)
    return names


def kernel(**inputs):
    import numpy as _np
    import concourse.bacc as _bacc
    from concourse import mybir as _mybir
    from concourse.bass_utils import run_bass_kernel_spmd as _run

    nc = _bacc.Bacc("TRN2", target_bir_lowering=False, num_devices=1)
    arrays, aps = {}, {}
    given = {name: _np.ascontiguousarray(value) for name, value in inputs.items()}
    given["const"] = constants()
    for name, a in given.items():
        arrays[f"in_{name}"] = a
        aps[name] = nc.dram_tensor(f"in_{name}", a.shape, _mybir.dt.from_np(a.dtype), kind="ExternalInput").ap()
    out = nc.dram_tensor("out", (1, SEQ, D), F32, kind="ExternalOutput").ap()
    program(nc, aps, out)
    r = _run(nc, [arrays], core_ids=[0])
    return r.results[0]["out"]
```
